# Optimizing a Trainium2 kernel written in Bass

```python
import math
import jax, jax.numpy as jnp
from jax import lax
import numpy as np

D_MODEL = 1024
BATCH = 1
SEQ = 256
DEPTH = 2

N_MIXERS = 2
N_A = (DEPTH + 1) // 2
N_B = DEPTH // 2

SSM_EXPAND = 2
D_INNER = SSM_EXPAND * D_MODEL
SSM_HEAD_DIM = 64
SSM_HEADS = D_INNER // SSM_HEAD_DIM
SSM_GROUPS = 8
SSM_HPG = SSM_HEADS // SSM_GROUPS
SSM_STATE = 128
CONV_K = 4
CONV_DIM = D_INNER + 2 * SSM_GROUPS * SSM_STATE
SSM_IN_DIM = D_INNER + CONV_DIM + SSM_HEADS
NORM_GROUP = D_INNER // SSM_GROUPS
CHUNK = 128
DT_MIN = 0.001
DT_MAX = 0.1

MLA_HEADS = 16
Q_LORA = 384
KV_LORA = 256
QK_NOPE = 64
QK_ROPE = 32
V_DIM = 64
QK_DIM = QK_NOPE + QK_ROPE
MLA_IN_DIM = Q_LORA + KV_LORA + QK_ROPE
ROPE_THETA = 10000.0
Q_BLOCK = 128

D_FF = 2816
EPS = 1e-6


def rms_norm(x, w):
    xf = x.astype(jnp.float32)
    y = xf * lax.rsqrt(jnp.mean(xf * xf, axis=-1, keepdims=True) + EPS)
    return (y * w.astype(jnp.float32)).astype(x.dtype)

def swiglu(h, w_gate, w_up, w_down):
    return (jax.nn.silu(h @ w_gate) * (h @ w_up)) @ w_down

def causal_depthwise_conv(u, w, b):
    y = lax.conv_general_dilated(u, w[:, None, :].astype(u.dtype), window_strides=(1,),
                                 padding=[(CONV_K - 1, 0)],
                                 dimension_numbers=("NWC", "WIO", "NWC"),
                                 feature_group_count=u.shape[-1])
    return y + b

def ssd_chunked(xs, dt, a, bm, cm):
    b, s = xs.shape[:2]
    nc = s // CHUNK

    def to_chunks(t):
        return jnp.swapaxes(t.reshape((b, nc, CHUNK) + t.shape[2:]), 0, 1)

    mask = jnp.tril(jnp.ones((CHUNK, CHUNK), dtype=bool))[None, :, :, None, None]

    def step(state, inp):
        xc, dtc, bc, cc = inp
        acs = jnp.cumsum(dtc * a, axis=1)
        seg = acs[:, :, None] - acs[:, None, :]
        decay = jnp.exp(jnp.where(mask, seg, -jnp.inf))
        cb = jnp.einsum("blgn,bsgn->blsg", cc, bc)
        xdt = xc * dtc[..., None]
        y_diag = jnp.einsum("blsg,blsgr,bsgrp->blgrp", cb, decay, xdt)
        y_off = jnp.einsum("blgn,bgrpn->blgrp", cc, state) * jnp.exp(acs)[..., None]
        decay_to_end = jnp.exp(acs[:, -1:] - acs)
        new_state = (state * jnp.exp(acs[:, -1])[..., None, None]
                     + jnp.einsum("bsgn,bsgr,bsgrp->bgrpn", bc, decay_to_end, xdt))
        return new_state, y_diag + y_off

    state0 = jnp.zeros((b, SSM_GROUPS, SSM_HPG, SSM_HEAD_DIM, SSM_STATE), jnp.float32)
    _, ys = lax.scan(step, state0, (to_chunks(xs), to_chunks(dt), to_chunks(bm), to_chunks(cm)))
    return jnp.swapaxes(ys, 0, 1).reshape(xs.shape)

def mamba2_mixer(h, w_in, conv_w, conv_b, dt_bias, a_log, d_skip, norm_w, w_out):
    b, s, _ = h.shape
    proj = h @ w_in
    z = proj[..., :D_INNER]
    xbc = proj[..., D_INNER:D_INNER + CONV_DIM]
    dt = proj[..., D_INNER + CONV_DIM:]
    xbc = jax.nn.silu(causal_depthwise_conv(xbc, conv_w, conv_b))
    xs = xbc[..., :D_INNER].astype(jnp.float32).reshape(b, s, SSM_GROUPS, SSM_HPG, SSM_HEAD_DIM)
    bm = xbc[..., D_INNER:D_INNER + SSM_GROUPS * SSM_STATE].astype(jnp.float32).reshape(b, s, SSM_GROUPS, SSM_STATE)
    cm = xbc[..., D_INNER + SSM_GROUPS * SSM_STATE:].astype(jnp.float32).reshape(b, s, SSM_GROUPS, SSM_STATE)
    dt = jax.nn.softplus(dt.astype(jnp.float32) + dt_bias.astype(jnp.float32)).reshape(b, s, SSM_GROUPS, SSM_HPG)
    a = (-jnp.exp(a_log.astype(jnp.float32))).reshape(SSM_GROUPS, SSM_HPG)
    y = ssd_chunked(xs, dt, a, bm, cm)
    y = y + d_skip.astype(jnp.float32).reshape(SSM_GROUPS, SSM_HPG)[:, :, None] * xs
    g = (y.reshape(b, s, D_INNER) * jax.nn.silu(z.astype(jnp.float32))).reshape(b, s, SSM_GROUPS, NORM_GROUP)
    g = g * lax.rsqrt(jnp.mean(g * g, axis=-1, keepdims=True) + EPS)
    g = g.reshape(b, s, D_INNER) * norm_w.astype(jnp.float32)
    return g.astype(h.dtype) @ w_out

def rope_cos_sin(positions):
    inv_freq = 1.0 / (ROPE_THETA ** (jnp.arange(0, QK_ROPE, 2, dtype=jnp.float32) / QK_ROPE))
    ang = positions.astype(jnp.float32)[..., None] * inv_freq
    return jnp.cos(ang), jnp.sin(ang)

def apply_rope(x, cos, sin):
    xf = x.astype(jnp.float32)
    x1, x2 = xf[..., :QK_ROPE // 2], xf[..., QK_ROPE // 2:]
    return jnp.concatenate([x1 * cos - x2 * sin, x2 * cos + x1 * sin], axis=-1).astype(x.dtype)

def causal_block_attention(q_nope, q_rope, k_nope, k_rope, v):
    s = q_nope.shape[1]
    scale = QK_DIM ** -0.5
    outs = []
    for i in range(s // Q_BLOCK):
        q0 = i * Q_BLOCK
        kend = q0 + Q_BLOCK
        sc = (jnp.einsum("bqhd,bkhd->bhqk", q_nope[:, q0:kend], k_nope[:, :kend])
              + jnp.einsum("bqhr,bkr->bhqk", q_rope[:, q0:kend], k_rope[:, :kend]))
        sc = sc.astype(jnp.float32) * scale
        qi = q0 + jnp.arange(Q_BLOCK)
        ki = jnp.arange(kend)
        sc = jnp.where(ki[None, :] <= qi[:, None], sc, -jnp.inf)
        p = jax.nn.softmax(sc, axis=-1).astype(v.dtype)
        outs.append(jnp.einsum("bhqk,bkhd->bqhd", p, v[:, :kend]))
    return jnp.concatenate(outs, axis=1)

def mla_mixer(h, positions, w_in, q_a_norm, kv_a_norm, w_q_b, w_kv_b, q_norm, k_norm, w_out):
    b, s, _ = h.shape
    proj = h @ w_in
    cq = rms_norm(proj[..., :Q_LORA], q_a_norm)
    ckv = rms_norm(proj[..., Q_LORA:Q_LORA + KV_LORA], kv_a_norm)
    k_rope = proj[..., Q_LORA + KV_LORA:]
    q = (cq @ w_q_b).reshape(b, s, MLA_HEADS, QK_DIM)
    kv = (ckv @ w_kv_b).reshape(b, s, MLA_HEADS, QK_NOPE + V_DIM)
    q_nope, q_rope = q[..., :QK_NOPE], q[..., QK_NOPE:]
    k_nope, v = kv[..., :QK_NOPE], kv[..., QK_NOPE:]
    q_nope = rms_norm(q_nope, q_norm[:QK_NOPE])
    q_rope = rms_norm(q_rope, q_norm[QK_NOPE:])
    k_nope = rms_norm(k_nope, k_norm[:QK_NOPE])
    k_rope = rms_norm(k_rope, k_norm[QK_NOPE:])
    cos, sin = rope_cos_sin(positions)
    q_rope = apply_rope(q_rope, cos[:, :, None], sin[:, :, None])
    k_rope = apply_rope(k_rope, cos, sin)
    o = causal_block_attention(q_nope, q_rope, k_nope, k_rope, v)
    return o.reshape(b, s, MLA_HEADS * V_DIM) @ w_out

def first_inputs(seed: int = 0) -> dict:
    key = jax.random.key(seed)
    ks = jax.random.split(key, 24)
    f32 = jnp.float32

    def nrm(k, shape, fan_in):
        return jax.random.normal(k, shape, f32) * fan_in ** -0.5

    def gain(k, shape):
        return 1.0 + 0.05 * jax.random.normal(k, shape, f32)

    x = jax.random.normal(ks[0], (BATCH, SEQ, D_MODEL), f32)
    offs = jax.random.randint(ks[1], (BATCH, 1), 0, 512, dtype=jnp.int32)
    positions = (jnp.arange(SEQ, dtype=jnp.int32)[None, :] + offs).astype(jnp.int32)

    norm_w = gain(ks[2], (DEPTH, 3, D_MODEL))
    ffn_w_gate = nrm(ks[3], (DEPTH, 2, D_MODEL, D_FF), D_MODEL)
    ffn_w_up = nrm(ks[4], (DEPTH, 2, D_MODEL, D_FF), D_MODEL)
    ffn_w_down = nrm(ks[5], (DEPTH, 2, D_FF, D_MODEL), D_FF)

    ssm_w_in = nrm(ks[6], (N_A, D_MODEL, SSM_IN_DIM), D_MODEL)
    ssm_conv_w = nrm(ks[7], (N_A, CONV_K, CONV_DIM), CONV_K)
    ssm_conv_b = 0.02 * jax.random.normal(ks[8], (N_A, CONV_DIM), f32)
    u = jax.random.uniform(ks[9], (N_A, SSM_HEADS), f32)
    dt0 = jnp.exp(u * (math.log(DT_MAX) - math.log(DT_MIN)) + math.log(DT_MIN))
    ssm_dt_bias = dt0 + jnp.log(-jnp.expm1(-dt0))
    ssm_a_log = jnp.log(jax.random.uniform(ks[10], (N_A, SSM_HEADS), f32, minval=1.0, maxval=16.0))
    ssm_d = 1.0 + 0.1 * jax.random.normal(ks[11], (N_A, SSM_HEADS), f32)
    ssm_norm_w = gain(ks[12], (N_A, D_INNER))
    ssm_w_out = nrm(ks[13], (N_A, D_INNER, D_MODEL), D_INNER)

    mla_w_in = nrm(ks[14], (N_B, D_MODEL, MLA_IN_DIM), D_MODEL)
    mla_q_a_norm = gain(ks[15], (N_B, Q_LORA))
    mla_kv_a_norm = gain(ks[16], (N_B, KV_LORA))
    mla_w_q_b = nrm(ks[17], (N_B, Q_LORA, MLA_HEADS * QK_DIM), Q_LORA)
    mla_w_kv_b = nrm(ks[18], (N_B, KV_LORA, MLA_HEADS * (QK_NOPE + V_DIM)), KV_LORA)
    mla_q_norm = gain(ks[19], (N_B, QK_DIM))
    mla_k_norm = gain(ks[20], (N_B, QK_DIM))
    mla_w_out = nrm(ks[21], (N_B, MLA_HEADS * V_DIM, D_MODEL), MLA_HEADS * V_DIM)

    return {"x": x, "positions": positions, "norm_w": norm_w,
            "ffn_w_gate": ffn_w_gate, "ffn_w_up": ffn_w_up, "ffn_w_down": ffn_w_down,
            "ssm_w_in": ssm_w_in, "ssm_conv_w": ssm_conv_w, "ssm_conv_b": ssm_conv_b,
            "ssm_dt_bias": ssm_dt_bias, "ssm_a_log": ssm_a_log, "ssm_d": ssm_d,
            "ssm_norm_w": ssm_norm_w, "ssm_w_out": ssm_w_out,
            "mla_w_in": mla_w_in, "mla_q_a_norm": mla_q_a_norm, "mla_kv_a_norm": mla_kv_a_norm,
            "mla_w_q_b": mla_w_q_b, "mla_w_kv_b": mla_w_kv_b, "mla_q_norm": mla_q_norm,
            "mla_k_norm": mla_k_norm, "mla_w_out": mla_w_out}

def first_block(x, positions, norm_w, ffn_w_gate, ffn_w_up, ffn_w_down,
              ssm_w_in, ssm_conv_w, ssm_conv_b, ssm_dt_bias, ssm_a_log, ssm_d,
              ssm_norm_w, ssm_w_out,
              mla_w_in, mla_q_a_norm, mla_kv_a_norm, mla_w_q_b, mla_w_kv_b,
              mla_q_norm, mla_k_norm, mla_w_out):
    for i in range(DEPTH):
        x = x + 0.5 * swiglu(rms_norm(x, norm_w[i, 0]), ffn_w_gate[i, 0], ffn_w_up[i, 0], ffn_w_down[i, 0])
        h = rms_norm(x, norm_w[i, 1])
        j = i // N_MIXERS
        if i % N_MIXERS == 0:
            x = x + mamba2_mixer(h, ssm_w_in[j], ssm_conv_w[j], ssm_conv_b[j], ssm_dt_bias[j],
                                 ssm_a_log[j], ssm_d[j], ssm_norm_w[j], ssm_w_out[j])
        else:
            x = x + mla_mixer(h, positions, mla_w_in[j], mla_q_a_norm[j], mla_kv_a_norm[j],
                              mla_w_q_b[j], mla_w_kv_b[j], mla_q_norm[j], mla_k_norm[j], mla_w_out[j])
        x = x + 0.5 * swiglu(rms_norm(x, norm_w[i, 2]), ffn_w_gate[i, 1], ffn_w_up[i, 1], ffn_w_down[i, 1])
    return x


DEPTH_2 = 1

CHUNK_2 = 64

MLSTM_HEADS = 4
MLSTM_HD = D_MODEL // MLSTM_HEADS
MLSTM_W = MLSTM_HEADS * MLSTM_HD

DIFF_HEADS = 8
DIFF_HD = D_MODEL // (2 * DIFF_HEADS)
DIFF_W = DIFF_HEADS * 2 * DIFF_HD

RET_HEADS = 4
RET_HD = D_MODEL // RET_HEADS
RET_W = RET_HEADS * RET_HD

FFN_HIDDEN = -(-8 * D_MODEL // (3 * 256)) * 256

IN_SIZES = (MLSTM_W, MLSTM_W, MLSTM_W, MLSTM_W, MLSTM_HEADS, MLSTM_HEADS,
            DIFF_W, DIFF_W, DIFF_W,
            RET_W, RET_W, RET_W, RET_W,
            3 * D_MODEL)
N_IN = sum(IN_SIZES)


def rmsnorm(x, g):
    x32 = x.astype(jnp.float32)
    y = x32 * lax.rsqrt(jnp.mean(x32 * x32, axis=-1, keepdims=True) + EPS)
    return (y * g.astype(jnp.float32)).astype(x.dtype)

def head_rms(x):
    x32 = x.astype(jnp.float32)
    return x32 * lax.rsqrt(jnp.mean(x32 * x32, axis=-1, keepdims=True) + EPS)

def causal_dwconv(x, w):
    K = w.shape[0]
    S = x.shape[1]
    xp = jnp.pad(x, ((0, 0), (K - 1, 0), (0, 0)))
    out = xp[:, 0:S] * w[0]
    for j in range(1, K):
        out = out + xp[:, j:j + S] * w[j]
    return out

def to_chunks(a):
    B, S = a.shape[0], a.shape[1]
    return jnp.moveaxis(a.reshape(B, S // CHUNK_2, CHUNK_2, *a.shape[2:]), 1, 0)

def from_chunks(a):
    a = jnp.moveaxis(a, 0, 1)
    return a.reshape(a.shape[0], a.shape[1] * a.shape[2], *a.shape[3:])

def mlstm(q, k, v, i_pre, f_pre):
    B, S, H, dh = q.shape
    f32 = jnp.float32
    q = q.astype(f32)
    k = k.astype(f32) * (dh ** -0.5)
    v = v.astype(f32)
    logf = jax.nn.log_sigmoid(f_pre.astype(f32))
    ig = i_pre.astype(f32)
    causal = jnp.tril(jnp.ones((CHUNK_2, CHUNK_2), dtype=bool))

    def step(carry, inp):
        C, n, m = carry
        qj, kj, vj, lf, igj = inp
        b = jnp.cumsum(lf, axis=1).transpose(0, 2, 1)
        igT = igj.transpose(0, 2, 1)
        g = b[..., -1]
        d_intra = b[..., :, None] - b[..., None, :] + igT[..., None, :]
        d_intra = jnp.where(causal, d_intra, -jnp.inf)
        d_inter = b + m[..., None]
        m_row = jnp.maximum(jnp.max(d_intra, axis=-1), d_inter)
        w_intra = jnp.exp(d_intra - m_row[..., None])
        w_inter = jnp.exp(d_inter - m_row)
        s = jnp.einsum('blhd,bshd->bhls', qj, kj) * w_intra
        w_int_t = w_inter.transpose(0, 2, 1)[..., None]
        num = (jnp.einsum('bhls,bshe->blhe', s, vj)
               + jnp.einsum('blhd,bhde->blhe', qj, C) * w_int_t)
        den = jnp.sum(s, axis=-1) + jnp.einsum('blhd,bhd->bhl', qj, n) * w_inter
        den = jnp.maximum(jnp.abs(den), jnp.exp(-m_row))
        h = num / den.transpose(0, 2, 1)[..., None]
        a = g[..., None] - b + igT
        m_new = jnp.maximum(g + m, jnp.max(a, axis=-1))
        w_old = jnp.exp(g + m - m_new)
        w_k = jnp.exp(a - m_new[..., None])
        C_new = w_old[..., None, None] * C + jnp.einsum('bhs,bshd,bshe->bhde', w_k, kj, vj)
        n_new = w_old[..., None] * n + jnp.einsum('bhs,bshd->bhd', w_k, kj)
        return (C_new, n_new, m_new), h

    init = (jnp.zeros((B, H, dh, dh), f32), jnp.zeros((B, H, dh), f32), jnp.zeros((B, H), f32))
    xs = (to_chunks(q), to_chunks(k), to_chunks(v), to_chunks(logf), to_chunks(ig))
    _, hs = lax.scan(step, init, xs)
    return from_chunks(hs)

def retention(q, k, v):
    B, S, H, dh = q.shape
    f32 = jnp.float32
    q = q.astype(f32)
    k = k.astype(f32) * (dh ** -0.5)
    v = v.astype(f32)
    log_gamma = jnp.log(1.0 - 2.0 ** (-5.0 - jnp.arange(H, dtype=f32)))
    pos = jnp.arange(CHUNK_2, dtype=f32)
    rel = pos[:, None] - pos[None, :]
    dmask = jnp.where(rel[None] >= 0, jnp.exp(log_gamma[:, None, None] * jnp.maximum(rel, 0.0)[None]), 0.0)
    xi = jnp.exp(log_gamma[None, :] * (pos[:, None] + 1.0))
    zeta = jnp.exp(log_gamma[:, None] * (CHUNK_2 - 1.0 - pos[None, :]))
    chunk_decay = jnp.exp(log_gamma * CHUNK_2)

    def step(R, inp):
        qj, kj, vj = inp
        s = jnp.einsum('blhd,bshd->bhls', qj, kj) * dmask[None]
        o = (jnp.einsum('bhls,bshe->blhe', s, vj)
             + jnp.einsum('blhd,bhde->blhe', qj, R) * xi[None, :, :, None])
        R_new = chunk_decay[None, :, None, None] * R + jnp.einsum('hs,bshd,bshe->bhde', zeta, kj, vj)
        return R_new, o

    R0 = jnp.zeros((B, H, dh, dh), f32)
    _, os_ = lax.scan(step, R0, (to_chunks(q), to_chunks(k), to_chunks(v)))
    return from_chunks(os_)

def diff_attention(q, k, v, lam):
    B, S, H, _, dh = q.shape
    f32 = jnp.float32
    q = q.astype(f32) * (dh ** -0.5)
    k = k.astype(f32)
    v = v.astype(f32)
    slopes = 2.0 ** (-8.0 * (jnp.arange(H, dtype=f32) + 1.0) / H)
    outs = []
    for blk in range(S // Q_BLOCK):
        q0 = blk * Q_BLOCK
        kend = q0 + Q_BLOCK
        qb = q[:, q0:kend]
        kb = k[:, :kend]
        vb = v[:, :kend]
        s = jnp.einsum('bqhcd,bkhcd->bhcqk', qb, kb)
        tq = jnp.arange(q0, kend)
        tk = jnp.arange(kend)
        dist = jnp.abs(tq[:, None] - tk[None, :]).astype(f32)
        allowed = (tk // CHUNK_2)[None, :] <= (tq // CHUNK_2)[:, None]
        bias = -slopes[:, None, None] * dist[None]
        s = jnp.where(allowed, s + bias[None, :, None], -jnp.inf)
        p = jax.nn.softmax(s, axis=-1)
        a = p[:, :, 0] - lam * p[:, :, 1]
        outs.append(jnp.einsum('bhqk,bkhe->bqhe', a, vb))
    return jnp.concatenate(outs, axis=1)

def split_in(proj):
    idx = np.cumsum(np.array(IN_SIZES))[:-1].tolist()
    return jnp.split(proj, idx, axis=-1)

def second_inputs(seed: int = 0) -> dict:
    key = jax.random.key(seed)
    ks = jax.random.split(key, 16)
    f32 = jnp.float32

    def nrm(kk, shape, scale):
        return jax.random.normal(kk, shape, f32) * scale

    x = nrm(ks[0], (BATCH, SEQ, D_MODEL), 1.0)
    norm_gains = 1.0 + nrm(ks[1], (DEPTH_2, 4, D_MODEL), 0.05)
    w_in = nrm(ks[2], (DEPTH_2, D_MODEL, N_IN), D_MODEL ** -0.5)
    mlstm_conv = nrm(ks[3], (DEPTH_2, CONV_K, 2 * MLSTM_W), CONV_K ** -0.5)
    f_bias = jnp.broadcast_to(jnp.linspace(3.0, 6.0, MLSTM_HEADS, dtype=f32), (DEPTH_2, MLSTM_HEADS))
    i_bias = jnp.zeros((DEPTH_2, MLSTM_HEADS), f32)
    mlstm_gate_bias = jnp.stack([i_bias, f_bias], axis=1) + nrm(ks[4], (DEPTH_2, 2, MLSTM_HEADS), 0.1)
    diff_lambda = nrm(ks[5], (DEPTH_2, 4, DIFF_HD), 0.1)
    diff_subln = 1.0 + nrm(ks[6], (DEPTH_2, 2 * DIFF_HD), 0.05)
    w_mlstm_out = nrm(ks[7], (DEPTH_2, MLSTM_W, D_MODEL), MLSTM_W ** -0.5)
    w_diff_out = nrm(ks[8], (DEPTH_2, DIFF_W, D_MODEL), DIFF_W ** -0.5)
    w_ret_out = nrm(ks[9], (DEPTH_2, RET_W, D_MODEL), RET_W ** -0.5)
    w_out = nrm(ks[10], (DEPTH_2, D_MODEL, D_MODEL), D_MODEL ** -0.5)
    w_ffn_in = nrm(ks[11], (DEPTH_2, D_MODEL, 2 * FFN_HIDDEN), D_MODEL ** -0.5)
    w_ffn_out = nrm(ks[12], (DEPTH_2, FFN_HIDDEN, D_MODEL), FFN_HIDDEN ** -0.5)
    return {"x": x, "norm_gains": norm_gains, "w_in": w_in, "mlstm_conv": mlstm_conv,
            "mlstm_gate_bias": mlstm_gate_bias, "diff_lambda": diff_lambda,
            "diff_subln": diff_subln, "w_mlstm_out": w_mlstm_out, "w_diff_out": w_diff_out,
            "w_ret_out": w_ret_out, "w_out": w_out, "w_ffn_in": w_ffn_in,
            "w_ffn_out": w_ffn_out}

def second_block(x, norm_gains, w_in, mlstm_conv, mlstm_gate_bias, diff_lambda, diff_subln,
              w_mlstm_out, w_diff_out, w_ret_out, w_out, w_ffn_in, w_ffn_out):
    B, S, _ = x.shape
    f32 = jnp.float32
    for l in range(DEPTH_2):
        g = norm_gains[l]
        h = rmsnorm(x, g[0])
        proj = h @ w_in[l]
        (mq, mk, mv, mo, mi, mf, dq, dk, dv, rq, rk, rv, rg, gates) = split_in(proj)

        qk = jax.nn.silu(causal_dwconv(jnp.concatenate([mq, mk], axis=-1), mlstm_conv[l]))
        mq_c, mk_c = jnp.split(qk, 2, axis=-1)
        hm = mlstm(mq_c.reshape(B, S, MLSTM_HEADS, MLSTM_HD),
                   mk_c.reshape(B, S, MLSTM_HEADS, MLSTM_HD),
                   mv.reshape(B, S, MLSTM_HEADS, MLSTM_HD),
                   mi + mlstm_gate_bias[l, 0],
                   mf + mlstm_gate_bias[l, 1])
        hm = jax.nn.sigmoid(mo.astype(f32)) * head_rms(hm).reshape(B, S, MLSTM_W)

        lam_init = 0.8 - 0.6 * math.exp(-0.3 * l)
        lmb = diff_lambda[l].astype(f32)
        lam = jnp.exp(jnp.sum(lmb[0] * lmb[1])) - jnp.exp(jnp.sum(lmb[2] * lmb[3])) + lam_init
        hd = diff_attention(dq.reshape(B, S, DIFF_HEADS, 2, DIFF_HD),
                            dk.reshape(B, S, DIFF_HEADS, 2, DIFF_HD),
                            dv.reshape(B, S, DIFF_HEADS, 2 * DIFF_HD), lam)
        hd = (rmsnorm(hd, diff_subln[l]) * (1.0 - lam_init)).reshape(B, S, DIFF_W)

        hr = retention(rq.reshape(B, S, RET_HEADS, RET_HD),
                       rk.reshape(B, S, RET_HEADS, RET_HD),
                       rv.reshape(B, S, RET_HEADS, RET_HD))
        hr = jax.nn.silu(rg.astype(f32)) * head_rms(hr).reshape(B, S, RET_W)

        gm, gd, gr = jnp.split(jax.nn.sigmoid(gates), 3, axis=-1)
        y = (gm * (hm.astype(x.dtype) @ w_mlstm_out[l])
             + gd * (hd.astype(x.dtype) @ w_diff_out[l])
             + gr * (hr.astype(x.dtype) @ w_ret_out[l]))
        y = y @ w_out[l]
        x = x + rmsnorm(y, g[1])

        h2 = rmsnorm(x, g[2])
        a, u = jnp.split(h2 @ w_ffn_in[l], 2, axis=-1)
        f = (jax.nn.silu(a) * u) @ w_ffn_out[l]
        x = x + rmsnorm(f, g[3])
    return x


def setup_inputs(seed=0):
    out = dict(first_inputs(seed))
    for name, value in second_inputs(seed + 1).items():
        if name != "x":
            out[name + "_2"] = value
    return out


def reference(
    x, positions, norm_w, ffn_w_gate, ffn_w_up, ffn_w_down, ssm_w_in, ssm_conv_w, ssm_conv_b,
    ssm_dt_bias, ssm_a_log, ssm_d, ssm_norm_w, ssm_w_out, mla_w_in, mla_q_a_norm, mla_kv_a_norm,
    mla_w_q_b, mla_w_kv_b, mla_q_norm, mla_k_norm, mla_w_out, norm_gains_2, w_in_2,
    mlstm_conv_2, mlstm_gate_bias_2, diff_lambda_2, diff_subln_2, w_mlstm_out_2, w_diff_out_2,
    w_ret_out_2, w_out_2, w_ffn_in_2, w_ffn_out_2,
):
    x = first_block(
        x, positions, norm_w, ffn_w_gate, ffn_w_up, ffn_w_down, ssm_w_in, ssm_conv_w,
        ssm_conv_b, ssm_dt_bias, ssm_a_log, ssm_d, ssm_norm_w, ssm_w_out, mla_w_in,
        mla_q_a_norm, mla_kv_a_norm, mla_w_q_b, mla_w_kv_b, mla_q_norm, mla_k_norm, mla_w_out,
    )
    return second_block(
        x, norm_gains_2, w_in_2, mlstm_conv_2, mlstm_gate_bias_2, diff_lambda_2, diff_subln_2,
        w_mlstm_out_2, w_diff_out_2, w_ret_out_2, w_out_2, w_ffn_in_2, w_ffn_out_2,
    )


_drawn_inputs = setup_inputs


def setup_inputs(seed=0):
    import zlib

    import numpy as np

    out = dict(_drawn_inputs(seed))
    spreads = {}
    factors = {'mla_q_a_norm': 6.337,
     'mla_q_norm': 6.525,
     'mla_k_norm': 6.452,
     'diff_lambda_2': 5.429,
     'diff_subln_2': 2.903}
    for name, (base, spread) in spreads.items():
        noise = np.random.default_rng([zlib.crc32(name.encode()), seed]).standard_normal(out[name].shape)
        drawn = base * np.exp(spread * noise) if base else spread * noise
        out[name] = __import__('jax').numpy.asarray(drawn.astype(out[name].dtype))
    for name, factor in factors.items():
        out[name] = (out[name] * factor).astype(out[name].dtype)
    return out
```

```python
import math
from contextlib import ExitStack

import numpy as np

import concourse.bass as bass
from concourse import mybir

FP32 = mybir.dt.float32
FP32R = mybir.dt.float32r
I32 = mybir.dt.int32
ALU = mybir.AluOpType
ACT = mybir.ActivationFunctionType
AX = mybir.AxisListType

P = 128
SEQ = 256
NT = SEQ // P
DM = 1024
KD = DM // P
EPS = 1e-6
FF = 2816
FCH = 256
NFF = FF // FCH
SLOTS = 3
BLK = 2048
BIG = 1e30

D_INNER, SSM_HEADS, SSM_P, SSM_N, SSM_G = 2048, 32, 64, 128, 8
SSM_R = SSM_HEADS // SSM_G
XBC = D_INNER + 2 * SSM_G * SSM_N
CONV_K = 4

MH, QL, KVL, DN, DR, DV = 16, 384, 256, 64, 32, 64
DQ = DN + DR
HR = DR // 2
ROPE_THETA = 10000.0
TWO_PI = (6.28125, 0.0019350051879882812, 3.0199159819567e-07)
ROUND = 12582912.0

LH, LD = 4, 256
LDV = LD + 1
DH, DHD = 8, 64
DCH = 64
C_MQ, C_MK, C_MV, C_MO, C_MI, C_MF = 0, 1024, 2048, 3072, 4096, 4100
C_DQ = 4104
C_DK, C_DV = C_DQ + DM, C_DQ + 2 * DM
C_RQ = C_DQ + 3 * DM
C_RK, C_RV, C_RG = C_RQ + DM, C_RQ + 2 * DM, C_RQ + 3 * DM
C_G = C_RQ + 4 * DM
LAM_INIT = 0.8 - 0.6 * math.exp(-0.3 * 0)
TRI = 3 * P


class Block:

    def __init__(self, size, loads):
        self.size, self.loads = size, loads


def rows_block(w, k0, nk, c0, nc):
    v = w.rearrange("(c p) n -> p c n", p=P)
    a = nk // 2
    return Block(nk * nc, [(lambda t, lo=lo, hi=hi: t[:, lo * nc:hi * nc].rearrange("p (k n) -> p k n", n=nc),
                            v[:, k0 + lo:k0 + hi, c0:c0 + nc]) for lo, hi in ((0, a), (a, nk))])


def pair_block(wa, wb, k0, nk, ca, cb, nc):
    out = []
    for side, (w, c) in enumerate(((wa, ca), (wb, cb))):
        v = w.rearrange("(c p) n -> p c n", p=P)
        out.append((lambda t, s=side: t[:, 0:nk * 2 * nc].rearrange("p (k s n) -> p k s n", s=2, n=nc)[:, :, s, :],
                    v[:, k0:k0 + nk, bass.ds(c, nc)]))
    return Block(nk * 2 * nc, out)


class Position:

    def __init__(self):
        self.n = 0


class Chain:

    def __init__(self, eng, sem):
        self.eng, self.sem, self.n = eng, sem, 0

    def mark(self, ins):
        ins.then_inc(self.sem, 1)
        self.n += 1

    def wait(self):
        self.eng.wait_ge(self.sem, self.n)

    def link(self, ins):
        self.mark(ins)
        self.wait()


def build(nc, x, positions, norm_w, ffn_w_gate, ffn_w_up, ffn_w_down, ssm_w_in, ssm_conv_w,
          ssm_conv_b, ssm_dt_bias, ssm_a_log, ssm_d, ssm_norm_w, ssm_w_out, mla_w_in, mla_q_a_norm,
          mla_kv_a_norm, mla_w_q_b, mla_w_kv_b, mla_q_norm, mla_k_norm, mla_w_out, norm_gains_2,
          w_in_2, mlstm_conv_2, mlstm_gate_bias_2, diff_lambda_2, diff_subln_2, w_mlstm_out_2,
          w_diff_out_2, w_ret_out_2, w_out_2, w_ffn_in_2, w_ffn_out_2, out):
    ctx = ExitStack()
    with ctx:
        ctx.enter_context(nc.allow_non_contiguous_dma(reason="small tables and narrow columns"))

        def sb(name, shape, dt=FP32, where=ctx):
            return where.enter_context(nc.sbuf_tensor(name, shape, dt))

        def sem(name):
            return ctx.enter_context(nc.semaphore(name))

        def sems(prefix, names):
            return {n: sem(f"{prefix}_{n}") for n in names.split()}

        blocks = []
        in2 = w_in_2[0]

        def ffn_blocks(wg, wu, cu, wd):
            n0 = len(blocks)
            def gate_up(j):
                return [pair_block(wg, wu, h * 4, 4, j * FCH, cu + j * FCH, FCH) for h in range(2)]
            def down(j):
                return rows_block(wd, 2 * j, 2, 0, DM)
            blocks.extend(gate_up(0))
            for j in range(1, NFF):
                blocks.extend(gate_up(j) + [down(j - 1)])
            blocks.append(down(NFF - 1))
            return n0

        def down_block(wd, j):
            v = wd.rearrange("(c p) n -> p c n", p=P)
            return Block(BLK, [(lambda t, h=h: t[:, h * DM:(h + 1) * DM].rearrange("p (k n) -> p k n", k=1),
                                v[:, bass.ds(2 * j + h, 1), :]) for h in range(2)])

        def natural_blocks(w, c0, chunks, width=512):
            n0 = len(blocks)
            for c in range(chunks):
                for h in range(2):
                    blocks.append(rows_block(w, 4 * h, 4, c0 + c * width, width))
            return n0

        def feature_blocks(w, c0, pairs):
            n0 = len(blocks)
            for c in range(pairs):
                blocks.append(rows_block(w, 0, KD, c0 + c * 2 * P, 2 * P))
            return n0

        def out_blocks(w, ks):
            n0 = len(blocks)
            for c in range(ks // 2):
                blocks.append(rows_block(w, 2 * c, 2, 0, DM))
            return n0

        FFN_W = [(ffn_w_gate[0, 0], ffn_w_up[0, 0], ffn_w_down[0, 0]),
                 (ffn_w_gate[0, 1], ffn_w_up[0, 1], ffn_w_down[0, 1]),
                 (ffn_w_gate[1, 0], ffn_w_up[1, 0], ffn_w_down[1, 0]),
                 (ffn_w_gate[1, 1], ffn_w_up[1, 1], ffn_w_down[1, 1]),
                 (w_ffn_in_2[0], w_ffn_in_2[0], w_ffn_out_2[0])]
        N = {}
        def ffn_add(i):
            wg, wu, wd = FFN_W[i]
            N[f"ffn{i}"] = ffn_blocks(wg, wu, FF if i == 4 else 0, wd)
        ffn_add(0)
        win = ssm_w_in[0]
        N["dt"] = len(blocks)
        blocks.append(rows_block(win, 0, KD, D_INNER + XBC, SSM_HEADS))
        N["bc"] = feature_blocks(win, 2 * D_INNER, 8)
        N["xs"] = feature_blocks(win, D_INNER, 8)
        N["z"] = natural_blocks(win, 0, 4)
        N["ssm_out"] = out_blocks(ssm_w_out[0], D_INNER // P)
        ffn_add(1)
        ffn_add(2)
        mw = mla_w_in[0]
        N["cq"] = natural_blocks(mw, 0, 1, QL)
        N["kvr"] = natural_blocks(mw, QL, 1, KVL + DR)
        N["wq"] = len(blocks)
        for c in range(3):
            blocks.append(rows_block(mla_w_q_b[0], 0, 3, c * 512, 512))
        N["wkv"] = len(blocks)
        for c in range(2):
            blocks.append(rows_block(mla_w_kv_b[0], 0, 2, c * 1024, 1024))
        N["mla_out"] = out_blocks(mla_w_out[0], KD)
        ffn_add(3)
        N["if"] = len(blocks)
        blocks.append(rows_block(in2, 0, KD, C_MI, 2 * LH))
        N["mqk"] = feature_blocks(in2, C_MQ, 8)
        N["mv"] = natural_blocks(in2, C_MV, 2)
        N["mo"] = natural_blocks(in2, C_MO, 2)
        N["gm"] = natural_blocks(in2, C_G, 2)
        N["mlstm_out"] = out_blocks(w_mlstm_out_2[0], KD)
        N["dqk"] = feature_blocks(in2, C_DQ, 8)
        N["dv"] = natural_blocks(in2, C_DV, 2)
        N["gd"] = natural_blocks(in2, C_G + DM, 2)
        N["diff_out"] = out_blocks(w_diff_out_2[0], KD)
        N["rqk"] = feature_blocks(in2, C_RQ, 8)
        N["rv"] = natural_blocks(in2, C_RV, 2)
        N["rg"] = natural_blocks(in2, C_RG, 2)
        N["gr"] = natural_blocks(in2, C_G + 2 * DM, 2)
        N["ret_out"] = out_blocks(w_ret_out_2[0], KD)
        N["y_out"] = out_blocks(w_out_2[0], KD)
        ffn_add(4)
        NB = len(blocks)

        raw = [sb(f"raw{s}", [P, BLK]) for s in range(SLOTS)]
        whi = [sb(f"whi{s}", [P, BLK], FP32R) for s in range(SLOTS)]
        wlo = [sb(f"wlo{s}", [P, BLK], FP32R) for s in range(SLOTS)]
        raw_loaded = [sem(f"raw_loaded{s}") for s in range(SLOTS)]
        hi_done, lo_done, block_used = sem("hi_done"), sem("lo_done"), sem("block_used")

        xs_ = sb("x_sb", [P, NT, DM])
        xn = sb("xn", [P, NT, DM])
        XTh = sb("XTh", [P, KD, SEQ], FP32R)
        XTl = sb("XTl", [P, KD, SEQ], FP32R)
        ident = sb("ident", [P, P])
        causal = sb("causal", [P, TRI])
        neghalf = sb("neghalf", [P, 16])
        ones = sb("ones", [P, SEQ])
        rows = [sb(f"rows{i}", [P, P]) for i in range(3)]
        cols = [sb(f"cols{i}", [P, P]) for i in range(3)]
        s_x, s_rows, s_rowt, s_rowc, s_const, s_out, s_gain = (
            sem(n) for n in "x_in rows_in rows_turned cols_done consts gout gain_in".split())
        NROW = [(norm_w.rearrange("i m (c p) -> (i m c) p", p=P), 0, 0),
                (norm_gains_2.rearrange("i m (c p) -> (i m c) p", p=P), 0, 48),
                (ssm_conv_b.rearrange("i (c p) -> (i c) p", p=P), 0, 80),
                (ssm_norm_w.rearrange("i (c p) -> (i c) p", p=P), 0, 112),
                (ssm_conv_w.rearrange("i k (c p) -> (i k c) p", p=P), 1, 0),
                (mlstm_conv_2.rearrange("i k (c p) -> (i k c) p", p=P), 2, 0),
                (mla_q_a_norm.rearrange("i (c p) -> (i c) p", p=P), 2, 64),
                (mla_kv_a_norm.rearrange("i (c p) -> (i c) p", p=P), 2, 67)]
        ROWS_IN = [P, P, 69]

        PS = ctx.enter_context(nc.psum_tensor("PS", [P, 8, 512], FP32))
        psD = PS[:, 0:4, :]
        psG = PS[:, 4:6, :]
        psT = PS[:, 6, :]
        psS = PS[:, 7, :]
        flatD = PS[:, 0:4, :].rearrange("p b n -> p (b n)")
        flatG = PS[:, 4:8, :].rearrange("p b n -> p (b n)")

        pe_own, act_own, dve_own, pool_own = (sem(f"{e}_own") for e in ("pe", "act", "dve", "pool"))

        ff_s = sb("ff_s", [P, NT, FCH])
        ff_a = sb("ff_a", [P, NT, FCH])
        aTh = sb("aTh", [P, 2 * SEQ], FP32R)
        aTl = sb("aTl", [P, 2 * SEQ], FP32R)
        stat = sb("stat", [P, NT])
        var = sb("var", [P, NT])
        rstd = sb("rstd", [P, NT])

        F_NAMES = "silu_done a_done t_done ah_done al_done x_done"
        N_NAMES = "sq_done var_done rstd_done n_done t_done h_done l_done"
        F, S_N = sems("ffn", F_NAMES), sems("norm", N_NAMES)

        def normed(i, k):
            return S_N["l_done"], KD * i + k + 1

        def load_block(sp, b, n, it=0):
            if n >= SLOTS or not isinstance(it, int):
                sp.wait_ge(lo_done, n + 1 - SLOTS + SLOTS * it)
            for place, src in b.loads:
                sp.dma_start(place(raw[n % SLOTS]), src).then_inc(raw_loaded[n % SLOTS], 16)

        def split_hi(act, n, it=0):
            s, size = n % SLOTS, blocks[n].size
            act.wait_ge(raw_loaded[s], 32 * (n // SLOTS + 1) + 32 * it)
            if n >= SLOTS or not isinstance(it, int):
                act.wait_ge(block_used, n + 1 - SLOTS + SLOTS * it)
            act.activation(whi[s][:, 0:size], raw[s][:, 0:size], ACT.Copy).then_inc(hi_done, 1)

        def split_lo(dve, n, it=0):
            s, size = n % SLOTS, blocks[n].size
            dve.wait_ge(hi_done, n + 1 + SLOTS * it)
            dve.tensor_tensor(wlo[s][:, 0:size], raw[s][:, 0:size], whi[s][:, 0:size].bitcast(FP32),
                              ALU.subtract).then_inc(lo_done, 1)

        def wait_block(pe, n, it=0):
            pe.wait_ge(lo_done, n + 1 + SLOTS * it)

        def mm3(pe, o, lh, ll, rh, rl, start, stop, **kw):
            pe.matmul(o, lh, rh, start=start, stop=False, **kw)
            pe.matmul(o, lh, rl, start=False, stop=False, **kw)
            return pe.matmul(o, ll, rh, start=False, stop=stop, **kw)

        def mul_rows(pe, n, it, k0, nk, width, banks, first, last, Xh=XTh, Xl=XTl, ready=None):
            s = n % SLOTS
            wait_block(pe, n, it)
            for k in range(nk):
                if ready is not None:
                    pe.wait_ge(*ready(k0 + k))
                sl = slice(k * width, (k + 1) * width)
                for t in range(NT):
                    ts_ = slice(t * P, (t + 1) * P)
                    m = mm3(pe, banks[t], Xh[:, k0 + k, ts_], Xl[:, k0 + k, ts_], whi[s][:, sl], wlo[s][:, sl],
                            first and k == 0, last and k == nk - 1)
            m.then_inc(block_used, 1)
            return m

        def mul_out(pe, n, it, lefts, first, last, bank=lambda t, c: psD[:, 2 * t + c, :]):
            s = n % SLOTS
            wait_block(pe, n, it)
            for k in range(2):
                lh, ll = lefts[k]
                for t in range(NT):
                    for c in range(2):
                        sl = slice(k * DM + c * 512, k * DM + (c + 1) * 512)
                        m = mm3(pe, bank(t, c), lh(t), ll(t), whi[s][:, sl], wlo[s][:, sl],
                                first and k == 0, last and k == 1)
            m.then_inc(block_used, 1)
            return m

        def mul_features(pe, n, bank):
            s = n % SLOTS
            wait_block(pe, n)
            for c in range(2):
                for k in range(KD):
                    sl = slice(k * 2 * P + c * P, k * 2 * P + (c + 1) * P)
                    o = bank[:, c * SEQ:(c + 1) * SEQ]
                    pe.matmul(o, whi[s][:, sl], XTh[:, k, :], start=(k == 0), stop=False)
                    pe.matmul(o, whi[s][:, sl], XTl[:, k, :], start=False, stop=False)
                    m = pe.matmul(o, wlo[s][:, sl], XTh[:, k, :], start=False, stop=(k == KD - 1))
            m.then_inc(block_used, 1)
            return m

        AT = [(lambda t, k=k: aTh[:, k * SEQ + t * P:k * SEQ + (t + 1) * P],
               lambda t, k=k: aTl[:, k * SEQ + t * P:k * SEQ + (t + 1) * P]) for k in range(2)]

        def ffn_pe(pe, i, norm):
            n0, f0 = N[f"ffn{i}"], NFF * i
            guard = [psG[:, t, :] for t in range(NT)]
            mul_rows(pe, n0, 0, 0, 4, 512, guard, True, False, ready=lambda k: normed(norm, k))
            mul_rows(pe, n0 + 1, 0, 4, 4, 512, guard, False, True, ready=lambda k: normed(norm, k))

            def turn(j):
                pe.wait_ge(F["a_done"], f0 + j + 1)
                for k in range(2):
                    for t in range(NT):
                        m = pe.transpose(psT[:, (2 * k + t) * P:(2 * k + t + 1) * P],
                                         ff_a[:, t, k * P:(k + 1) * P], ident[:, :])
                m.then_inc(F["t_done"], 1)

            def step(j, first=False):
                turn(j)
                mul_rows(pe, n0 + 2, j, 0, 4, 512, guard, True, False)
                mul_rows(pe, n0 + 3, j, 4, 4, 512, guard, False, True)
                pe.wait_ge(F["al_done"], f0 + j + 1)
                mul_out(pe, n0 + 4, j, AT, first, False)

            step(0, True)
            with pe.Fori(1, NFF - 1) as j:
                step(j)
            turn(NFF - 1)
            pe.wait_ge(F["al_done"], f0 + NFF)
            mul_out(pe, n0 + 3 * NFF - 1, 0, AT, False, True)

        def ffn_act(act, i, at):
            n0, f0 = N[f"ffn{i}"], NFF * i

            def silu(j, up):
                act.wait_ge(block_used, up + 1)
                act.activation(ff_s[:, :, :], psG[:, :, 0:FCH], ACT.Silu).then_inc(F["silu_done"], 1)

            def left_hi(j):
                act.wait_ge(F["t_done"], f0 + j + 1)
                act.activation(aTh[:, :], psT, ACT.Copy).then_inc(F["ah_done"], 1)

            hi_upto(act, at, n0 + 2)
            silu(0, n0 + 1)
            with act.Fori(0, NFF - 1) as j:
                left_hi(j)
                for c in range(3):
                    split_hi(act, n0 + 3 + c, j)
                silu(j + 1, n0 + 3 + 3 * j)
            at.n = n0 + 3 * NFF
            left_hi(NFF - 1)
            hi_upto(act, at, at.n + 1)

        def ffn_dve(dve, i, at, own):
            n0, f0 = N[f"ffn{i}"], NFF * i

            def gate(j):
                dve.wait_ge(F["silu_done"], f0 + j + 1)
                dve.tensor_tensor(ff_a[:, :, :], psG[:, :, FCH:2 * FCH], ff_s[:, :, :], ALU.mult)\
                   .then_inc(F["a_done"], 1)

            def left_lo(j):
                dve.wait_ge(F["ah_done"], f0 + j + 1)
                dve.tensor_tensor(aTl[:, :], psT, aTh[:, :].bitcast(FP32), ALU.subtract)\
                   .then_inc(F["al_done"], 1)

            lo_upto(dve, at, n0 + 2)
            gate(0)
            with dve.Fori(0, NFF - 1) as j:
                left_lo(j)
                for c in range(3):
                    split_lo(dve, n0 + 3 + c, j)
                gate(j + 1)
            at.n = n0 + 3 * NFF
            left_lo(NFF - 1)
            lo_upto(dve, at, at.n + 1)
            dve.wait_ge(block_used, n0 + 3 * NFF)
            if i < 4:
                dve.scalar_tensor_tensor(out=xs_[:, :, :].rearrange("p t n -> p (t n)"), in0=flatD, scalar=0.5,
                                         in1=xs_[:, :, :].rearrange("p t n -> p (t n)"),
                                         op0=ALU.mult, op1=ALU.add).then_inc(F["x_done"], 1)

        def hi_upto(act, at, n):
            while at.n <= min(n, NB - 1):
                split_hi(act, at.n)
                at.n += 1

        def lo_upto(dve, at, n):
            while at.n <= min(n, NB - 1):
                split_lo(dve, at.n)
                at.n += 1

        def norm_act(act, i, x_ready, col):
            S = S_N
            act.wait_ge(*x_ready)
            for t in range(NT):
                act.activation(xn[:, t, :], xs_[:, t, :], ACT.Square, accum_out=stat[:, t:t + 1])\
                   .then_inc(S["sq_done"], 1)
            for c in range(KD):
                act.wait_ge(S["t_done"], 4 * i + c // 2 + 1)
                act.activation(XTh[:, c, :], flatD[:, c * SEQ:(c + 1) * SEQ], ACT.Copy,
                               scale=cols[0][:, col + c:col + c + 1]).then_inc(S["h_done"], 1)

        def norm_dve(dve, i, col):
            S = S_N
            dve.wait_ge(S["sq_done"], NT * (i + 1))
            dve.tensor_scalar(var[:, :], stat[:, :], 1.0 / DM, EPS, ALU.mult, ALU.add).then_inc(S["var_done"], 1)
            dve.wait_ge(S["rstd_done"], i + 1)
            for t in range(NT):
                dve.tensor_scalar(xn[:, t, :], xs_[:, t, :], rstd[:, t:t + 1], None, ALU.mult)\
                   .then_inc(S["n_done"], 1)
            for c in range(KD):
                dve.wait_ge(S["h_done"], KD * i + 2 * (c // 2) + 2)
                dve.scalar_tensor_tensor(out=XTl[:, c, :], in0=flatD[:, c * SEQ:(c + 1) * SEQ],
                                         scalar=cols[0][:, col + c:col + c + 1], in1=XTh[:, c, :].bitcast(FP32),
                                         op0=ALU.mult, op1=ALU.subtract).then_inc(S["l_done"], 1)

        def norm_pool(pool, i):
            S = S_N
            pool.wait_ge(S["var_done"], i + 1)
            pool.tensor_tensor(rstd[:, :], var[:, :], neghalf[:, 0:NT], ALU.pow).then_inc(S["rstd_done"], 1)

        def norm_pe(pe, i):
            S = S_N
            pe.wait_ge(S["n_done"], NT * (i + 1))
            for c in range(KD):
                for t in range(NT):
                    m = pe.transpose(flatD[:, (2 * c + t) * P:(2 * c + t + 1) * P],
                                     xn[:, t, c * P:(c + 1) * P], ident[:, :])
                if c % 2:
                    m.then_inc(S["t_done"], 1)

        def left_pe(pe, S, src, ready, base=0):
            for b in range(4):
                pe.wait_ge(*ready(b))
                for c in range(2):
                    for t in range(NT):
                        k = 2 * b + c
                        m = pe.transpose(flatG[:, (2 * k + t) * P:(2 * k + t + 1) * P], src[:, t, k * P:(k + 1) * P],
                                         ident[:, :])
                m.then_inc(S["lt"], 1)

        def left_act(act, S, Xh, base=0):
            for b in range(4):
                act.wait_ge(S["lt"], base + b + 1)
                act.activation(Xh[:, 2 * b:2 * b + 2, :], PS[:, 4 + b, :].rearrange("p (k n) -> p k n", k=2), ACT.Copy)\
                   .then_inc(S["lh"], 1)

        def left_dve(dve, S, Xh, Xl, base=0):
            for b in range(4):
                dve.wait_ge(S["lh"], base + b + 1)
                dve.tensor_tensor(Xl[:, 2 * b:2 * b + 2, :], PS[:, 4 + b, :].rearrange("p (k n) -> p k n", k=2),
                                  Xh[:, 2 * b:2 * b + 2, :].bitcast(FP32), ALU.subtract).then_inc(S["ll"], 1)

        def project_pe(pe, S, n, Xh, Xl, base=0):
            for b in range(4):
                pe.wait_ge(S["ll"], base + b + 1)
                left = [(lambda t, k=k: Xh[:, k, t * P:(t + 1) * P], lambda t, k=k: Xl[:, k, t * P:(t + 1) * P])
                        for k in (2 * b, 2 * b + 1)]
                mul_out(pe, n + b, 0, left, b == 0, b == 3)

        posi = sb("posi", [P, NT], I32)
        posf = sb("posf", [P, NT])
        freq = sb("freq", [P, HR])
        ang = sb("ang", [P, NT, HR])
        turns = sb("turns", [P, NT, HR])
        trig = sb("trig", [P, 2, NT, HR])
        qn_row = sb("qn_row", [P, DQ])
        kn_row = sb("kn_row", [P, DQ])
        mss = sb("mss", [P, 3, NT])
        mvar = sb("mvar", [P, 3, NT])
        mrs = sb("mrs", [P, 3, NT])
        hss = sb("hss", [P, 3, NT * MH])
        hvar = sb("hvar", [P, 3, NT * MH])
        hrs = sb("hrs", [P, 3, NT * MH])
        krot = sb("krot", [P, NT, DR])
        ktmp = sb("ktmp", [P, 4, NT, HR])
        mx = sb("mx", [P, 2, NT])
        nmx = sb("nmx", [P, 2, NT])
        psum_ = sb("prob_sum", [P, NT, MH])
        rsum = sb("rsum", [P, NT, MH])
        notyet = sb("notyet", [P, TRI])
        ssm_ctx = ExitStack()
        conv_acc = sb("conv_acc", [P, 2, 2, SEQ])
        dt_nat = ff_a[:, :, 0:SSM_HEADS]
        hrow = sb("hrow", [SSM_HEADS, 8, SEQ], where=ssm_ctx)
        H_X, H_E, H_LN, H_D, H_Q, H_DT, H_DA, H_ACS = range(8)
        dtb = sb("dtb", [SSM_HEADS, 1], where=ssm_ctx)
        alog = sb("alog", [SSM_HEADS, 1], where=ssm_ctx)
        expa = sb("expa", [SSM_HEADS, 1], where=ssm_ctx)
        dskip = sb("dskip", [P, SSM_HEADS], where=ssm_ctx)
        hcol = sb("hcol", [P, 2, NT, SSM_HEADS], where=ssm_ctx)
        xs_t = sb("xs_t", [P, 3, 2, SEQ], where=ssm_ctx)
        zs = sb("zs", [P, NT, D_INNER], where=ssm_ctx)
        decay = sb("decay", [P, SSM_R * TRI], where=ssm_ctx)
        mix = sb("mix", [P, SSM_R * TRI], where=ssm_ctx)
        cb = sb("cb", [P, TRI], where=ssm_ctx)
        dxs = sb("dxs", [P, 2, NT, SSM_R * SSM_P], where=ssm_ctx)
        gss = sb("gss", [P, SSM_G, NT], where=ssm_ctx)
        gvar = sb("gvar", [P, SSM_G, NT], where=ssm_ctx)
        grstd = sb("grstd", [P, SSM_G, NT], where=ssm_ctx)
        sq_junk = ff_s
        with ExitStack() as sub:
            BC = sb("BC", [P, 2 * SSM_G, SEQ], where=sub)
            xs_nat = sb("xs_nat", [P, NT, D_INNER], where=sub)
        with ExitStack() as sub:
            gTh = sb("gTh", [P, D_INNER // P, SEQ], FP32R, where=sub)
            gTl = sb("gTl", [P, D_INNER // P, SEQ], FP32R, where=sub)
        ssm_ctx.close()
        A = sems("ssm", "in dtn dtt xb e dta dtN coln acc tap silu turned nat z b seg cbm e_done m dx y yz sq var r gs "
                        "gt gh gl x_done")
        NXB = 16
        HALF = SSM_R * SEQ

        def xbc_tiles(i):
            return (16 + 2 * i, 17 + 2 * i) if i < 8 else (2 * (i - 8), 2 * (i - 8) + 1)

        def ssm_pe(pe):
            nd, nx, nz, no = N["dt"], N["bc"], N["z"], N["ssm_out"]
            mul_rows(pe, nd, 0, 0, KD, SSM_HEADS, [psT[:, 0:SSM_HEADS], psS[:, 0:SSM_HEADS]], True, True,
                     ready=lambda k: normed(1, k))
            pe.wait_ge(A["dtn"], 1)
            for t in range(NT):
                m = pe.transpose(psT[0:SSM_HEADS, t * P:(t + 1) * P], dt_nat[:, t, :], ident[:, :])
            m.then_inc(A["dtt"], 1)
            for i in range(NXB + 2):
                if i < NXB:
                    if i >= 4:
                        pe.wait_ge(A["tap"], i - 3)
                    mul_features(pe, nx + i, psD[:, i % 4, :])
                if i == 2:
                    pe.wait_ge(A["dta"], 1)
                    for kind, row in enumerate((H_DT, H_ACS)):
                        for t in range(NT):
                            c = (kind * NT + t) * SSM_HEADS
                            m = pe.transpose(psS[:, c:c + SSM_HEADS], hrow[:, row, t * P:(t + 1) * P],
                                             ident[0:SSM_HEADS, 0:SSM_HEADS])
                    m.then_inc(A["dtN"], 1)
                b = i - 10
                if b >= 0:
                    pe.wait_ge(A["silu"], 8 + b + 1)
                    if b >= 2:
                        pe.wait_ge(A["nat"], b - 1)
                    for t in range(NT):
                        for c in range(2):
                            m = pe.transpose(psG[:, b % 2, t * SEQ + c * P:t * SEQ + (c + 1) * P],
                                             xs_t[:, b % 3, c, t * P:(t + 1) * P], ident[:, :])
                    m.then_inc(A["turned"], 1)

            def z_block(k):
                q, h = k // 2, k % 2
                if h == 0:
                    if q < 2:
                        pe.wait_ge(A["tap"], 14 + 2 * q)
                    else:
                        pe.wait_ge(A["z"], q - 1)
                mul_rows(pe, nz + k, 0, 4 * h, 4, 512, [psD[:, (2 * q) % 4 + t, :] for t in range(NT)], h == 0, h == 1)

            def scores(g):
                if g == 0:
                    pe.wait_ge(A["coln"], 1)
                    pe.wait_ge(A["nat"], 8)
                else:
                    pe.wait_ge(A["seg"], g)
                    pe.wait_ge(A["cbm"], g)
                for r in range(SSM_R):
                    h = g * SSM_R + r
                    pe.matmul(psG[:, r // 2, (r % 2) * SEQ:(r % 2 + 1) * SEQ],
                              ident[0:SSM_HEADS, h:h + 1].to_broadcast([SSM_HEADS, P]), hrow[:, H_ACS, :],
                              start=True, stop=True)
                pe.matmul(psT[:, 0:SEQ], BC[:, g, 0:P], BC[:, SSM_G + g, :], start=True, stop=True)
                pe.matmul(psT[:, SEQ:TRI], BC[:, g, P:SEQ], BC[:, SSM_G + g, P:SEQ], start=True, stop=True)\
                  .then_inc(A["b"], 1)

            def outputs(g):
                pe.wait_ge(A["m"], g + 1)
                pe.wait_ge(A["dx"], g + 1)
                if g >= 1:
                    pe.wait_ge(A["yz"], g)
                W = SSM_R * SSM_P
                for t in range(NT):
                    pe.matmul(psS[:, t * W:(t + 1) * W], ident[:, :], dxs[:, g % 2, t, :], start=True, stop=False)
                    for r in range(SSM_R):
                        o = psS[:, t * W + r * SSM_P:t * W + (r + 1) * SSM_P]
                        hc = slice((g * SSM_R + r) * SSM_P, (g * SSM_R + r + 1) * SSM_P)
                        m = pe.matmul(o, mix[:, r * SEQ + t * P:r * SEQ + (t + 1) * P], xs_nat[:, 0, hc],
                                      start=False, stop=(t == 0 and r == 3))
                        if t == 1:
                            m = pe.matmul(o, mix[:, HALF + r * P:HALF + (r + 1) * P], xs_nat[:, 1, hc],
                                          start=False, stop=(r == 3))
                m.then_inc(A["y"], 1)

            scores(0)
            z_block(0)
            z_block(1)
            for g in range(SSM_G):
                outputs(g)
                if g + 1 < SSM_G:
                    scores(g + 1)
                if g + 2 < 8:
                    z_block(g + 2)

            def turn(g):
                pe.wait_ge(A["gs"], g + 1)
                if g >= 2:
                    pe.wait_ge(A["gl"], g - 1)
                for c in range(2):
                    for t in range(NT):
                        m = pe.transpose(psG[:, g % 2, c * SEQ + t * P:c * SEQ + (t + 1) * P],
                                         zs[:, t, (2 * g + c) * P:(2 * g + c + 1) * P], ident[:, :])
                m.then_inc(A["gt"], 1)

            turn(0)
            pe.wait_ge(A["z"], 4)
            for g in range(SSM_G):
                if g + 1 < SSM_G:
                    turn(g + 1)
                pe.wait_ge(A["gl"], g + 1)
                left = [(lambda t, k=k: gTh[:, k, t * P:(t + 1) * P], lambda t, k=k: gTl[:, k, t * P:(t + 1) * P])
                        for k in (2 * g, 2 * g + 1)]
                mul_out(pe, no + g, 0, left, g == 0, g == SSM_G - 1)

        def conv_act(act, S, i, n, tiles, taps, bias, dst, prev):
            if n is not None:
                act.wait_ge(block_used, n + 1)
                if i >= 2:
                    act.wait_ge(S["silu"], i - 1)
                for c in range(2):
                    m = act.activation(conv_acc[:, i % 2, c, :], psD[:, i % 4, c * SEQ:(c + 1) * SEQ], ACT.Identity,
                                       scale=taps(tiles[c], CONV_K - 1), bias=bias(tiles[c]))
                m.then_inc(S["acc"], 1)
            if prev is not None:
                act.wait_ge(S["tap"], i)
                act.activation(prev, conv_acc[:, (i - 1) % 2, :, :], ACT.Silu).then_inc(S["silu"], 1)

        def conv_dve(dve, own, S, i, tiles, taps):
            dve.wait_ge(S["acc"], i + 1)
            for j in range(CONV_K - 2, -1, -1):
                sh = CONV_K - 1 - j
                for c in range(2):
                    a = conv_acc[:, i % 2, c, sh:SEQ]
                    m = dve.scalar_tensor_tensor(out=a, in0=psD[:, i % 4, c * SEQ:(c + 1) * SEQ - sh],
                                                 scalar=taps(tiles[c], j), in1=a, op0=ALU.mult, op1=ALU.add)
                if j:
                    own.link(m)
                else:
                    m.then_inc(S["tap"], 1)

        def ssm_taps(ct, j):
            return cols[1][:, j * (XBC // P) + ct:j * (XBC // P) + ct + 1]

        def ssm_act(act, at, own):
            nd, nx, nz, no = N["dt"], N["bc"], N["z"], N["ssm_out"]
            hi_upto(act, at, nd + 2)
            act.wait_ge(block_used, nd + 1)
            act.activation(dt_nat, PS[:, 6:8, 0:SSM_HEADS], ACT.Copy).then_inc(A["dtn"], 1)
            act.wait_ge(A["in"], 48)
            act.activation(expa[:, :], alog[:, :], ACT.Exp).then_inc(A["e"], 1)
            act.wait_ge(A["xb"], 1)
            act.activation(hrow[:, H_E, :], hrow[:, H_Q, :], ACT.Exp, scale=-1.0).then_inc(A["e"], 1)
            act.wait_ge(A["e"], 2)
            act.activation(hrow[:, H_LN, :], hrow[:, H_E, :], ACT.Ln, bias=ones[0:SSM_HEADS, 0:1]).then_inc(A["e"], 1)
            for i in range(NXB + 1):
                hi_upto(act, at, nx + i + 2)
                if i - 1 < 8:
                    prev = BC[:, 2 * (i - 1):2 * i, :] if i else None
                else:
                    prev = xs_t[:, (i - 9) % 3, :, :]
                    if i - 9 >= 3:
                        act.wait_ge(A["turned"], i - 9 - 2)
                conv_act(act, A, i, nx + i if i < NXB else None, xbc_tiles(i) if i < NXB else None, ssm_taps,
                         lambda ct: cols[0][:, 80 + ct:81 + ct], None, prev)
                if i >= 11:
                    ssm_nat(act, i - 11)
            for b in range(6, 8):
                ssm_nat(act, b)
            for g in range(-1, SSM_G):
                hi_upto(act, at, nz + g + 3)
                if g + 1 < SSM_G:
                    act.wait_ge(A["seg"], g + 2)
                    act.activation(decay[:, :], decay[:, :], ACT.Exp).then_inc(A["e_done"], 1)
                if g >= 0:
                    act.wait_ge(A["yz"], g + 1)
                    for t in range(NT):
                        act.activation(sq_junk[:, t, :], zs[:, t, g * 256:(g + 1) * 256], ACT.Square,
                                       accum_out=gss[:, g, t:t + 1]).then_inc(A["sq"], 1)
                k = g + 2
                if k < 8 and k % 2:
                    act.wait_ge(block_used, nz + k + 1)
                    q = k // 2
                    act.activation(zs[:, :, q * 512:(q + 1) * 512], psD[:, (2 * q) % 4:(2 * q) % 4 + 2, :], ACT.Silu)\
                       .then_inc(A["z"], 1)
            for g in range(SSM_G):
                hi_upto(act, at, no + g + 1)
                act.wait_ge(A["gt"], g + 1)
                for c in range(2):
                    k = 2 * g + c
                    act.activation(gTh[:, k, :], psG[:, g % 2, c * SEQ:(c + 1) * SEQ], ACT.Copy,
                                   scale=cols[0][:, 112 + k:113 + k]).then_inc(A["gh"], 1)
            hi_upto(act, at, no + 9)

        def ssm_nat(act, b):
            act.wait_ge(A["turned"], b + 1)
            act.activation(xs_nat[:, :, b * 256:(b + 1) * 256],
                           psG[:, b % 2, :].rearrange("p (t n) -> p t n", t=NT), ACT.Copy).then_inc(A["nat"], 1)

        def ssm_dve(dve, at, own):
            nd, nx, nz, no = N["dt"], N["bc"], N["z"], N["ssm_out"]
            H = SSM_HEADS
            lo_upto(dve, at, nd + 2)
            dve.wait_ge(A["in"], 48)
            dve.wait_ge(A["dtt"], 1)
            own.link(dve.tensor_scalar(hrow[:, H_X, :], psT[0:H, 0:SEQ], dtb[:, 0:1], None, ALU.add))
            dve.scalar_tensor_tensor(out=hrow[:, H_Q, :], in0=hrow[:, H_X, :], scalar=-1.0, in1=hrow[:, H_X, :],
                                     op0=ALU.mult, op1=ALU.max).then_inc(A["xb"], 1)
            dve.wait_ge(A["e"], 3)
            own.link(dve.tensor_scalar(hrow[:, H_D, :], hrow[:, H_E, :], 1.0, -1.0, ALU.add, ALU.add))
            own.link(dve.tensor_scalar(hrow[:, H_Q, :], hrow[:, H_D, :], 1e-30, None, ALU.max))
            own.link(dve.reciprocal(hrow[:, H_Q, :], hrow[:, H_Q, :]))
            own.link(dve.tensor_tensor(hrow[:, H_Q, :], hrow[:, H_Q, :], hrow[:, H_E, :], ALU.mult))
            own.link(dve.tensor_tensor(hrow[:, H_Q, :], hrow[:, H_Q, :], hrow[:, H_LN, :], ALU.mult))
            own.link(dve.scalar_tensor_tensor(out=hrow[:, H_D, :], in0=hrow[:, H_D, :], scalar=0.0,
                                              in1=hrow[:, H_E, :], op0=ALU.is_equal, op1=ALU.mult))
            own.link(dve.tensor_tensor(hrow[:, H_Q, :], hrow[:, H_Q, :], hrow[:, H_D, :], ALU.add))
            own.link(dve.scalar_tensor_tensor(out=hrow[:, H_DT, :], in0=hrow[:, H_X, :], scalar=0.0,
                                              in1=hrow[:, H_Q, :], op0=ALU.max, op1=ALU.add))
            own.link(dve.tensor_scalar(hrow[:, H_DA, :], hrow[:, H_DT, :], expa[:, 0:1], -1.0, ALU.mult, ALU.mult))
            dve.tensor_tensor_scan(out=hrow[:, H_ACS, :], data0=ones[0:H, :], data1=hrow[:, H_DA, :], initial=0.0,
                                   op0=ALU.mult, op1=ALU.add).then_inc(A["dta"], 1)
            for i in range(NXB):
                lo_upto(dve, at, nx + i + 2)
                conv_dve(dve, own, A, i, xbc_tiles(i), ssm_taps)
                if i == 2:
                    dve.wait_ge(A["dtN"], 1)
                    dve.tensor_copy(hcol[:, :, :, :].rearrange("p k t h -> p (k t h)"), psS[:, 0:4 * H])\
                       .then_inc(A["coln"], 1)
            dve.wait_ge(A["coln"], 1)
            for g in range(-1, SSM_G):
                gs = slice(g * 256, (g + 1) * 256)
                lo_upto(dve, at, nz + g + 3)
                if g >= 0:
                    dve.wait_ge(A["y"], g + 1)
                    dve.wait_ge(A["z"], g // 2 + 1)
                    dve.tensor_tensor(zs[:, :, gs], psS.rearrange("p (t n) -> p t n", t=NT), zs[:, :, gs], ALU.mult)\
                       .then_inc(A["yz"], 1)
                if g + 1 < SSM_G:
                    dve.wait_ge(A["b"], g + 2)
                    if g >= 0:
                        dve.wait_ge(A["m"], g + 1)
                    for s, (c0, w) in enumerate(((0, SEQ), (P, P))):
                        for r in range(SSM_R):
                            h = (g + 1) * SSM_R + r
                            o = decay[:, r * SEQ:(r + 1) * SEQ] if s == 0 else decay[:, HALF + r * P:HALF + (r + 1) * P]
                            m = dve.tensor_scalar(o, psG[:, r // 2, (r % 2) * SEQ + c0:(r % 2) * SEQ + c0 + w],
                                                  hcol[:, 1, s, h:h + 1], 0.0, ALU.subtract, ALU.min)
                    m.then_inc(A["seg"], 1)
                    dve.tensor_tensor(cb[:, :], psT[:, 0:TRI], causal[:, :], ALU.mult).then_inc(A["cbm"], 1)
                if g >= 0:
                    dve.wait_ge(A["sq"], 2 * g + 2)
                    dve.tensor_scalar(gvar[:, g, :], gss[:, g, :], 1.0 / 256, EPS, ALU.mult, ALU.add)\
                       .then_inc(A["var"], 1)
                if g + 1 < SSM_G:
                    dve.wait_ge(A["e_done"], g + 2)
                    dve.wait_ge(A["cbm"], g + 2)
                    for s in range(NT):
                        for r in range(SSM_R):
                            h = (g + 1) * SSM_R + r
                            sl = slice(r * SEQ, (r + 1) * SEQ) if s == 0 else slice(HALF + r * P, HALF + (r + 1) * P)
                            m = dve.scalar_tensor_tensor(out=mix[:, sl], in0=decay[:, sl], scalar=hcol[:, 0, s, h:h + 1],
                                                         in1=cb[:, 0:SEQ] if s == 0 else cb[:, SEQ:TRI],
                                                         op0=ALU.mult, op1=ALU.mult)
                    m.then_inc(A["m"], 1)
                if g >= 0:
                    dve.wait_ge(A["r"], g + 1)
                    for t in range(NT):
                        m = dve.tensor_scalar(zs[:, t, gs], zs[:, t, gs], grstd[:, g, t:t + 1], None, ALU.mult)
                    m.then_inc(A["gs"], 1)
            for g in range(SSM_G):
                lo_upto(dve, at, no + g + 1)
                dve.wait_ge(A["gh"], 2 * g + 2)
                for c in range(2):
                    k = 2 * g + c
                    m = dve.scalar_tensor_tensor(out=gTl[:, k, :], in0=psG[:, g % 2, c * SEQ:(c + 1) * SEQ],
                                                 scalar=cols[0][:, 112 + k:113 + k], in1=gTh[:, k, :].bitcast(FP32),
                                                 op0=ALU.mult, op1=ALU.subtract)
                m.then_inc(A["gl"], 1)
            lo_upto(dve, at, no + 9)
            dve.wait_ge(block_used, no + 8)
            dve.tensor_tensor(xs_[:, :, :].rearrange("p t n -> p (t n)"), flatD,
                              xs_[:, :, :].rearrange("p t n -> p (t n)"), ALU.add).then_inc(A["x_done"], 1)

        def ssm_pool(pool):
            def skip(g):
                if g >= 2:
                    pool.wait_ge(A["y"], g - 1)
                for t in range(NT):
                    m = pool.tensor_tensor(dxs[:, g % 2, t, :].rearrange("p (r n) -> p r n", r=SSM_R),
                                           xs_nat[:, t, g * 256:(g + 1) * 256].rearrange("p (r n) -> p r n", r=SSM_R),
                                           dskip[:, g * SSM_R:(g + 1) * SSM_R].unsqueeze(2)
                                           .to_broadcast([P, SSM_R, SSM_P]), ALU.mult)
                m.then_inc(A["dx"], 1)
            pool.wait_ge(A["in"], 48)
            pool.wait_ge(A["nat"], 8)
            skip(0)
            skip(1)
            for g in range(SSM_G):
                pool.wait_ge(A["var"], g + 1)
                pool.tensor_tensor(grstd[:, g, :], gvar[:, g, :], neghalf[:, 0:NT], ALU.pow).then_inc(A["r"], 1)
                if g + 2 < SSM_G:
                    skip(g + 2)

        mla_ctx = ExitStack()
        q_nat = sb("q_nat", [P, NT, MH, DQ], where=mla_ctx)
        k_nat = sb("k_nat", [P, NT, MH, DQ], where=mla_ctx)
        v_nat = sb("v_nat", [P, NT, MH, DV], where=mla_ctx)
        qT = sb("qT", [DQ, MH, SEQ], where=mla_ctx)
        kT = sb("kT", [DQ, MH, SEQ], where=mla_ctx)
        with ExitStack() as sub:
            cn = sb("cn", [P, NT, QL + KVL], where=sub)
            cTh = sb("cTh", [P, 5, SEQ], FP32R, where=sub)
            cTl = sb("cTl", [P, 5, SEQ], FP32R, where=sub)
        with ExitStack() as sub:
            sqh = sb("sqh", [P, NT, MH, DQ], where=sub)
        with ExitStack() as sub:
            sS = sb("sS", [P, 2, TRI], where=sub)
            prob = sb("prob", [P, 2, TRI], where=sub)
            probT = sb("probT", [P, 2, TRI], where=sub)
            rtmp = sb("rtmp", [P, 4, MH, HR], where=sub)
        mla_ctx.close()
        M = sems("mla", "in freq trig_in turned trig_out sq var r cn ct ch cl copied ksq sqs hred hr qs krr krd qr kb qt qtc "
                        "ktc s add nm e pt ptc o od lt lh ll x_done mask")
        RW = KVL + DR

        def mla_tables_pool(pool, own):
            for i in range(HR):
                m = pool.memset(freq[:, i:i + 1], float(np.float32(1.0) / np.float32(ROPE_THETA) ** np.float32(2 * i / DR)))
            own.mark(m)
            own.mark(pool.memset(notyet[:, :], 0.0))
            own.wait()
            pool.affine_select(out=notyet[:, 0:P], in_=notyet[:, 0:P], compare_op=ALU.is_ge, fill=-BIG, base=0,
                               pattern=[[-1, P]], channel_multiplier=1).then_inc(M["mask"], 1)
            pool.affine_select(out=notyet[:, 2 * P:TRI], in_=notyet[:, 2 * P:TRI], compare_op=ALU.is_ge, fill=-BIG,
                               base=0, pattern=[[-1, P]], channel_multiplier=1).then_inc(M["mask"], 1)

        def mla_tables_dve(dve, own):
            dve.wait_ge(M["in"], 48)
            dve.wait_ge(M["mask"], 2)
            own.link(dve.tensor_copy(posf[:, :], posi[:, :]))
            for t in range(NT):
                m = dve.tensor_scalar(ang[:, t, :], freq[:, :], posf[:, t:t + 1], None, ALU.mult)
            own.link(m)
            for k, shift in enumerate((0.0, 0.25)):
                n, r = turns[:, :, :], trig[:, k, :, :]
                own.link(dve.tensor_scalar(n, ang[:, :, :], 1.0 / (2 * math.pi), shift, ALU.mult, ALU.add))
                own.link(dve.tensor_scalar(n, n, ROUND, None, ALU.add))
                own.link(dve.tensor_scalar(n, n, -ROUND, None, ALU.add))
                own.link(dve.scalar_tensor_tensor(out=r, in0=n, scalar=-TWO_PI[0], in1=ang[:, :, :],
                                                  op0=ALU.mult, op1=ALU.add))
                for c in TWO_PI[1:]:
                    own.link(dve.scalar_tensor_tensor(out=r, in0=n, scalar=-c, in1=r, op0=ALU.mult, op1=ALU.add))
                own.link(dve.tensor_scalar(r, r, math.pi / 2 if k else 0.0, 3.1415925, ALU.add, ALU.min))
                dve.tensor_scalar(r, r, -3.1415925, None, ALU.max).then_inc(M["trig_in"], 1)
                dve.wait_ge(M["trig_in"], k + 1)

        def mla_tables_act(act):
            act.wait_ge(M["trig_in"], 2)
            act.activation(trig[:, :, :, :], trig[:, :, :, :], ACT.Sin).then_inc(M["trig_out"], 1)

        KV_BANKS = [[2, 3, 4, 5], [6, 7, 0, 1]]

        def mla_pe(pe):
            nq, nk = N["cq"], N["kvr"]
            G = [psG[:, t, 0:QL] for t in range(NT)]
            mul_rows(pe, nq, 0, 0, 4, QL, G, True, False, ready=lambda k: normed(4, k))
            mul_rows(pe, nq + 1, 0, 4, 4, QL, G, False, True, ready=lambda k: normed(4, k))
            H = [PS[:, 6 + t, 0:RW] for t in range(NT)]
            mul_rows(pe, nk, 0, 0, 4, RW, H, True, False)
            mul_rows(pe, nk + 1, 0, 4, 4, RW, H, False, True)
            pe.wait_ge(M["cn"], 4)
            for c in range(5):
                for t in range(NT):
                    m = pe.transpose(flatD[:, (2 * c + t) * P:(2 * c + t + 1) * P], cn[:, t, c * P:(c + 1) * P], ident[:, :])
                if c % 2 or c == 4:
                    m.then_inc(M["ct"], 1)
            pe.wait_ge(M["cl"], 5)
            QB = [psG, PS[:, 6:8, :], psD[:, 0:2, :]]
            for c in range(3):
                mul_rows(pe, N["wq"] + c, 0, 0, 3, 512, [QB[c][:, t, :] for t in range(NT)], True, True, Xh=cTh, Xl=cTl)
            left = [(lambda t, k=k: cTh[:, k, t * P:(t + 1) * P], lambda t, k=k: cTl[:, k, t * P:(t + 1) * P]) for k in (3, 4)]
            pe.wait_ge(M["copied"], 1)
            mul_out(pe, N["wkv"], 0, left, True, True, bank=lambda t, c: PS[:, KV_BANKS[0][2 * t + c], :])
            pe.wait_ge(M["copied"], 3)
            mul_out(pe, N["wkv"] + 1, 0, left, True, True, bank=lambda t, c: PS[:, KV_BANKS[1][2 * t + c], :])
            for i in range(MH // 2):
                for src, sem_, bank, done in ((k_nat, (M["kb"], 3), 4, M["ktc"]), (q_nat, (M["qr"], 1), 6, M["qtc"])):
                    pe.wait_ge(*sem_)
                    if src is q_nat:
                        pe.wait_ge(M["qs"], 1)
                    if i == 0:
                        pe.wait_ge(M["copied"], 11)
                    if i >= 2:
                        pe.wait_ge(done, i - 1)
                    for h in range(2):
                        for t in range(NT):
                            m = pe.transpose(PS[0:DQ, bank + i % 2, h * SEQ + t * P:h * SEQ + (t + 1) * P],
                                             src[:, t, 2 * i + h, :], ident[:, :])
                    m.then_inc(M["qt"], 1)
            for h in range(MH + 2):
                if h < MH:
                    if h == 0:
                        pe.wait_ge(M["ktc"], MH // 2)
                        pe.wait_ge(M["qtc"], MH // 2)
                    if h >= 2:
                        pe.wait_ge(M["nm"], h - 1)
                    pe.matmul(psG[:, h % 2, 0:P], qT[:, h, 0:P], kT[:, h, 0:P], start=True, stop=True)
                    pe.matmul(psG[:, h % 2, P:TRI], qT[:, h, P:SEQ], kT[:, h, :], start=True, stop=True)\
                      .then_inc(M["s"], 1)
                if 1 <= h <= MH:
                    g = h - 1
                    pe.wait_ge(M["e"], 2 * g + 2)
                    if g >= 2:
                        pe.wait_ge(M["ptc"], g - 1)
                    for c in range(3):
                        m = pe.transpose(PS[:, 6 + g % 2, c * P:(c + 1) * P], prob[:, g % 2, c * P:(c + 1) * P], ident[:, :])
                    m.then_inc(M["pt"], 1)
                if h >= 2:
                    g = h - 2
                    pe.wait_ge(M["ptc"], g + 1)
                    if g % 4 == 0 and g >= 8:
                        pe.wait_ge(M["od"], g // 4 - 1)
                    b = psD[:, (g // 4) % 2, :]
                    o = [b[:, t * 256 + (g % 4) * DV:t * 256 + (g % 4 + 1) * DV] for t in range(NT)]
                    pe.matmul(o[0], probT[:, g % 2, 0:P], v_nat[:, 0, g, :], start=True, stop=True)
                    pe.matmul(o[1], probT[:, g % 2, P:2 * P], v_nat[:, 0, g, :], start=True, stop=False)
                    pe.matmul(o[1], probT[:, g % 2, 2 * P:TRI], v_nat[:, 1, g, :], start=False, stop=True)\
                      .then_inc(M["o"], 1)
            left_pe(pe, M, xn, lambda b: (M["od"], b + 1))
            project_pe(pe, M, N["mla_out"], XTh, XTl)

        def mla_act(act, at, own):
            nq, nk = N["cq"], N["kvr"]
            hi_upto(act, at, nq + 3)
            act.wait_ge(block_used, nq + 2)
            for t in range(NT):
                act.activation(cn[:, t, 0:QL], psG[:, t, 0:QL], ACT.Square, accum_out=mss[:, 0, t:t + 1]).then_inc(M["sq"], 1)
            hi_upto(act, at, nk + 3)
            act.wait_ge(block_used, nk + 2)
            for t in range(NT):
                act.activation(cn[:, t, QL:QL + KVL], PS[:, 6 + t, 0:KVL], ACT.Square, accum_out=mss[:, 1, t:t + 1])\
                   .then_inc(M["sq"], 1)
                act.activation(krot[:, t, :], PS[:, 6 + t, KVL:RW], ACT.Square, accum_out=mss[:, 2, t:t + 1])\
                   .then_inc(M["sq"], 1)
            for c in range(5):
                act.wait_ge(M["ct"], c // 2 + 1)
                act.activation(cTh[:, c, :], flatD[:, c * SEQ:(c + 1) * SEQ], ACT.Copy, scale=cols[2][:, 64 + c:65 + c])\
                   .then_inc(M["ch"], 1)
            QB = [psG, PS[:, 6:8, :], psD[:, 0:2, :]]
            qf = q_nat[:, :, :, :].rearrange("p t h d -> p t (h d)")
            for c in range(3):
                hi_upto(act, at, N["wq"] + c + 2)
                act.wait_ge(block_used, N["wq"] + c + 1)
                act.activation(qf[:, :, c * 512:(c + 1) * 512], QB[c], ACT.Copy).then_inc(M["copied"], 1)
            act.wait_ge(M["copied"], 3)
            hi_upto(act, at, N["wkv"] + 2)
            act.wait_ge(block_used, N["wkv"])
            for c in range(2):
                hi_upto(act, at, N["wkv"] + c + 2)
                act.wait_ge(block_used, N["wkv"] + c + 1)
                for t in range(NT):
                    b = KV_BANKS[c][2 * t]
                    v = PS[:, b:b + 2, :].rearrange("p b (h e) -> p (b h) e", e=DN + DV)
                    act.activation(k_nat[:, t, 8 * c:8 * c + 8, 0:DN], v[:, :, 0:DN], ACT.Copy).then_inc(M["copied"], 1)
                    act.activation(v_nat[:, t, 8 * c:8 * c + 8, :], v[:, :, DN:DN + DV], ACT.Copy).then_inc(M["copied"], 1)
            act.activation(sqh[:, :, :, :], q_nat[:, :, :, :], ACT.Square).then_inc(M["sqs"], 1)
            act.wait_ge(M["copied"], 11)
            act.wait_ge(M["hred"], 2)
            act.activation(sqh[:, :, :, 0:DN], k_nat[:, :, :, 0:DN], ACT.Square).then_inc(M["sqs"], 1)
            for i in range(MH // 2):
                act.wait_ge(M["qt"], 2 * i + 2)
                act.activation(qT[:, 2 * i:2 * i + 2, :], PS[0:DQ, 6 + i % 2, :].rearrange("p (h n) -> p h n", h=2), ACT.Copy)\
                   .then_inc(M["qtc"], 1)
            for h in range(MH):
                act.wait_ge(M["nm"], h + 1)
                if h >= 2:
                    act.wait_ge(M["pt"], h - 1)
                for t, sl in enumerate((slice(0, P), slice(P, TRI))):
                    act.activation(prob[:, h % 2, sl], sS[:, h % 2, sl], ACT.Exp, scale=DQ ** -0.5,
                                   bias=nmx[:, h % 2, t:t + 1], accum_out=psum_[:, t, h:h + 1]).then_inc(M["e"], 1)
            left_act(act, M, XTh)
            hi_upto(act, at, N["mla_out"] + 5)

        def mla_dve(dve, at, own):
            nq, nk = N["cq"], N["kvr"]
            lo_upto(dve, at, nk + 3)
            dve.wait_ge(M["sq"], 6)
            for k, w in enumerate((QL, KVL, DR)):
                m = dve.tensor_scalar(mvar[:, k, :], mss[:, k, :], 1.0 / w, EPS, ALU.mult, ALU.add)
            m.then_inc(M["var"], 1)
            dve.wait_ge(M["r"], 1)
            for t in range(NT):
                dve.tensor_scalar(cn[:, t, 0:QL], psG[:, t, 0:QL], mrs[:, 0, t:t + 1], None, ALU.mult).then_inc(M["cn"], 1)
                dve.tensor_scalar(cn[:, t, QL:QL + KVL], PS[:, 6 + t, 0:KVL], mrs[:, 1, t:t + 1], None, ALU.mult)\
                   .then_inc(M["cn"], 1)
            for t in range(NT):
                m = dve.scalar_tensor_tensor(out=krot[:, t, :], in0=PS[:, 6 + t, KVL:RW], scalar=mrs[:, 2, t:t + 1],
                                             in1=kn_row[:, DN:DQ], op0=ALU.mult, op1=ALU.mult)
            m.then_inc(M["krr"], 1)
            for c in range(5):
                dve.wait_ge(M["ch"], min(2 * (c // 2) + 2, 5))
                dve.scalar_tensor_tensor(out=cTl[:, c, :], in0=flatD[:, c * SEQ:(c + 1) * SEQ],
                                         scalar=cols[2][:, 64 + c:65 + c], in1=cTh[:, c, :].bitcast(FP32),
                                         op0=ALU.mult, op1=ALU.subtract).then_inc(M["cl"], 1)
            dve.wait_ge(M["krr"], 1)
            dve.wait_ge(M["trig_out"], 1)
            sin, cos = trig[:, 0, :, :], trig[:, 1, :, :]
            k1, k2 = krot[:, :, 0:HR], krot[:, :, HR:DR]
            for j, (a, b) in enumerate(((k1, cos), (k2, sin), (k2, cos), (k1, sin))):
                m = dve.tensor_tensor(ktmp[:, j, :, :], a, b, ALU.mult)
            own.link(m)
            dve.tensor_tensor(k1, ktmp[:, 0, :, :], ktmp[:, 1, :, :], ALU.subtract)
            own.link(dve.tensor_tensor(k2, ktmp[:, 2, :, :], ktmp[:, 3, :, :], ALU.add))
            for t in range(NT):
                dve.tensor_copy(k_nat[:, t, :, DN:DQ], krot[:, t, :].unsqueeze(1).to_broadcast([P, MH, DR]))\
                   .then_inc(M["kb"], 1)
            lo_upto(dve, at, N["wkv"] + 3)
            dve.wait_ge(M["sqs"], 1)
            sv = sqh[:, :, :, :].rearrange("p t h d -> p (t h) d")
            dve.tensor_reduce(out=hss[:, 0, :], in_=sv[:, :, 0:DN], axis=AX.X, op=ALU.add).then_inc(M["hred"], 1)
            dve.tensor_reduce(out=hss[:, 2, :], in_=sv[:, :, DN:DQ], axis=AX.X, op=ALU.add).then_inc(M["hred"], 1)
            dve.wait_ge(M["sqs"], 2)
            own.link(dve.tensor_reduce(out=hss[:, 1, :], in_=sv[:, :, 0:DN], axis=AX.X, op=ALU.add))
            dve.tensor_scalar(hvar[:, 0:2, :], hss[:, 0:2, :], 1.0 / DN, EPS, ALU.mult, ALU.add)
            dve.wait_ge(M["hred"], 2)
            dve.tensor_scalar(hvar[:, 2, :], hss[:, 2, :], 1.0 / DR, EPS, ALU.mult, ALU.add).then_inc(M["var"], 1)
            dve.wait_ge(M["hr"], 1)
            for src, i, row in ((k_nat, 1, kn_row), (q_nat, 0, qn_row)):
                v = src[:, :, :, :].rearrange("p t h d -> p (t h) d")[:, :, 0:DN]
                own.link(dve.tensor_tensor(v, v, hrs[:, i, :].unsqueeze(2).to_broadcast([P, NT * MH, DN]), ALU.mult))
                dve.tensor_tensor(v, v, row[:, 0:DN].unsqueeze(1).to_broadcast([P, NT * MH, DN]), ALU.mult)\
                   .then_inc(M["kb"] if i else M["qs"], 1)
            for i in range(MH // 2):
                dve.wait_ge(M["qt"], 2 * i + 1)
                dve.tensor_copy(kT[:, 2 * i:2 * i + 2, :], PS[0:DQ, 4 + i % 2, :].rearrange("p (h n) -> p h n", h=2))\
                   .then_inc(M["ktc"], 1)
            for h in range(MH + 2):
                if h < MH:
                    dve.wait_ge(M["s"], h + 1)
                    if h >= 2:
                        dve.wait_ge(M["e"], 2 * h - 2)
                    for t, sl in enumerate((slice(0, P), slice(P, TRI))):
                        m = dve.tensor_tensor_reduce(out=sS[:, h % 2, sl], in0=psG[:, h % 2, sl], in1=notyet[:, sl],
                                                     scale=1.0, scalar=-3.0e38, op0=ALU.add, op1=ALU.max,
                                                     accum_out=mx[:, h % 2, t:t + 1])
                    own.link(m)
                    dve.tensor_scalar(nmx[:, h % 2, :], mx[:, h % 2, :], -DQ ** -0.5, None, ALU.mult).then_inc(M["nm"], 1)
                if 1 <= h <= MH:
                    g = h - 1
                    dve.wait_ge(M["pt"], g + 1)
                    if g >= 2:
                        dve.wait_ge(M["o"], g - 1)
                    dve.tensor_copy(probT[:, g % 2, :], PS[:, 6 + g % 2, 0:TRI]).then_inc(M["ptc"], 1)
                if h >= 2 and (h - 2) % 4 == 3:
                    g = (h - 2) // 4
                    hs = slice(4 * g, 4 * g + 4)
                    own.link(dve.reciprocal(rsum[:, :, hs], psum_[:, :, hs]))
                    dve.wait_ge(M["o"], 4 * g + 4)
                    dve.tensor_tensor(xn[:, :, g * 256:(g + 1) * 256].rearrange("p t (h d) -> p t h d", h=4),
                                      psD[:, g % 2, :].rearrange("p (t h d) -> p t h d", t=NT, h=4),
                                      rsum[:, :, hs].unsqueeze(3).to_broadcast([P, NT, 4, DV]), ALU.mult)\
                       .then_inc(M["od"], 1)
            lo_upto(dve, at, N["mla_out"] + 1)
            left_dve(dve, M, XTh, XTl)
            lo_upto(dve, at, N["mla_out"] + 5)
            dve.wait_ge(block_used, N["mla_out"] + 4)
            dve.tensor_tensor(xs_[:, :, :].rearrange("p t n -> p (t n)"), flatD,
                              xs_[:, :, :].rearrange("p t n -> p (t n)"), ALU.add).then_inc(M["x_done"], 1)

        def mla_pool(pool, own):
            pool.wait_ge(M["var"], 1)
            pool.tensor_tensor(mrs[:, :, :], mvar[:, :, :], neghalf[:, 0:1].unsqueeze(2).to_broadcast([P, 3, NT]), ALU.pow)\
                .then_inc(M["r"], 1)
            pool.wait_ge(M["var"], 2)
            pool.tensor_tensor(hrs[:, :, :], hvar[:, :, :],
                               neghalf[:, 0:1].unsqueeze(2).to_broadcast([P, 3, NT * MH]), ALU.pow).then_inc(M["hr"], 1)
            pool.wait_ge(M["hr"], 1)
            pool.wait_ge(M["trig_out"], 1)
            for t in range(NT):
                v = q_nat[:, t, :, DN:DQ]
                own.link(pool.tensor_tensor(v, v, hrs[:, 2, t * MH:(t + 1) * MH].unsqueeze(2).to_broadcast([P, MH, DR]),
                                            ALU.mult))
                own.link(pool.tensor_tensor(v, v, qn_row[:, DN:DQ].unsqueeze(1).to_broadcast([P, MH, DR]), ALU.mult))
                q1, q2 = q_nat[:, t, :, DN:DN + HR], q_nat[:, t, :, DN + HR:DQ]
                sin = trig[:, 0, t, :].unsqueeze(1).to_broadcast([P, MH, HR])
                cos = trig[:, 1, t, :].unsqueeze(1).to_broadcast([P, MH, HR])
                for j, (a, b) in enumerate(((q1, cos), (q2, sin), (q2, cos), (q1, sin))):
                    m = pool.tensor_tensor(rtmp[:, j, :, :], a, b, ALU.mult)
                own.link(m)
                pool.tensor_tensor(q1, rtmp[:, 0, :, :], rtmp[:, 1, :, :], ALU.subtract)
                m = pool.tensor_tensor(q2, rtmp[:, 2, :, :], rtmp[:, 3, :, :], ALU.add)
                if t == 0:
                    own.link(m)
            m.then_inc(M["qr"], 1)

        b2 = ExitStack()
        QK = sb("QK", [P, 2 * KD, SEQ], where=b2)
        V = sb("V", [P, NT, LH * LDV], where=b2)
        Y = sb("Y", [P, NT, DM], where=b2)
        GT = sb("GT", [P, NT, DM], where=b2)
        HTh = sb("HTh", [P, KD, SEQ], FP32R, where=b2)
        HTl = sb("HTl", [P, KD, SEQ], FP32R, where=b2)
        gain_row = sb("gain_row", [P, DM], where=b2)
        lam_row = sb("lam_row", [P, 4, DHD], where=b2)
        sub_row = sb("sub_row", [P, 2 * DHD], where=b2)
        gbias = sb("gbias", [LH, 2], where=b2)
        lcol = sb("lcol", [P, 2, NT, LH], where=b2)
        lsum = sb("lsum", [P, 2], where=b2)
        neglam = sb("neglam", [P, 1], where=b2)
        oss = sb("oss", [P, 16, NT], where=b2)
        ovar = sb("ovar", [P, 16, NT], where=b2)
        ors = sb("ors", [P, 16, NT], where=b2)
        den = sb("den", [P, 3, NT], where=b2)
        dmx = sb("dmx", [P, 2, NT, 2], where=b2)
        dnm = sb("dnm", [P, 2, NT, 2], where=b2)
        dsum = sb("dsum", [P, 2, NT, 2], where=b2)
        with ExitStack() as sub:
            gate_w = sb("gate_w", [P, TRI], where=sub)
            W = sb("W", [P, TRI], where=sub)
            rdec = sb("rdec", [P, LH, TRI], where=sub)
        with ExitStack() as sub:
            dist = sb("dist", [P, TRI], where=sub)
            U = sb("U", [P, 2, 2, TRI], where=sub)
            AW = sb("AW", [P, TRI], where=sub)
            AWT = sb("AWT", [P, TRI], where=sub)
        b2.close()
        grow = Y[0:LH, :, :].rearrange("p t (r n) -> p (t r) n", n=SEQ)
        G_F, G_E, G_LN, G_D, G_Q, G_I, G_B, G_CM = range(8)
        B = sems("b2", "in ifn ift x0 e gr gcolt gcol acc tap silu cp gev vone hs yv fcp s seg w wm W o sq var r h "
                       "lt lh ll dm nm de aw at atc ssq lam dtab rtab zsq zvar zr x_done")

        def chunk(pe, n, pair):
            banks = [psD[:, 2 * pair + t, :] for t in range(NT)]
            mul_rows(pe, n, 0, 0, 4, 512, banks, True, False)
            mul_rows(pe, n + 1, 0, 4, 4, 512, banks, False, True)

        def half_chunk(pe, n0, k, wait):
            pair, h = k // 2, k % 2
            if h == 0:
                pe.wait_ge(*wait(pair))
            mul_rows(pe, n0 + k, 0, 4 * h, 4, 512, [psD[:, 2 * pair + t, :] for t in range(NT)], h == 0, h == 1)

        def scores_T(pe, h):
            for k in range(2):
                pe.matmul(psG[:, 0, 0:SEQ], QK[:, KD + 2 * h + k, 0:P], QK[:, 2 * h + k, :], start=(k == 0), stop=(k == 1))
            for k in range(2):
                m = pe.matmul(psG[:, 0, SEQ:TRI], QK[:, KD + 2 * h + k, P:SEQ], QK[:, 2 * h + k, P:SEQ],
                              start=(k == 0), stop=(k == 1))
            return m

        def values_T(pe, h, width):
            v = V[:, :, h * width:(h + 1) * width]
            pe.matmul(PS[:, 6, 0:width], W[:, 0:P], v[:, 0, :], start=True, stop=True)
            pe.matmul(PS[:, 7, 0:width], W[:, P:2 * P], v[:, 0, :], start=True, stop=False)
            return pe.matmul(PS[:, 7, 0:width], W[:, 2 * P:TRI], v[:, 1, :], start=False, stop=True)

        def b2_pe(pe):
            pe_n = N["if"]
            mul_rows(pe, pe_n, 0, 0, KD, 2 * LH, [psT[:, 0:2 * LH], psS[:, 0:2 * LH]], True, True,
                     ready=lambda k: normed(6, k))
            pe.wait_ge(B["ifn"], 1)
            for k in range(2):
                for t in range(NT):
                    c = k * SEQ + t * P
                    m = pe.transpose(psT[0:LH, c:c + P], ff_a[:, t, k * LH:(k + 1) * LH], ident[:, :])
            m.then_inc(B["ift"], 1)
            for i in range(8):
                if i >= 4:
                    pe.wait_ge(B["tap"], i - 3)
                mul_features(pe, N["mqk"] + i, psD[:, i % 4, :])
                if i == 3:
                    pe.wait_ge(B["gr"], 1)
                    pe.wait_ge(B["e"], 3)
                    for k, r in enumerate((G_D, G_LN)):
                        for t in range(NT):
                            c = (k * NT + t) * LH
                            m = pe.transpose(psS[:, c:c + LH], grow[:, r, t * P:(t + 1) * P], ident[0:LH, 0:LH])
                    m.then_inc(B["gcolt"], 1)
            for c in range(2):
                pe.wait_ge(B["tap"], 6 + 2 * c)
                chunk(pe, N["mv"] + 2 * c, c)
            pe.wait_ge(B["silu"], 8)
            pe.wait_ge(B["gcol"], 1)
            for h in range(LH):
                if h:
                    pe.wait_ge(B["W"], h)
                pe.matmul(psG[:, 1, 0:SEQ], ident[0:LH, h:h + 1].to_broadcast([LH, P]), grow[:, G_CM, :],
                          start=True, stop=True)
                scores_T(pe, h).then_inc(B["s"], 1)
                half_chunk(pe, N["mo"], h, lambda q: (B["cp"], q + 1))
                pe.wait_ge(B["W"], h + 1)
                pe.wait_ge(B["cp"], 2)
                pe.wait_ge(B["vone"], 1)
                if h:
                    pe.wait_ge(B["h"], h)
                values_T(pe, h, LDV).then_inc(B["o"], 1)
            for c in range(2):
                pe.wait_ge(B["gev"], 1 + c)
                chunk(pe, N["gm"] + 2 * c, c)
            left_pe(pe, B, xn, lambda b: (B["hs"], b // 2 + 1))
            pe.wait_ge(B["gev"], 4)
            project_pe(pe, B, N["mlstm_out"], HTh, HTl)

            pe.wait_ge(B["yv"], 1)
            for i in range(8):
                if i >= 4:
                    pe.wait_ge(B["fcp"], i - 3)
                mul_features(pe, N["dqk"] + i, psD[:, i % 4, :])
            for c in range(2):
                pe.wait_ge(B["fcp"], 6 + 2 * c)
                chunk(pe, N["dv"] + 2 * c, c)
            pe.wait_ge(B["fcp"], 8)
            pe.wait_ge(B["cp"], 4)
            for h in range(DH + 2):
                if h < DH:
                    if h:
                        pe.wait_ge(B["dm"], h)
                    for c in range(2):
                        ps = slice(c * DHD, (c + 1) * DHD)
                        pe.matmul(psG[:, c, 0:P], QK[ps, h, 0:P], QK[ps, KD + h, 0:P], start=True, stop=True)
                        m = pe.matmul(psG[:, c, P:TRI], QK[ps, h, P:SEQ], QK[ps, KD + h, :], start=True, stop=True)
                    m.then_inc(B["ssq"], 1)
                    if h % 2 == 0:
                        half_chunk(pe, N["gd"], h // 2, lambda q: (B["cp"], 3 + q))
                if h >= 2:
                    g = h - 2
                    pe.wait_ge(B["atc"], g + 1)
                    if g:
                        pe.wait_ge(B["h"], LH + g)
                    v = V[:, :, g * 2 * DHD:(g + 1) * 2 * DHD]
                    pe.matmul(psS[:, 0:P], AWT[:, 0:P], v[:, 0, :], start=True, stop=True)
                    pe.matmul(psS[:, P:2 * P], AWT[:, P:2 * P], v[:, 0, :], start=True, stop=False)
                    pe.matmul(psS[:, P:2 * P], AWT[:, 2 * P:TRI], v[:, 1, :], start=False, stop=True).then_inc(B["o"], 1)
                if 1 <= h <= DH:
                    pe.wait_ge(B["aw"], h)
                    for c in range(3):
                        m = pe.transpose(psT[:, c * P:(c + 1) * P], AW[:, c * P:(c + 1) * P], ident[:, :])
                    m.then_inc(B["at"], 1)
            left_pe(pe, B, xn, lambda b: (B["h"], LH + 2 * b + 2))
            pe.wait_ge(B["gev"], 6)
            project_pe(pe, B, N["diff_out"], HTh, HTl, 4)

            pe.wait_ge(B["yv"], 2)
            for i in range(8):
                if i >= 4:
                    pe.wait_ge(B["fcp"], 8 + i - 3)
                mul_features(pe, N["rqk"] + i, psD[:, i % 4, :])
            for c in range(2):
                pe.wait_ge(B["fcp"], 14 + 2 * c)
                chunk(pe, N["rv"] + 2 * c, c)
            pe.wait_ge(B["fcp"], 16)
            pe.wait_ge(B["cp"], 6)
            for h in range(LH):
                if h:
                    pe.wait_ge(B["W"], LH + h)
                scores_T(pe, h).then_inc(B["s"], 1)
                half_chunk(pe, N["rg"], h, lambda q: (B["cp"], 5 + q))
                pe.wait_ge(B["W"], LH + h + 1)
                if h:
                    pe.wait_ge(B["h"], LH + DH + h)
                values_T(pe, h, LD).then_inc(B["o"], 1)
            for c in range(2):
                pe.wait_ge(B["gev"], 7 + c)
                chunk(pe, N["gr"] + 2 * c, c)
            left_pe(pe, B, xn, lambda b: (B["hs"], 2 + b // 2 + 1))
            pe.wait_ge(B["gev"], 10)
            project_pe(pe, B, N["ret_out"], HTh, HTl, 8)
            left_pe(pe, B, Y, lambda b: (B["yv"], 3))
            project_pe(pe, B, N["y_out"], HTh, HTl, 12)

        def b2_taps(ct, j):
            return cols[2][:, j * 2 * KD + ct:j * 2 * KD + ct + 1]

        def values_act(act, at, n, first, dst):
            for c in range(2):
                hi_upto(act, at, n + 2 * c + 3)
                act.wait_ge(block_used, n + 2 * c + 2)
                act.activation(dst(c), PS[:, 2 * c:2 * c + 2, :] if dst(c).shape[-1] == 512 else
                               PS[:, 2 * c:2 * c + 2, :].rearrange("p t (h n) -> p t h n", h=2), ACT.Copy)\
                   .then_inc(B["cp"], 1)

        def gate_act(act, at, n, c, func, free):
            hi_upto(act, at, n + 2 * c + 3)
            act.wait_ge(block_used, n + 2 * c + 2)
            if free is not None:
                act.wait_ge(*free)
            act.activation(GT[:, :, c * 512:(c + 1) * 512], PS[:, 2 * c:2 * c + 2, :], func).then_inc(B["gev"], 1)

        def squares_act(act, at, i, width, banks):
            act.wait_ge(B["o"], i + 1)
            for t in range(NT):
                act.activation(ff_s[:, t, 0:width], banks[t], ACT.Square, accum_out=oss[:, i, t:t + 1]).then_inc(B["sq"], 1)

        def features_act(act, at, n):
            for i in range(8):
                hi_upto(act, at, n + i + 2)
                act.wait_ge(block_used, n + i + 1)
                act.activation(QK[:, 2 * i:2 * i + 2, :], PS[:, i % 4, :].rearrange("p (c n) -> p c n", c=2), ACT.Copy)\
                   .then_inc(B["fcp"], 1)

        def b2_act(act, at, own):
            hi_upto(act, at, N["if"] + 2)
            act.wait_ge(block_used, N["if"] + 1)
            act.activation(ff_a[:, :, 0:2 * LH], PS[:, 6:8, 0:2 * LH], ACT.Copy).then_inc(B["ifn"], 1)
            act.wait_ge(B["x0"], 1)
            act.activation(grow[:, G_E, :], grow[:, G_Q, :], ACT.Exp, scale=-1.0).then_inc(B["e"], 1)
            act.wait_ge(B["e"], 1)
            act.activation(grow[:, G_LN, :], grow[:, G_E, :], ACT.Ln, bias=ones[0:LH, 0:1]).then_inc(B["e"], 1)
            act.wait_ge(B["gr"], 1)
            act.activation(grow[:, G_LN, :], grow[:, G_Q, :], ACT.Exp, scale=-1.0).then_inc(B["e"], 1)
            act.wait_ge(B["lam"], 1)
            act.activation(lsum[:, :], lsum[:, :], ACT.Exp).then_inc(B["lam"], 1)
            n = N["mqk"]
            for i in range(9):
                hi_upto(act, at, n + i + 2)
                conv_act(act, B, i, n + i if i < 8 else None, (2 * i, 2 * i + 1), b2_taps, lambda ct: 0.0, None,
                         QK[:, 2 * (i - 1):2 * i, :] if i else None)
            Vh = V[:, :, :].rearrange("p t (h n) -> p t h n", n=LDV)
            values_act(act, at, N["mv"], 0, lambda c: Vh[:, :, 2 * c:2 * c + 2, 0:LD])
            for h in range(LH):
                hi_upto(act, at, N["mo"] + h + 2)
                act.wait_ge(B["seg"], h + 1)
                act.activation(gate_w[:, :], gate_w[:, :], ACT.Exp, scale=-1.0).then_inc(B["w"], 1)
                squares_act(act, at, h, LD, [PS[:, 6, 0:LD], PS[:, 7, 0:LD]])
                if h % 2:
                    gate_act(act, at, N["mo"], h // 2, ACT.Sigmoid, None)
            for c in range(2):
                gate_act(act, at, N["gm"], c, ACT.Sigmoid, (B["hs"], c + 1))
            left_act(act, B, HTh)
            hi_upto(act, at, N["mlstm_out"] + 4)

            features_act(act, at, N["dqk"])
            values_act(act, at, N["dv"], 2, lambda c: V[:, :, c * 512:(c + 1) * 512])
            for h in range(DH + 1):
                hi_upto(act, at, N["gd"] + h // 2 + 2)
                if h < DH:
                    act.wait_ge(B["nm"], h + 1)
                    for t, sl in enumerate((slice(0, P), slice(P, TRI))):
                        for c in range(2):
                            act.activation(U[:, h % 2, c, sl], U[:, h % 2, c, sl], ACT.Exp, scale=DHD ** -0.5,
                                           bias=dnm[:, h % 2, t, c:c + 1],
                                           accum_out=dsum[:, h % 2, t, c:c + 1]).then_inc(B["de"], 1)
                if h >= 1:
                    g = h - 1
                    act.wait_ge(B["at"], g + 1)
                    if g:
                        act.wait_ge(B["o"], LH + g)
                    act.activation(AWT[:, :], psT[:, 0:TRI], ACT.Copy).then_inc(B["atc"], 1)
                if h >= 2:
                    squares_act(act, at, LH + h - 2, P, [psS[:, 0:P], psS[:, P:2 * P]])
            squares_act(act, at, LH + DH - 1, P, [psS[:, 0:P], psS[:, P:2 * P]])
            for c in range(2):
                gate_act(act, at, N["gd"], c, ACT.Sigmoid, (B["yv"], 1))
            left_act(act, B, HTh, 4)
            hi_upto(act, at, N["diff_out"] + 4)

            for h in range(LH):
                act.wait_ge(B["rtab"], 1)
                act.activation(rdec[:, h, :], gate_w[:, :], ACT.Exp,
                               scale=math.log(1.0 - 2.0 ** (-5.0 - h))).then_inc(B["rtab"], 1)
            features_act(act, at, N["rqk"])
            values_act(act, at, N["rv"], 4, lambda c: V[:, :, c * 512:(c + 1) * 512])
            for h in range(LH):
                hi_upto(act, at, N["rg"] + h + 2)
                squares_act(act, at, LH + DH + h, LD, [PS[:, 6, 0:LD], PS[:, 7, 0:LD]])
                if h % 2:
                    gate_act(act, at, N["rg"], h // 2, ACT.Silu, (B["yv"], 2))
            for c in range(2):
                gate_act(act, at, N["gr"], c, ACT.Sigmoid, (B["hs"], 2 + c + 1))
            left_act(act, B, HTh, 8)
            hi_upto(act, at, N["ret_out"] + 4)
            left_act(act, B, HTh, 12)
            hi_upto(act, at, N["y_out"] + 5)
            post_act(act, 0, N["y_out"] + 4)

        def post_act(act, i, used):
            act.wait_ge(block_used, used)
            for t in range(NT):
                act.activation(xn[:, t, :], flatD[:, t * DM:(t + 1) * DM], ACT.Square, accum_out=stat[:, t:t + 1])\
                   .then_inc(B["zsq"], 1)

        def post_dve(dve, own, i, gain_ready):
            dve.wait_ge(B["zsq"], NT * (i + 1))
            dve.tensor_scalar(var[:, :], stat[:, :], 1.0 / DM, EPS, ALU.mult, ALU.add).then_inc(B["zvar"], 1)
            dve.wait_ge(B["zr"], i + 1)
            dve.wait_ge(*gain_ready)
            for t in range(NT):
                own.link(dve.scalar_tensor_tensor(out=xn[:, t, :], in0=flatD[:, t * DM:(t + 1) * DM],
                                                  scalar=rstd[:, t:t + 1], in1=gain_row[:, :],
                                                  op0=ALU.mult, op1=ALU.mult))
            dve.tensor_tensor(xs_[:, :, :], xs_[:, :, :], xn[:, :, :], ALU.add).then_inc(B["x_done"], 1)

        def post_pool(pool, i):
            pool.wait_ge(B["zvar"], i + 1)
            pool.tensor_tensor(rstd[:, :], var[:, :], neghalf[:, 0:NT], ALU.pow).then_inc(B["zr"], 1)

        def head_norm_dve(dve, own, i, width, eps_scale=None):
            dve.wait_ge(B["sq"], NT * (i + 1))
            if eps_scale is None:
                dve.tensor_scalar(ovar[:, i, :], oss[:, i, :], 1.0 / width, EPS, ALU.mult, ALU.add).then_inc(B["var"], 1)
            else:
                own.link(dve.tensor_tensor(ovar[:, i, :], oss[:, i, :], eps_scale, ALU.mult))
                own.link(dve.tensor_tensor(ovar[:, i, :], ovar[:, i, :], eps_scale, ALU.mult))
                dve.tensor_scalar(ovar[:, i, :], ovar[:, i, :], 1.0 / width, EPS, ALU.mult, ALU.add).then_inc(B["var"], 1)
            dve.wait_ge(B["r"], i + 1)

        def gate_out_dve(dve, first):
            for c in range(2):
                dve.wait_ge(B["gev"], first + c)
                dve.tensor_tensor(xn[:, :, c * 512:(c + 1) * 512], xn[:, :, c * 512:(c + 1) * 512],
                                  GT[:, :, c * 512:(c + 1) * 512], ALU.mult).then_inc(B["hs"], 1)

        def b2_dve(dve, at, own):
            lo_upto(dve, at, N["if"] + 2)
            dve.wait_ge(B["in"], 80)
            Vh = V[:, :, :].rearrange("p t (h n) -> p t h n", n=LDV)
            dve.memset(Vh[:, :, :, LD:LDV], 1.0).then_inc(B["vone"], 1)
            for k in range(2):
                m = dve.tensor_tensor(ff_s[:, 0, k * DHD:(k + 1) * DHD], lam_row[:, 2 * k, :], lam_row[:, 2 * k + 1, :],
                                      ALU.mult)
            own.link(m)
            dve.tensor_reduce(out=lsum[:, :], in_=ff_s[:, 0, 0:2 * DHD].rearrange("p (k n) -> p k n", k=2), axis=AX.X,
                              op=ALU.add).then_inc(B["lam"], 1)
            own.link(dve.tensor_scalar(sub_row[:, :], sub_row[:, :], 1.0 - LAM_INIT, None, ALU.mult))
            dve.wait_ge(B["ift"], 1)
            dve.tensor_scalar(grow[:, G_I, :], psT[0:LH, 0:SEQ], gbias[:, 0:1], None, ALU.add)
            own.link(dve.tensor_scalar(grow[:, G_F, :], psT[0:LH, SEQ:2 * SEQ], gbias[:, 1:2], None, ALU.add))
            dve.scalar_tensor_tensor(out=grow[:, G_Q, :], in0=grow[:, G_F, :], scalar=-1.0, in1=grow[:, G_F, :],
                                     op0=ALU.mult, op1=ALU.max).then_inc(B["x0"], 1)
            dve.wait_ge(B["e"], 2)
            own.link(dve.tensor_scalar(grow[:, G_D, :], grow[:, G_E, :], 1.0, -1.0, ALU.add, ALU.add))
            own.link(dve.tensor_scalar(grow[:, G_Q, :], grow[:, G_D, :], 1e-30, None, ALU.max))
            own.link(dve.reciprocal(grow[:, G_Q, :], grow[:, G_Q, :]))
            own.link(dve.tensor_tensor(grow[:, G_Q, :], grow[:, G_Q, :], grow[:, G_E, :], ALU.mult))
            own.link(dve.tensor_tensor(grow[:, G_Q, :], grow[:, G_Q, :], grow[:, G_LN, :], ALU.mult))
            own.link(dve.scalar_tensor_tensor(out=grow[:, G_D, :], in0=grow[:, G_D, :], scalar=0.0,
                                              in1=grow[:, G_E, :], op0=ALU.is_equal, op1=ALU.mult))
            own.link(dve.tensor_tensor(grow[:, G_Q, :], grow[:, G_Q, :], grow[:, G_D, :], ALU.add))
            own.link(dve.scalar_tensor_tensor(out=grow[:, G_F, :], in0=grow[:, G_F, :], scalar=0.0,
                                              in1=grow[:, G_Q, :], op0=ALU.min, op1=ALU.subtract))
            own.link(dve.tensor_tensor_scan(out=grow[:, G_B, :], data0=ones[0:LH, :], data1=grow[:, G_F, :],
                                            initial=0.0, op0=ALU.mult, op1=ALU.add))
            own.link(dve.tensor_tensor(grow[:, G_D, :], grow[:, G_I, :], grow[:, G_B, :], ALU.subtract))
            own.link(dve.tensor_tensor_scan(out=grow[:, G_CM, :], data0=grow[:, G_D, :], data1=grow[:, G_D, :],
                                            initial=0.0, op0=ALU.max, op1=ALU.max))
            dve.tensor_tensor(grow[:, G_Q, :], grow[:, G_B, :], grow[:, G_CM, :], ALU.add).then_inc(B["gr"], 1)
            for i in range(8):
                lo_upto(dve, at, N["mqk"] + i + 2)
                conv_dve(dve, own, B, i, (2 * i, 2 * i + 1), b2_taps)
                if i == 3:
                    dve.wait_ge(B["gcolt"], 1)
                    dve.tensor_copy(lcol[:, :, :, :].rearrange("p k t h -> p (k t h)"), psS[:, 0:4 * LH])\
                       .then_inc(B["gcol"], 1)
            lo_upto(dve, at, N["mv"] + 5)
            dve.wait_ge(B["gcol"], 1)
            for h in range(LH):
                lo_upto(dve, at, N["mo"] + h + 1)
                dve.wait_ge(B["s"], h + 1)
                if h:
                    dve.wait_ge(B["W"], h)
                for t, (sl, c0) in enumerate(((slice(0, SEQ), 0), (slice(SEQ, TRI), P))):
                    m = dve.tensor_scalar(gate_w[:, sl], psG[:, 1, c0:SEQ], lcol[:, 0, t, h:h + 1], 0.0,
                                          ALU.subtract, ALU.max)
                m.then_inc(B["seg"], 1)
                lo_upto(dve, at, N["mo"] + h + 2)
                dve.wait_ge(B["wm"], h + 1)
                if h:
                    dve.wait_ge(B["o"], h)
                dve.scalar_tensor_tensor(out=W[:, :], in0=psG[:, 0, 0:TRI], scalar=LD ** -0.5, in1=gate_w[:, :],
                                         op0=ALU.mult, op1=ALU.mult).then_inc(B["W"], 1)
                dve.wait_ge(B["sq"], NT * (h + 1))
                own.link(dve.tensor_copy(den[:, 0, :], PS[:, 6:8, LD]))
                own.link(dve.scalar_tensor_tensor(out=den[:, 1, :], in0=den[:, 0, :], scalar=-1.0, in1=den[:, 0, :],
                                                  op0=ALU.mult, op1=ALU.max))
                own.link(dve.tensor_tensor(den[:, 1, :], den[:, 1, :], lcol[:, 1, :, h], ALU.max))
                own.link(dve.reciprocal(den[:, 2, :], den[:, 1, :]))
                head_norm_dve(dve, own, h, LD, den[:, 2, :])
                own.link(dve.tensor_tensor(den[:, 2, :], den[:, 2, :], ors[:, h, :], ALU.mult))
                for t in range(NT):
                    m = dve.tensor_scalar(xn[:, t, h * LD:(h + 1) * LD], PS[:, 6 + t, 0:LD], den[:, 2, t:t + 1], None,
                                          ALU.mult)
                m.then_inc(B["h"], 1)
            dve.wait_ge(B["h"], LH)
            gate_out_dve(dve, 1)
            lo_upto(dve, at, N["mlstm_out"] + 1)
            left_dve(dve, B, HTh, HTl)
            lo_upto(dve, at, N["mlstm_out"] + 4)
            dve.wait_ge(block_used, N["mlstm_out"] + 4)
            dve.wait_ge(B["gev"], 4)
            dve.tensor_tensor(Y[:, :, :].rearrange("p t n -> p (t n)"), flatD, GT[:, :, :].rearrange("p t n -> p (t n)"),
                              ALU.mult).then_inc(B["yv"], 1)

            dve.wait_ge(B["dtab"], 2)
            own.link(dve.scalar_tensor_tensor(out=dist[:, :], in0=dist[:, :], scalar=-1.0, in1=dist[:, :],
                                              op0=ALU.mult, op1=ALU.max))
            dve.memset(dist[0:64, 64:P], BIG)
            own.link(dve.memset(dist[0:64, P + 192:TRI], BIG))
            dve.wait_ge(B["lam"], 2)
            own.link(dve.tensor_tensor(neglam[:, :], lsum[:, 1:2], lsum[:, 0:1], ALU.subtract))
            own.link(dve.tensor_scalar(neglam[:, :], neglam[:, :], -LAM_INIT, None, ALU.add))
            lo_upto(dve, at, N["dv"] + 5)
            for h in range(DH + 3):
                lo_upto(dve, at, N["gd"] + min(h // 2, 3) + 2)
                if h < DH:
                    slope = 2.0 ** (-8.0 * (h + 1.0) / DH)
                    dve.wait_ge(B["ssq"], h + 1)
                    if h >= 2:
                        dve.wait_ge(B["aw"], h - 1)
                    own.mark(dve.scalar_tensor_tensor(out=U[:, h % 2, :, :],
                                                      in0=dist[:, :].unsqueeze(1).to_broadcast([P, 2, TRI]),
                                                      scalar=-slope * DHD ** 0.5, in1=psG[:, :, 0:TRI],
                                                      op0=ALU.mult, op1=ALU.add))
                    own.wait()
                    dve.tensor_reduce(out=dmx[:, h % 2, 0, :], in_=U[:, h % 2, :, 0:P], axis=AX.X, op=ALU.max)\
                       .then_inc(B["dm"], 1)
                    own.link(dve.tensor_reduce(out=dmx[:, h % 2, 1, :], in_=U[:, h % 2, :, P:TRI], axis=AX.X, op=ALU.max))
                    dve.wait_ge(B["dm"], h + 1)
                    dve.tensor_scalar(dnm[:, h % 2, :, :], dmx[:, h % 2, :, :], -DHD ** -0.5, None, ALU.mult)\
                       .then_inc(B["nm"], 1)
                if 1 <= h <= DH:
                    g, u = h - 1, (h - 1) % 2
                    dve.wait_ge(B["de"], 4 * g + 4)
                    own.link(dve.reciprocal(dsum[:, u, :, :], dsum[:, u, :, :]))
                    own.link(dve.tensor_scalar(dsum[:, u, :, 1], dsum[:, u, :, 1], neglam[:, 0:1], None, ALU.mult))
                    if g:
                        dve.wait_ge(B["at"], g)
                    for t, sl in enumerate((slice(0, P), slice(P, TRI))):
                        m = dve.tensor_scalar(AW[:, sl], U[:, u, 0, sl], dsum[:, u, t, 0:1], None, ALU.mult)
                    own.link(m)
                    for t, sl in enumerate((slice(0, P), slice(P, TRI))):
                        m = dve.scalar_tensor_tensor(out=AW[:, sl], in0=U[:, u, 1, sl], scalar=dsum[:, u, t, 1:2],
                                                     in1=AW[:, sl], op0=ALU.mult, op1=ALU.add)
                    m.then_inc(B["aw"], 1)
                if h >= 3:
                    g = h - 3
                    head_norm_dve(dve, own, LH + g, P)
                    for t in range(NT):
                        m = dve.scalar_tensor_tensor(out=xn[:, t, g * P:(g + 1) * P], in0=psS[:, t * P:(t + 1) * P],
                                                     scalar=ors[:, LH + g, t:t + 1], in1=sub_row[:, :],
                                                     op0=ALU.mult, op1=ALU.mult)
                    m.then_inc(B["h"], 1)
            lo_upto(dve, at, N["diff_out"] + 1)
            left_dve(dve, B, HTh, HTl, 4)
            lo_upto(dve, at, N["diff_out"] + 4)
            add_gated(dve, own, N["diff_out"] + 4, 6)

            lo_upto(dve, at, N["rv"] + 1)
            dve.wait_ge(B["rtab"], LH + 1)
            own.link(dve.scalar_tensor_tensor(out=rdec[:, :, :], in0=rdec[:, :, :], scalar=LD ** -0.5,
                                              in1=causal[:, :].unsqueeze(1).to_broadcast([P, LH, TRI]),
                                              op0=ALU.mult, op1=ALU.mult))
            lo_upto(dve, at, N["rv"] + 5)
            for h in range(LH):
                lo_upto(dve, at, N["rg"] + h + 2)
                dve.wait_ge(B["s"], LH + h + 1)
                if h:
                    dve.wait_ge(B["o"], LH + DH + h)
                dve.tensor_tensor(W[:, :], psG[:, 0, 0:TRI], rdec[:, h, :], ALU.mult).then_inc(B["W"], 1)
                head_norm_dve(dve, own, LH + DH + h, LD)
                for t in range(NT):
                    m = dve.tensor_scalar(xn[:, t, h * LD:(h + 1) * LD], PS[:, 6 + t, 0:LD],
                                          ors[:, LH + DH + h, t:t + 1], None, ALU.mult)
                m.then_inc(B["h"], 1)
            dve.wait_ge(B["h"], 2 * LH + DH)
            gate_out_dve(dve, 7)
            lo_upto(dve, at, N["ret_out"] + 1)
            left_dve(dve, B, HTh, HTl, 8)
            lo_upto(dve, at, N["ret_out"] + 4)
            add_gated(dve, own, N["ret_out"] + 4, 10)
            left_dve(dve, B, HTh, HTl, 12)
            lo_upto(dve, at, N["y_out"] + 5)
            post_dve(dve, own, 0, (B["in"], 80))

        def add_gated(dve, own, used, gev):
            dve.wait_ge(block_used, used)
            dve.wait_ge(B["gev"], gev)
            own.link(dve.tensor_tensor(GT[:, :, :].rearrange("p t n -> p (t n)"), flatD,
                                       GT[:, :, :].rearrange("p t n -> p (t n)"), ALU.mult))
            dve.tensor_tensor(Y[:, :, :], Y[:, :, :], GT[:, :, :], ALU.add).then_inc(B["yv"], 1)

        def b2_pool(pool, own):
            for h in range(LH):
                pool.wait_ge(B["w"], h + 1)
                pool.tensor_tensor(gate_w[:, :], gate_w[:, :], causal[:, :], ALU.mult).then_inc(B["wm"], 1)
                pool.wait_ge(B["var"], h + 1)
                pool.tensor_tensor(ors[:, h, :], ovar[:, h, :], neghalf[:, 0:NT], ALU.pow).then_inc(B["r"], 1)
            pool.wait_ge(B["o"], LH)
            pool.iota(dist[:, 0:P], [[-1, P]], base=0, channel_multiplier=1, allow_small_or_imprecise_dtypes=True)\
                .then_inc(B["dtab"], 1)
            pool.iota(dist[:, P:TRI], [[-1, SEQ]], base=P, channel_multiplier=1, allow_small_or_imprecise_dtypes=True)\
                .then_inc(B["dtab"], 1)
            for g in range(DH):
                i = LH + g
                pool.wait_ge(B["var"], i + 1)
                pool.tensor_tensor(ors[:, i, :], ovar[:, i, :], neghalf[:, 0:NT], ALU.pow).then_inc(B["r"], 1)
            pool.wait_ge(B["h"], LH + DH)
            own.mark(pool.iota(gate_w[:, 0:SEQ], [[1, SEQ]], base=0, channel_multiplier=-1,
                               allow_small_or_imprecise_dtypes=True))
            own.link(pool.iota(gate_w[:, SEQ:TRI], [[1, P]], base=0, channel_multiplier=-1,
                               allow_small_or_imprecise_dtypes=True))
            pool.tensor_scalar(gate_w[:, :], gate_w[:, :], 0.0, None, ALU.max).then_inc(B["rtab"], 1)
            for h in range(LH):
                i = LH + DH + h
                pool.wait_ge(B["var"], i + 1)
                pool.tensor_tensor(ors[:, i, :], ovar[:, i, :], neghalf[:, 0:NT], ALU.pow).then_inc(B["r"], 1)
            post_pool(pool, 0)

        block = ctx.enter_context(nc.Block())

        @block.sync
        def _(sp):
            sp.dma_start(xs_[:, :, :], x[0].rearrange("(t p) n -> p t n", p=P)).then_inc(s_x, 16)
            for src, r, at in NROW:
                sp.dma_start(rows[r][at:at + src.shape[0], :], src).then_inc(s_rows, 16)

            def stream(lo, hi):
                for n in range(lo, hi):
                    load_block(sp, blocks[n], n)

            def ffn_stream(i):
                wg, wu, wd = FFN_W[i]
                n0, cu = N[f"ffn{i}"], (FF if i == 4 else 0)

                def gate_up(j, ahead, h):
                    return pair_block(wg, wu, h * 4, 4, j * FCH + ahead * FCH, j * FCH + (cu + ahead * FCH), FCH)

                stream(n0 + 2, n0 + 3)
                with sp.Fori(0, NFF - 2) as j:
                    load_block(sp, gate_up(j, 1, 1), n0 + 3, j)
                    load_block(sp, down_block(wd, j), n0 + 4, j)
                    load_block(sp, gate_up(j, 2, 0), n0 + 5, j)
                stream(n0 + 3 * NFF - 3, n0 + 3 * NFF)

            sp.dma_start(dtb[:, :], ssm_dt_bias.rearrange("i h -> h i")).then_inc(A["in"], 16)
            sp.dma_start(alog[:, :], ssm_a_log.rearrange("i h -> h i")).then_inc(A["in"], 16)
            sp.dma_start(dskip[:, :], ssm_d[0:1, :].to_broadcast([P, SSM_HEADS])).then_inc(A["in"], 16)
            sp.dma_start(posi[:, :], positions.rearrange("b (t p) -> p (b t)", p=P)).then_inc(M["in"], 16)
            sp.dma_start(qn_row[:, :], mla_q_norm[0:1, :].to_broadcast([P, DQ])).then_inc(M["in"], 16)
            sp.dma_start(kn_row[:, :], mla_k_norm[0:1, :].to_broadcast([P, DQ])).then_inc(M["in"], 16)
            stream(0, 2)
            ffn_stream(0)
            stream(N["dt"], N["ssm_out"] + 8)
            stream(N["ffn1"], N["ffn1"] + 2)
            ffn_stream(1)
            stream(N["ffn2"], N["ffn2"] + 2)
            ffn_stream(2)
            stream(N["cq"], N["mla_out"] + 4)
            stream(N["ffn3"], N["ffn3"] + 2)
            ffn_stream(3)
            sp.wait_ge(M["x_done"], 1)
            for dst, src in ((gain_row[:, :], norm_gains_2[0, 1:2, :].to_broadcast([P, DM])),
                             (lam_row[:, :, :].rearrange("p k n -> p (k n)"),
                              diff_lambda_2.rearrange("i k n -> i (k n)").to_broadcast([P, 4 * DHD])),
                             (sub_row[:, :], diff_subln_2[0:1, :].to_broadcast([P, 2 * DHD])),
                             (gbias[:, 0:1], mlstm_gate_bias_2[0, 0:1, :].rearrange("k h -> h k")),
                             (gbias[:, 1:2], mlstm_gate_bias_2[0, 1:2, :].rearrange("k h -> h k"))):
                sp.dma_start(dst, src).then_inc(B["in"], 16)
            stream(N["if"], N["ffn4"] + 2)
            sp.wait_ge(B["x_done"], 1)
            sp.dma_start(gain_row[:, :], norm_gains_2[0, 3:4, :].to_broadcast([P, DM])).then_inc(B["in"], 16)
            ffn_stream(4)
            sp.wait_ge(B["x_done"], 2)
            sp.dma_start(out[0].rearrange("(t p) n -> p t n", p=P), xs_[:, :, :]).then_inc(s_out, 16)
            sp.wait_ge(s_out, 16)

        @block.gpsimd
        def _(pool):
            own = Chain(pool, pool_own)
            own.mark(pool.memset(ident[:, :], 0.0))
            own.mark(pool.memset(causal[:, :], 1.0))
            pool.memset(neghalf[:, :], -0.5)
            pool.memset(ones[:, :], 1.0).then_inc(s_const, 1)
            own.wait()
            pool.affine_select(out=ident[:, :], in_=ident[:, :], compare_op=ALU.not_equal, fill=1.0,
                               base=0, pattern=[[-1, P]], channel_multiplier=1).then_inc(s_const, 1)
            for c in (0, 2 * P):
                pool.affine_select(out=causal[:, c:c + P], in_=causal[:, c:c + P], compare_op=ALU.is_ge,
                                   fill=0.0, base=0, pattern=[[1, P]], channel_multiplier=-1).then_inc(s_const, 1)
            mla_tables_pool(pool, own)
            norm_pool(pool, 0)
            norm_pool(pool, 1)
            ssm_pool(pool)
            norm_pool(pool, 2)
            norm_pool(pool, 3)
            norm_pool(pool, 4)
            mla_pool(pool, own)
            norm_pool(pool, 5)
            norm_pool(pool, 6)
            b2_pool(pool, own)
            norm_pool(pool, 7)
            post_pool(pool, 1)

        @block.scalar
        def _(act):
            at, own = Position(), Chain(act, act_own)
            for i in range(3):
                act.wait_ge(s_rowt, i + 1)
                act.activation(cols[i][:, 0:ROWS_IN[i]], PS[:, 4 + i, 0:ROWS_IN[i]], ACT.Copy).then_inc(s_rowc, 1)
            hi_upto(act, at, 1)
            act.wait_ge(s_rowc, 3)
            act.wait_ge(s_const, 4)
            mla_tables_act(act)
            norm_act(act, 0, (s_x, 16), 0)
            ffn_act(act, 0, at)
            norm_act(act, 1, (F["x_done"], 1), 8)
            ssm_act(act, at, own)
            norm_act(act, 2, (A["x_done"], 1), 16)
            ffn_act(act, 1, at)
            norm_act(act, 3, (F["x_done"], 2), 24)
            ffn_act(act, 2, at)
            norm_act(act, 4, (F["x_done"], 3), 32)
            mla_act(act, at, own)
            norm_act(act, 5, (M["x_done"], 1), 40)
            ffn_act(act, 3, at)
            norm_act(act, 6, (F["x_done"], 4), 48)
            b2_act(act, at, own)
            norm_act(act, 7, (B["x_done"], 1), 64)
            ffn_act(act, 4, at)
            post_act(act, 1, NB)

        @block.vector
        def _(dve):
            at, own = Position(), Chain(dve, dve_own)
            mla_tables_dve(dve, own)
            lo_upto(dve, at, 1)
            dve.wait_ge(s_rowc, 3)
            dve.wait_ge(s_const, 4)
            norm_dve(dve, 0, 0)
            ffn_dve(dve, 0, at, own)
            norm_dve(dve, 1, 8)
            ssm_dve(dve, at, own)
            norm_dve(dve, 2, 16)
            ffn_dve(dve, 1, at, own)
            norm_dve(dve, 3, 24)
            ffn_dve(dve, 2, at, own)
            norm_dve(dve, 4, 32)
            mla_dve(dve, at, own)
            norm_dve(dve, 5, 40)
            ffn_dve(dve, 3, at, own)
            norm_dve(dve, 6, 48)
            b2_dve(dve, at, own)
            norm_dve(dve, 7, 64)
            ffn_dve(dve, 4, at, own)
            post_dve(dve, own, 1, (B["in"], 96))

        @block.tensor
        def _(pe):
            own = Chain(pe, pe_own)
            pe.wait_ge(s_const, 4)
            pe.wait_ge(s_rows, 16 * len(NROW))
            for i in range(3):
                pe.transpose(PS[:, 4 + i, 0:ROWS_IN[i]], rows[i][0:ROWS_IN[i], :], ident[0:ROWS_IN[i], 0:ROWS_IN[i]])\
                  .then_inc(s_rowt, 1)
            norm_pe(pe, 0)
            pe.wait_ge(s_rowc, 3)
            ffn_pe(pe, 0, 0)
            norm_pe(pe, 1)
            ssm_pe(pe)
            norm_pe(pe, 2)
            ffn_pe(pe, 1, 2)
            norm_pe(pe, 3)
            ffn_pe(pe, 2, 3)
            norm_pe(pe, 4)
            mla_pe(pe)
            norm_pe(pe, 5)
            ffn_pe(pe, 3, 5)
            norm_pe(pe, 6)
            b2_pe(pe)
            norm_pe(pe, 7)
            ffn_pe(pe, 4, 7)


_INS = ['x', 'positions', 'norm_w', 'ffn_w_gate', 'ffn_w_up', 'ffn_w_down', 'ssm_w_in', 'ssm_conv_w',
        'ssm_conv_b', 'ssm_dt_bias', 'ssm_a_log', 'ssm_d', 'ssm_norm_w', 'ssm_w_out', 'mla_w_in',
        'mla_q_a_norm', 'mla_kv_a_norm', 'mla_w_q_b', 'mla_w_kv_b', 'mla_q_norm', 'mla_k_norm', 'mla_w_out',
        'norm_gains_2', 'w_in_2', 'mlstm_conv_2', 'mlstm_gate_bias_2', 'diff_lambda_2', 'diff_subln_2',
        'w_mlstm_out_2', 'w_diff_out_2', 'w_ret_out_2', 'w_out_2', 'w_ffn_in_2', 'w_ffn_out_2']


def kernel(**inputs):
    import concourse.bacc as bacc
    from concourse.bass_utils import run_bass_kernel_spmd

    nc = bacc.Bacc("TRN2", target_bir_lowering=False, num_devices=1)
    arrays, args = {}, []
    for name in _INS:
        a = np.ascontiguousarray(inputs[name])
        arrays[f"in_{name}"] = a
        args.append(nc.dram_tensor(f"in_{name}", a.shape, mybir.dt.from_np(a.dtype), kind="ExternalInput").ap())
    args.append(nc.dram_tensor("out_x", (1, SEQ, DM), FP32, kind="ExternalOutput").ap())
    build(nc, *args)
    return run_bass_kernel_spmd(nc, [arrays], core_ids=[0]).results[0]["out_x"]
```

```python
import math
from contextlib import ExitStack

import numpy as np

import concourse.bass as bass
from concourse import mybir

FP32 = mybir.dt.float32
FP32R = mybir.dt.float32r
I32 = mybir.dt.int32
ALU = mybir.AluOpType
ACT = mybir.ActivationFunctionType
AX = mybir.AxisListType

P = 128
SEQ = 256
NT = SEQ // P
DM = 1024
KD = DM // P
EPS = 1e-6
FF = 2816
FCH = 256
NFF = FF // FCH
SLOTS = 3
BLK = 2048
BIG = 1e30

D_INNER, SSM_HEADS, SSM_P, SSM_N, SSM_G = 2048, 32, 64, 128, 8
SSM_R = SSM_HEADS // SSM_G
XBC = D_INNER + 2 * SSM_G * SSM_N
CONV_K = 4

MH, QL, KVL, DN, DR, DV = 16, 384, 256, 64, 32, 64
DQ = DN + DR
HR = DR // 2
ROPE_THETA = 10000.0
TWO_PI = (6.28125, 0.0019350051879882812, 3.0199159819567e-07)
ROUND = 12582912.0

LH, LD = 4, 256
LDV = LD + 1
DH, DHD = 8, 64
C_MQ, C_MV, C_MO, C_MI = 0, 2 * DM, 3 * DM, 4 * DM
C_DQ = 4104
C_DV = C_DQ + 2 * DM
C_RQ = C_DQ + 3 * DM
C_RV, C_RG = C_RQ + 2 * DM, C_RQ + 3 * DM
C_G = C_RQ + 4 * DM
LAM_INIT = 0.8 - 0.6 * math.exp(-0.3 * 0)
TRI = 3 * P


class Block:

    def __init__(self, size, loads):
        self.size, self.loads = size, loads


def rows_block(w, k0, nk, c0, nc):
    v = w.rearrange("(c p) n -> p c n", p=P)
    a, columns = nk // 2, slice(c0, c0 + nc) if isinstance(c0, int) else bass.ds(c0, nc)
    return Block(nk * nc, [(lambda t, lo=lo, hi=hi: t[:, lo * nc:hi * nc].rearrange("p (k n) -> p k n", n=nc),
                            v[:, k0 + lo:k0 + hi, columns]) for lo, hi in ((0, a), (a, nk))])


class Position:

    def __init__(self):
        self.n = 0


class Chain:

    def __init__(self, eng, sem):
        self.eng, self.sem, self.n = eng, sem, 0

    def mark(self, ins):
        ins.then_inc(self.sem, 1)
        self.n += 1

    def wait(self):
        self.eng.wait_ge(self.sem, self.n)

    def link(self, ins):
        self.mark(ins)
        self.wait()


def build(nc, x, positions, norm_w, ffn_w_gate, ffn_w_up, ffn_w_down, ssm_w_in, ssm_conv_w,
          ssm_conv_b, ssm_dt_bias, ssm_a_log, ssm_d, ssm_norm_w, ssm_w_out, mla_w_in, mla_q_a_norm,
          mla_kv_a_norm, mla_w_q_b, mla_w_kv_b, mla_q_norm, mla_k_norm, mla_w_out, norm_gains_2,
          w_in_2, mlstm_conv_2, mlstm_gate_bias_2, diff_lambda_2, diff_subln_2, w_mlstm_out_2,
          w_diff_out_2, w_ret_out_2, w_out_2, w_ffn_in_2, w_ffn_out_2, out):
    ctx = ExitStack()
    with ctx:
        ctx.enter_context(nc.allow_non_contiguous_dma(reason="small tables and narrow columns"))

        def sb(name, shape, dt=FP32, where=ctx):
            return where.enter_context(nc.sbuf_tensor(name, shape, dt))

        def sem(name):
            return ctx.enter_context(nc.semaphore(name))

        def sems(prefix, names):
            return {n: sem(f"{prefix}_{n}") for n in names.split()}

        blocks = []
        in2 = w_in_2[0]

        def ffn_blocks(wg, wu, cu, wd):
            n0 = len(blocks)
            def gate_up(j):
                return [rows_block(wg, 0, KD, j * FCH, FCH), rows_block(wu, 0, KD, cu + j * FCH, FCH)]
            def down(j):
                return rows_block(wd, 2 * j, 2, 0, DM)
            blocks.extend(gate_up(0))
            for j in range(1, NFF):
                blocks.extend(gate_up(j) + [down(j - 1)])
            blocks.append(down(NFF - 1))
            return n0

        def down_block(wd, j):
            v = wd.rearrange("(c p) n -> p c n", p=P)
            return Block(BLK, [(lambda t, h=h: t[:, h * DM:(h + 1) * DM].rearrange("p (k n) -> p k n", k=1),
                                v[:, bass.ds(2 * j + h, 1), :]) for h in range(2)])

        def natural_blocks(w, c0, chunks, width=512):
            n0 = len(blocks)
            for c in range(chunks):
                for h in range(2):
                    blocks.append(rows_block(w, 4 * h, 4, c0 + c * width, width))
            return n0

        def feature_blocks(w, c0, pairs):
            n0 = len(blocks)
            for c in range(pairs):
                blocks.append(rows_block(w, 0, KD, c0 + c * 2 * P, 2 * P))
            return n0

        def out_blocks(w, ks):
            n0 = len(blocks)
            for c in range(ks // 2):
                blocks.append(rows_block(w, 2 * c, 2, 0, DM))
            return n0

        FFN_W = [(ffn_w_gate[0, 0], ffn_w_up[0, 0], ffn_w_down[0, 0]),
                 (ffn_w_gate[0, 1], ffn_w_up[0, 1], ffn_w_down[0, 1]),
                 (ffn_w_gate[1, 0], ffn_w_up[1, 0], ffn_w_down[1, 0]),
                 (ffn_w_gate[1, 1], ffn_w_up[1, 1], ffn_w_down[1, 1]),
                 (w_ffn_in_2[0], w_ffn_in_2[0], w_ffn_out_2[0])]
        N = {}
        def ffn_add(i):
            wg, wu, wd = FFN_W[i]
            N[f"ffn{i}"] = ffn_blocks(wg, wu, FF if i == 4 else 0, wd)
        ffn_add(0)
        win = ssm_w_in[0]
        N["bc0"] = feature_blocks(win, 2 * D_INNER, 1)
        N["dt"] = len(blocks)
        blocks.append(rows_block(win, 0, KD, D_INNER + XBC, SSM_HEADS))
        N["bc"] = feature_blocks(win, 2 * D_INNER + 2 * P, 7) - 1
        N["xs"] = feature_blocks(win, D_INNER, 8)
        N["z"] = natural_blocks(win, 0, 4)
        N["ssm_out"] = out_blocks(ssm_w_out[0], D_INNER // P)
        ffn_add(1)
        ffn_add(2)
        mw = mla_w_in[0]
        N["cq"] = natural_blocks(mw, 0, 1, QL)
        N["kvr"] = natural_blocks(mw, QL, 1, KVL + DR)
        N["wq"] = len(blocks)
        for c in range(3):
            blocks.append(rows_block(mla_w_q_b[0], 0, 3, c * 512, 512))
        N["wkv"] = len(blocks)
        for c in range(2):
            blocks.append(rows_block(mla_w_kv_b[0], 0, 2, c * 1024, 1024))
        N["mla_out"] = out_blocks(mla_w_out[0], KD)
        ffn_add(3)
        N["mqk0"] = feature_blocks(in2, C_MQ, 1)
        N["if"] = len(blocks)
        blocks.append(rows_block(in2, 0, KD, C_MI, 2 * LH))
        N["mqk"] = feature_blocks(in2, C_MQ + 2 * P, 7) - 1
        N["mv"] = natural_blocks(in2, C_MV, 2)
        N["mo"] = natural_blocks(in2, C_MO, 2)
        N["gm"] = natural_blocks(in2, C_G, 2)
        N["mlstm_out"] = out_blocks(w_mlstm_out_2[0], KD)
        N["dqk"] = feature_blocks(in2, C_DQ, 8)
        N["dv"] = natural_blocks(in2, C_DV, 2)
        N["gd"] = natural_blocks(in2, C_G + DM, 2)
        N["diff_out"] = out_blocks(w_diff_out_2[0], KD)
        N["rqk"] = feature_blocks(in2, C_RQ, 8)
        N["rv"] = natural_blocks(in2, C_RV, 2)
        N["rg"] = natural_blocks(in2, C_RG, 2)
        N["gr"] = natural_blocks(in2, C_G + 2 * DM, 2)
        N["ret_out"] = out_blocks(w_ret_out_2[0], KD)
        N["y_out"] = out_blocks(w_out_2[0], KD)
        ffn_add(4)
        NB = len(blocks)

        raw = [sb(f"raw{s}", [P, BLK]) for s in range(SLOTS)]
        whi = [sb(f"whi{s}", [P, BLK], FP32R) for s in range(SLOTS)]
        wlo = [sb(f"wlo{s}", [P, BLK], FP32R) for s in range(SLOTS)]
        raw_loaded = [sem(f"raw_loaded{s}") for s in range(SLOTS)]
        hi_done, lo_done, block_used = sem("hi_done"), sem("lo_done"), sem("block_used")

        xs_ = sb("x_sb", [P, NT, DM])
        xn = sb("xn", [P, NT, DM])
        XTh = sb("XTh", [P, KD, SEQ], FP32R)
        XTl = sb("XTl", [P, KD, SEQ], FP32R)
        ident = sb("ident", [P, P])
        causal = sb("causal", [P, TRI])
        ident_r = sb("ident_r", [P, P], FP32R)
        neghalf = sb("neghalf", [P, 16])
        ones = sb("ones", [P, SEQ])
        rows = [sb(f"rows{i}", [P, P]) for i in range(3)]
        cols = [sb(f"cols{i}", [P, P]) for i in range(3)]
        x_in = [sem(f"x_in{t}") for t in range(NT)]
        s_rows, s_rowt, s_rowc, s_const, s_out = (
            sem(n) for n in "rows_in rows_turned cols_done consts gout".split())
        NROW = [(norm_w.rearrange("i m (c p) -> (i m c) p", p=P), 0, 0),
                (norm_gains_2.rearrange("i m (c p) -> (i m c) p", p=P), 0, 48),
                (ssm_conv_b.rearrange("i (c p) -> (i c) p", p=P), 0, 80),
                (ssm_norm_w.rearrange("i (c p) -> (i c) p", p=P), 0, 112),
                (ssm_conv_w.rearrange("i k (c p) -> (i k c) p", p=P), 1, 0),
                (mlstm_conv_2.rearrange("i k (c p) -> (i k c) p", p=P), 2, 0),
                (mla_q_a_norm.rearrange("i (c p) -> (i c) p", p=P), 2, 64),
                (mla_kv_a_norm.rearrange("i (c p) -> (i c) p", p=P), 2, 67)]
        ROWS_IN = [P, P, 69]

        PS = ctx.enter_context(nc.psum_tensor("PS", [P, 8, 512], FP32))
        psD = PS[:, 0:4, :]
        psG = PS[:, 4:6, :]
        psT = PS[:, 6, :]
        psS = PS[:, 7, :]
        flatD = PS[:, 0:4, :].rearrange("p b n -> p (b n)")
        flatG = PS[:, 4:8, :].rearrange("p b n -> p (b n)")

        pe_own, act_own, dve_own, pool_own = (sem(f"{e}_own") for e in ("pe", "act", "dve", "pool"))

        ff_s = sb("ff_s", [P, NT, FCH])
        ff_a = sb("ff_a", [P, NT, FCH])
        aTh = sb("aTh", [P, 2 * SEQ], FP32R)
        aTl = sb("aTl", [P, 2 * SEQ], FP32R)
        with ExitStack() as gap:
            sb("last_gap", [P, 10240], where=gap)
            last_hi = sb("last_hi", [P, 2 * SEQ], FP32R, where=gap)
            last_lo = sb("last_lo", [P, 2 * SEQ], FP32R, where=gap)
        stat = sb("stat", [P, NT])
        var = sb("var", [P, NT])
        rstd = sb("rstd", [P, NT])

        F_NAMES = "silu_done a_done ah_done al_done"
        N_NAMES = "sq_done var_done rstd_done n_done t_done h_done l_done"
        F, S_N = sems("ffn", F_NAMES), sems("norm", N_NAMES)
        tile0_done, x_added = sem("tile0_done"), sem("x_added")

        def normed(i, k):
            return S_N["l_done"], KD * i + k + 1

        def load_block(sp, b, n, it=0):
            if n >= SLOTS or not isinstance(it, int):
                sp.wait_ge(lo_done, n + 1 - SLOTS + SLOTS * it)
            for place, src in b.loads:
                sp.dma_start(place(raw[n % SLOTS]), src).then_inc(raw_loaded[n % SLOTS], 16)

        def split_hi(act, n, it=0):
            s, size = n % SLOTS, blocks[n].size
            act.wait_ge(raw_loaded[s], 32 * (n // SLOTS + 1) + 32 * it)
            if n >= SLOTS or not isinstance(it, int):
                act.wait_ge(block_used, n + 1 - SLOTS + SLOTS * it)
            act.activation(whi[s][:, 0:size], raw[s][:, 0:size], ACT.Copy).then_inc(hi_done, 1)

        def split_lo(dve, n, it=0):
            s, size = n % SLOTS, blocks[n].size
            dve.wait_ge(hi_done, n + 1 + SLOTS * it)
            dve.tensor_tensor(wlo[s][:, 0:size], raw[s][:, 0:size], whi[s][:, 0:size].bitcast(FP32),
                              ALU.subtract).then_inc(lo_done, 1)

        def wait_block(pe, n, it=0):
            pe.wait_ge(lo_done, n + 1 + SLOTS * it)

        def mm3(pe, o, lh, ll, rh, rl, start, stop, **kw):
            pe.matmul(o, lh, rh, start=start, stop=False, **kw)
            pe.matmul(o, lh, rl, start=False, stop=False, **kw)
            return pe.matmul(o, ll, rh, start=False, stop=stop, **kw)

        def mul_rows(pe, n, it, k0, nk, width, banks, first, last, Xh=XTh, Xl=XTl, ready=None, part=None):
            s, part = n % SLOTS, part or range(nk)
            wait_block(pe, n, it)
            for k in part:
                if ready is not None:
                    pe.wait_ge(*ready(k0 + k))
                sl = slice(k * width, (k + 1) * width)
                for t in range(NT):
                    ts_ = slice(t * P, (t + 1) * P)
                    m = mm3(pe, banks[t], Xh[:, k0 + k, ts_], Xl[:, k0 + k, ts_], whi[s][:, sl], wlo[s][:, sl],
                            first and k == 0, last and k == nk - 1)
            if part[-1] == nk - 1:
                m.then_inc(block_used, 1)
            return m

        def mul_out_part(pe, n, lefts, t, k, first, last, bank=lambda t, c: psD[:, 2 * t + c, :], halves=(0, 1)):
            s, (lh, ll) = n % SLOTS, lefts[k]
            for c in halves:
                sl = slice(k * DM + c * 512, k * DM + (c + 1) * 512)
                m = mm3(pe, bank(t, c), lh(t), ll(t), whi[s][:, sl], wlo[s][:, sl], first and k == 0, last and k == 1)
            return m

        def mul_out(pe, n, it, lefts, first, last, bank=lambda t, c: psD[:, 2 * t + c, :], by_tile=False,
                    by_half=None):
            wait_block(pe, n, it)
            if by_half:
                for c in range(2):
                    for k in range(2):
                        for t in range(NT):
                            m = mul_out_part(pe, n, lefts, t, k, first, last, bank, (c,))
                    m.then_inc(*((by_half, 1) if c == 0 else (block_used, 1)))
                return m
            for t, k in [(t, k) for t in range(NT) for k in range(2)] if by_tile else\
                        [(t, k) for k in range(2) for t in range(NT)]:
                m = mul_out_part(pe, n, lefts, t, k, first, last, bank)
                if by_tile and (t, k) == (0, 1):
                    m.then_inc(tile0_done, 1)
            m.then_inc(block_used, 1)
            return m

        def mul_features(pe, n, bank, it=0):
            s = n % SLOTS
            wait_block(pe, n, it)
            for c in range(2):
                for k in range(KD):
                    sl = slice(k * 2 * P + c * P, k * 2 * P + (c + 1) * P)
                    o = bank[:, c * SEQ:(c + 1) * SEQ]
                    pe.matmul(o, whi[s][:, sl], XTh[:, k, :], start=(k == 0), stop=False)
                    pe.matmul(o, whi[s][:, sl], XTl[:, k, :], start=False, stop=False)
                    m = pe.matmul(o, wlo[s][:, sl], XTh[:, k, :], start=False, stop=(k == KD - 1))
            m.then_inc(block_used, 1)
            return m

        def mul_first_features(pe, n, norm, banks=psG):
            s = n % SLOTS
            wait_block(pe, n)
            for k in range(KD):
                pe.wait_ge(*normed(norm, k))
                for c in range(2):
                    sl = slice(k * 2 * P + c * P, k * 2 * P + (c + 1) * P)
                    o = banks[:, c, 0:SEQ]
                    pe.matmul(o, whi[s][:, sl], XTh[:, k, :], start=(k == 0), stop=False)
                    pe.matmul(o, whi[s][:, sl], XTl[:, k, :], start=False, stop=False)
                    m = pe.matmul(o, wlo[s][:, sl], XTh[:, k, :], start=False, stop=(k == KD - 1))
            m.then_inc(block_used, 1)

        def mul_narrow(pe, n, parts):
            s, size = n % SLOTS, blocks[n].size // KD
            wait_block(pe, n)
            for o, c0, width in parts:
                for k in range(KD):
                    sl = slice(k * size + c0, k * size + c0 + width)
                    pe.matmul(o, whi[s][:, sl], XTh[:, k, :], start=(k == 0), stop=False)
                    pe.matmul(o, whi[s][:, sl], XTl[:, k, :], start=False, stop=False)
                    m = pe.matmul(o, wlo[s][:, sl], XTh[:, k, :], start=False, stop=(k == KD - 1))
            m.then_inc(block_used, 1)

        def features(i):
            if i == 0:
                return psG[:, :, 0:SEQ]
            return psD[:, i % 4, :].rearrange("p (c n) -> p c n", c=2)

        def halves(a):
            return [(lambda t, k=k: a[0][:, k * SEQ + t * P:k * SEQ + (t + 1) * P],
                     lambda t, k=k: a[1][:, k * SEQ + t * P:k * SEQ + (t + 1) * P]) for k in range(2)]

        A_T = (aTh, aTl)
        A_LAST = (last_hi[:, :], last_lo[:, :])

        def flat(a):
            return a[:, :, :].rearrange("p c n -> p (c n)")

        GATE, UP = psG[:, 0, :], psG[:, 1, :]
        GATE0, UP0 = psD[:, 2:4, 0:SEQ], psS

        def ffn_pe(pe, i, norm):
            n0, f0 = N[f"ffn{i}"], NFF * i
            mul_first_features(pe, n0, norm, psD[:, 2:4, :])
            mul_features(pe, n0 + 1, UP0)
            mul_features(pe, n0 + 2, GATE)
            mul_features(pe, n0 + 3, UP)
            pe.wait_ge(F["al_done"], f0 + 1)
            mul_out(pe, n0 + 4, 0, halves(A_T), True, False)
            with pe.Fori(1, NFF - 1) as j:
                pe.wait_ge(F["a_done"], f0 + j + 1)
                mul_features(pe, n0 + 2, GATE, j)
                mul_features(pe, n0 + 3, UP, j)
                pe.wait_ge(F["al_done"], f0 + j + 1)
                mul_out(pe, n0 + 4, j, halves(A_T), False, False)
            pe.wait_ge(F["al_done"], f0 + NFF)
            mul_out(pe, n0 + 3 * NFF - 1, 0, halves(A_LAST), False, True, by_tile=True)

        def ffn_act(act, i, at):
            n0, f0 = N[f"ffn{i}"], NFF * i

            def silu(gate, out, ready):
                act.wait_ge(block_used, ready)
                act.activation(out, gate, ACT.Silu).then_inc(F["silu_done"], 1)

            def left_hi(j, a, free=None):
                if free is not None:
                    act.wait_ge(block_used, free)
                act.wait_ge(F["a_done"], f0 + j + 1)
                act.activation(a, flat(ff_a), ACT.Copy).then_inc(F["ah_done"], 1)

            hi_upto(act, at, n0 + 2)
            silu(GATE0, ff_s[:, :, :], n0 + 1)
            split_hi(act, n0 + 3)
            left_hi(0, aTh[:, :])
            for c in range(1, 3):
                split_hi(act, n0 + 3 + c)
            silu(GATE, flat(ff_s), n0 + 3)
            with act.Fori(1, NFF - 1) as j:
                split_hi(act, n0 + 3, j)
                left_hi(j, aTh[:, :], n0 + 2 + 3 * j)
                for c in range(1, 3):
                    split_hi(act, n0 + 3 + c, j)
                silu(GATE, flat(ff_s), n0 + 3 + 3 * j)
            at.n = n0 + 3 * NFF
            left_hi(NFF - 1, A_LAST[0])
            hi_upto(act, at, at.n + 1)

        def ffn_dve(dve, i, at):
            n0, f0 = N[f"ffn{i}"], NFF * i

            def gated(j, up, out, silu, ready, free=None):
                if free is not None:
                    dve.wait_ge(F["al_done"], free)
                dve.wait_ge(block_used, ready)
                dve.wait_ge(F["silu_done"], f0 + j + 1)
                dve.tensor_tensor(out, up, silu, ALU.mult).then_inc(F["a_done"], 1)

            def left_lo(j, hi, lo):
                dve.wait_ge(F["ah_done"], f0 + j + 1)
                dve.tensor_tensor(lo, flat(ff_a), hi.bitcast(FP32), ALU.subtract).then_inc(F["al_done"], 1)

            lo_upto(dve, at, n0 + 2)
            gated(0, UP0, flat(ff_a), flat(ff_s), n0 + 2)
            split_lo(dve, n0 + 3)
            left_lo(0, aTh[:, :], aTl[:, :])
            for c in range(1, 3):
                split_lo(dve, n0 + 3 + c)
            gated(1, UP, flat(ff_a), flat(ff_s), n0 + 4, f0 + 1)
            with dve.Fori(1, NFF - 1) as j:
                split_lo(dve, n0 + 3, j)
                left_lo(j, aTh[:, :], aTl[:, :])
                for c in range(1, 3):
                    split_lo(dve, n0 + 3 + c, j)
                gated(j + 1, UP, flat(ff_a), flat(ff_s), n0 + 4 + 3 * j, f0 + j + 1)
            at.n = n0 + 3 * NFF
            left_lo(NFF - 1, *A_LAST)
            lo_upto(dve, at, at.n + 1)

        def hi_upto(act, at, n):
            while at.n <= min(n, NB - 1):
                split_hi(act, at.n)
                at.n += 1

        def lo_upto(dve, at, n):
            while at.n <= min(n, NB - 1):
                split_lo(dve, at.n)
                at.n += 1

        diag = ff_s[:, :, 0:P]
        XT_BANK = [6, 7, 0, 1]

        def x_turned(c):
            return PS[:, XT_BANK[c // 2], (c % 2) * SEQ:(c % 2 + 1) * SEQ]

        def add_product(dve, i, used, scale):
            def add(t):
                if t == 0:
                    dve.wait_ge(tile0_done, i + 1)
                else:
                    dve.wait_ge(block_used, used)
                dve.scalar_tensor_tensor(out=xs_[:, t, :], in0=flatD[:, t * DM:(t + 1) * DM], scalar=scale,
                                         in1=xs_[:, t, :], op0=ALU.mult, op1=ALU.add).then_inc(x_added, 1)
            return add

        def norm_squares(act, i):
            S = S_N
            for t in range(NT):
                if i == 0:
                    act.wait_ge(x_in[t], 16)
                else:
                    act.wait_ge(x_added, NT * (i - 1) + t + 1)
                act.activation(xn[:, t, :], xs_[:, t, :], ACT.Square, accum_out=stat[:, t:t + 1])\
                   .then_inc(S["sq_done"], 1)

        def norm_hi(act, i, col):
            S = S_N
            for c in range(KD):
                act.wait_ge(S["t_done"], 4 * i + c // 2 + 1)
                act.activation(XTh[:, c, :], x_turned(c), ACT.Copy,
                               scale=cols[0][:, col + c:col + c + 1]).then_inc(S["h_done"], 1)

        def norm_act(act, i, col):
            norm_squares(act, i)
            norm_hi(act, i, col)

        def norm_dve(dve, i, col, update=None, between=lambda: None,
                     early=True):
            S = S_N

            def rms(t):
                dve.wait_ge(S["sq_done"], NT * i + t + 1)
                dve.tensor_scalar(var[:, t:t + 1], stat[:, t:t + 1], 1.0 / DM, EPS, ALU.mult, ALU.add)\
                   .then_inc(S["var_done"], 1)

            def scaled_identity(t):
                dve.wait_ge(S["rstd_done"], NT * i + t + 1)
                dve.tensor_scalar(diag[:, t, :], ident[:, :], rstd[:, t:t + 1], None, ALU.mult)\
                   .then_inc(S["n_done"], 1)

            if update:
                update(0)
            if early:
                rms(0)
            if update:
                update(1)
            if not early:
                rms(0)
            scaled_identity(0)
            rms(1)
            scaled_identity(1)
            between()
            for c in range(KD):
                dve.wait_ge(S["h_done"], KD * i + 2 * (c // 2) + 2)
                dve.scalar_tensor_tensor(out=XTl[:, c, :], in0=x_turned(c), scalar=cols[0][:, col + c:col + c + 1],
                                         in1=XTh[:, c, :].bitcast(FP32), op0=ALU.mult, op1=ALU.subtract)\
                   .then_inc(S["l_done"], 1)

        def norm_pool(pool, i):
            S = S_N
            for t in range(NT):
                pool.wait_ge(S["var_done"], NT * i + t + 1)
                pool.tensor_tensor(rstd[:, t:t + 1], var[:, t:t + 1], neghalf[:, 0:1], ALU.pow)\
                    .then_inc(S["rstd_done"], 1)

        def norm_pe(pe, i):
            S = S_N
            for t in range(NT):
                pe.wait_ge(S["n_done"], NT * i + t + 1)
                for c in range(KD):
                    m = pe.matmul(x_turned(c)[:, t * P:(t + 1) * P], xs_[:, t, c * P:(c + 1) * P], diag[:, t, :],
                                  start=True, stop=True)
                    if t == 1 and c % 2:
                        m.then_inc(S["t_done"], 1)

        def left_pe(pe, S, src, ready):
            for b in range(4):
                pe.wait_ge(*ready(b))
                for c in range(2):
                    for t in range(NT):
                        k = 2 * b + c
                        m = pe.transpose(flatG[:, (2 * k + t) * P:(2 * k + t + 1) * P], src[:, t, k * P:(k + 1) * P],
                                         ident[:, :])
                m.then_inc(S["lt"], 1)

        def left_act(act, S, Xh, base=0):
            for b in range(4):
                act.wait_ge(S["lt"], base + b + 1)
                act.activation(Xh[:, 2 * b:2 * b + 2, :], PS[:, 4 + b, :].rearrange("p (k n) -> p k n", k=2), ACT.Copy)\
                   .then_inc(S["lh"], 1)

        def left_dve(dve, S, Xh, Xl, base=0):
            for b in range(4):
                dve.wait_ge(S["lh"], base + b + 1)
                dve.tensor_tensor(Xl[:, 2 * b:2 * b + 2, :], PS[:, 4 + b, :].rearrange("p (k n) -> p k n", k=2),
                                  Xh[:, 2 * b:2 * b + 2, :].bitcast(FP32), ALU.subtract).then_inc(S["ll"], 1)

        def project_pe(pe, S, n, Xh, Xl, base=0, by_tile=False, by_half=None):
            for b in range(4):
                pe.wait_ge(S["ll"], base + b + 1)
                left = [(lambda t, k=k: Xh[:, k, t * P:(t + 1) * P], lambda t, k=k: Xl[:, k, t * P:(t + 1) * P])
                        for k in (2 * b, 2 * b + 1)]
                mul_out(pe, n + b, 0, left, b == 0, b == 3, by_tile=by_tile and b == 3,
                        by_half=by_half if b == 3 else None)

        posi = sb("posi", [P, NT], I32)
        posf = sb("posf", [P, NT])
        freq = sb("freq", [P, HR])
        ang = sb("ang", [P, NT, HR])
        turns = sb("turns", [P, NT, HR])
        trig = sb("trig", [P, 2, NT, HR])
        qn_row = sb("qn_row", [P, DQ])
        kn_row = sb("kn_row", [P, DQ])
        q_gain = sb("q_gain", [DQ, 1])
        k_gain = sb("k_gain", [DN, 1])
        mss = sb("mss", [P, 3, NT])
        mvar = sb("mvar", [P, 3, NT])
        mrs = sb("mrs", [P, 3, NT])
        krot = sb("krot", [P, NT, DR])
        ktmp = sb("ktmp", [P, 4, NT, HR])
        mx = sb("mx", [P, 2, NT])
        nmx = sb("nmx", [P, 2, NT])
        psum_ = sb("prob_sum", [P, NT, MH])
        rsum = sb("rsum", [P, NT, MH])
        notyet = sb("notyet", [P, TRI])
        ssm_ctx = ExitStack()
        conv_acc = sb("conv_acc", [P, 2, 2, SEQ])
        hrow = sb("hrow", [SSM_HEADS, 8, SEQ], where=ssm_ctx)
        acs_hi, acs_lo = aTh[0:SSM_HEADS, 0:SEQ], aTl[0:SSM_HEADS, 0:SEQ]
        H_X, H_E, H_LN, H_D, H_Q, H_DT, H_DA, H_ACS = range(8)
        dtb = sb("dtb", [SSM_HEADS, 1], where=ssm_ctx)
        alog = sb("alog", [SSM_HEADS, 1], where=ssm_ctx)
        expa = sb("expa", [SSM_HEADS, 1], where=ssm_ctx)
        dskip = sb("dskip", [P, SSM_HEADS], where=ssm_ctx)
        hcol = sb("hcol", [P, 2, NT, SSM_HEADS], where=ssm_ctx)
        xs_t = sb("xs_t", [P, 3, 2, SEQ], where=ssm_ctx)
        zs = sb("zs", [P, NT, D_INNER], where=ssm_ctx)
        decay = sb("decay", [P, SSM_R * TRI], where=ssm_ctx)
        mix = sb("mix", [P, SSM_R * TRI], where=ssm_ctx)
        masked = sb("masked", [P, SEQ], FP32R, where=ssm_ctx)
        dxs = sb("dxs", [P, 2, NT, SSM_R * SSM_P], where=ssm_ctx)
        gss = sb("gss", [P, SSM_G, NT], where=ssm_ctx)
        gvar = sb("gvar", [P, SSM_G, NT], where=ssm_ctx)
        grstd = sb("grstd", [P, SSM_G, NT], where=ssm_ctx)
        sq_junk = ff_s
        with ExitStack() as sub:
            BC = sb("BC", [P, 2 * SSM_G, SEQ], where=sub)
            xs_nat = sb("xs_nat", [P, NT, D_INNER], where=sub)
        with ExitStack() as sub:
            gTh = sb("gTh", [P, D_INNER // P, SEQ], FP32R, where=sub)
            gTl = sb("gTl", [P, D_INNER // P, SEQ], FP32R, where=sub)
        ssm_ctx.close()
        A = sems("ssm", "in xb e dta dtN coln acc tap silu turned nat z b masked e_done m dx y y_read yz sq var r gs "
                        "gt gh gl")
        NXB = 16
        HALF = SSM_R * SEQ

        def xbc_tiles(i):
            return (16 + 2 * i, 17 + 2 * i) if i < 8 else (2 * (i - 8), 2 * (i - 8) + 1)

        def ssm_pe(pe):
            nd, nx, nz, no = N["dt"], N["bc"], N["z"], N["ssm_out"]
            def z_block(k):
                q, h = k // 2, k % 2
                if h == 0:
                    pe.wait_ge(*((A["z"], q) if q else (A["tap"], 14)))
                mul_rows(pe, nz + k, 0, 4 * h, 4, 512, [psD[:, t, :] for t in range(NT)], h == 0, h == 1)

            mul_first_features(pe, N["bc0"], 1)
            mul_narrow(pe, nd, [(psT[0:SSM_HEADS, 0:SEQ], 0, SSM_HEADS)])
            for i in range(NXB + 2):
                if i == NXB:
                    z_block(0)
                if 1 <= i < NXB:
                    if i >= 4:
                        pe.wait_ge(A["tap"], i - 3)
                    mul_features(pe, nx + i, psD[:, i % 4, :])
                if i == 6:
                    pe.wait_ge(A["dta"], 1)
                    for kind, row in enumerate((H_DT, H_ACS)):
                        for t in range(NT):
                            c = (kind * NT + t) * SSM_HEADS
                            m = pe.transpose(psS[:, c:c + SSM_HEADS], hrow[:, row, t * P:(t + 1) * P],
                                             ident[0:SSM_HEADS, 0:SSM_HEADS])
                    m.then_inc(A["dtN"], 1)
                b = i - 10
                if b >= 0:
                    pe.wait_ge(A["silu"], 8 + b + 1)
                    if b >= 2:
                        pe.wait_ge(A["nat"], b - 1)
                    for t in range(NT):
                        for c in range(2):
                            m = pe.transpose(psG[:, b % 2, t * SEQ + c * P:t * SEQ + (c + 1) * P],
                                             xs_t[:, b % 3, c, t * P:(t + 1) * P], ident[:, :])
                    m.then_inc(A["turned"], 1)

            def scores(g):
                if g == 0:
                    pe.wait_ge(A["coln"], 1)
                    pe.wait_ge(A["nat"], 8)
                    pe.wait_ge(A["masked"], 1)
                    pe.wait_ge(A["tap"], 16)
                else:
                    pe.wait_ge(A["e_done"], g)
                    pe.wait_ge(A["m"], g)
                for b, width in ((psG[:, 0, :], SEQ), (psG[:, 1, :], SEQ), (psD[:, 3, :], P)):
                    pe.matmul(b.rearrange("p (r n) -> p r n", n=width), ident_r[:, :],
                              masked[:, 0:width].unsqueeze(1).to_broadcast([P, 512 // width, width]),
                              start=True, stop=False)
                for r in range(SSM_R):
                    h = g * SSM_R + r
                    one = ident_r[0:SSM_HEADS, h:h + 1].to_broadcast([SSM_HEADS, P])
                    for o, q0 in ((psG[:, r // 2, (r % 2) * SEQ:(r % 2 + 1) * SEQ], 0), (psD[:, 3, r * P:(r + 1) * P], P)):
                        pe.matmul(o, one, acs_hi[:, q0:SEQ], start=False, stop=False)
                        pe.matmul(o, one, acs_lo[:, q0:SEQ], start=False, stop=r % 2 == 1 if q0 == 0 else r == 3)
                pe.matmul(psT[:, 0:SEQ], BC[:, g, 0:P], BC[:, SSM_G + g, :], start=True, stop=True)
                pe.matmul(psT[:, SEQ:TRI], BC[:, g, P:SEQ], BC[:, SSM_G + g, P:SEQ], start=True, stop=True)\
                  .then_inc(A["b"], 1)

            def outputs(g):
                pe.wait_ge(A["m"], g + 1)
                pe.wait_ge(A["dx"], g + 1)
                if g >= 1:
                    pe.wait_ge(A["y_read"], g)
                W = SSM_R * SSM_P
                for t in range(NT):
                    for r in range(SSM_R):
                        o = psS[:, t * W + r * SSM_P:t * W + (r + 1) * SSM_P]
                        hc = slice((g * SSM_R + r) * SSM_P, (g * SSM_R + r + 1) * SSM_P)
                        m = pe.matmul(o, mix[:, r * SEQ + t * P:r * SEQ + (t + 1) * P], xs_nat[:, 0, hc],
                                      start=True, stop=(t == 0))
                        if t == 1:
                            m = pe.matmul(o, mix[:, HALF + r * P:HALF + (r + 1) * P], xs_nat[:, 1, hc],
                                          start=False, stop=True)
                m.then_inc(A["y"], 1)

            scores(0)
            z_block(1)
            for g in range(SSM_G):
                if g + 1 < SSM_G:
                    scores(g + 1)
                outputs(g)
                if g + 2 < 8:
                    z_block(g + 2)

            def turn(g):
                pe.wait_ge(A["gs"], g + 1)
                if g >= 2:
                    pe.wait_ge(A["gl"], g - 1)
                for c in range(2):
                    for t in range(NT):
                        m = pe.transpose(psG[:, g % 2, c * SEQ + t * P:c * SEQ + (t + 1) * P],
                                         zs[:, t, (2 * g + c) * P:(2 * g + c + 1) * P], ident[:, :])
                m.then_inc(A["gt"], 1)

            turn(0)
            pe.wait_ge(A["z"], 4)
            for g in range(SSM_G):
                if g + 1 < SSM_G:
                    turn(g + 1)
                pe.wait_ge(A["gl"], g + 1)
                left = [(lambda t, k=k: gTh[:, k, t * P:(t + 1) * P], lambda t, k=k: gTl[:, k, t * P:(t + 1) * P])
                        for k in (2 * g, 2 * g + 1)]
                mul_out(pe, no + g, 0, left, g == 0, g == SSM_G - 1, by_tile=g == SSM_G - 1)

        def conv_act(act, S, i, n, tiles, taps, bias, prev):
            if n is not None:
                act.wait_ge(block_used, n + 1)
                if i >= 2:
                    act.wait_ge(S["silu"], i - 1)
                for c in range(2):
                    m = act.activation(conv_acc[:, i % 2, c, :], features(i)[:, c, :], ACT.Identity,
                                       scale=taps(tiles[c], CONV_K - 1), bias=bias(tiles[c]))
                m.then_inc(S["acc"], 1)
            if prev is not None:
                act.wait_ge(S["tap"], i)
                act.activation(prev, conv_acc[:, (i - 1) % 2, :, :], ACT.Silu).then_inc(S["silu"], 1)

        def conv_dve(dve, own, S, i, tiles, taps):
            dve.wait_ge(S["acc"], i + 1)
            for j in range(CONV_K - 2, -1, -1):
                sh = CONV_K - 1 - j
                for c in range(2):
                    a = conv_acc[:, i % 2, c, sh:SEQ]
                    m = dve.scalar_tensor_tensor(out=a, in0=features(i)[:, c, 0:SEQ - sh],
                                                 scalar=taps(tiles[c], j), in1=a, op0=ALU.mult, op1=ALU.add)
                if j:
                    own.link(m)
                else:
                    m.then_inc(S["tap"], 1)

        def ssm_taps(ct, j):
            return cols[1][:, j * (XBC // P) + ct:j * (XBC // P) + ct + 1]

        def ssm_act(act, at):
            nd, nx, nz, no = N["dt"], N["bc"], N["z"], N["ssm_out"]
            hi_upto(act, at, nd + 2)
            act.wait_ge(A["in"], 48)
            act.activation(expa[:, :], alog[:, :], ACT.Exp).then_inc(A["e"], 1)
            for i in range(NXB + 1):
                hi_upto(act, at, nx + i + 2)
                if i == 1:
                    act.wait_ge(A["xb"], 1)
                    act.activation(hrow[:, H_E, :], hrow[:, H_Q, :], ACT.Exp, scale=-1.0).then_inc(A["e"], 1)
                if i == 2:
                    act.wait_ge(A["e"], 2)
                    act.activation(hrow[:, H_LN, :], hrow[:, H_E, :], ACT.Ln, bias=ones[0:SSM_HEADS, 0:1])\
                       .then_inc(A["e"], 1)
                if i - 1 < 8:
                    prev = BC[:, 2 * (i - 1):2 * i, :] if i else None
                else:
                    prev = xs_t[:, (i - 9) % 3, :, :]
                    if i - 9 >= 3:
                        act.wait_ge(A["turned"], i - 9 - 2)
                conv_act(act, A, i, (nx + i if i else N["bc0"]) if i < NXB else None, xbc_tiles(i) if i < NXB else None, ssm_taps,
                         lambda ct: cols[0][:, 80 + ct:81 + ct], prev)
                if i >= 11:
                    ssm_nat(act, i - 11)
            for b in range(6, 8):
                ssm_nat(act, b)
            mla_tables_act(act)
            for g in range(-1, SSM_G):
                hi_upto(act, at, nz + g + 3)
                if g + 1 < SSM_G:
                    act.wait_ge(A["b"], g + 2)
                    if g >= 0:
                        act.wait_ge(A["m"], g + 1)
                    for r in range(SSM_R):
                        h = (g + 1) * SSM_R + r
                        act.activation(decay[:, r * SEQ:(r + 1) * SEQ], psG[:, r // 2, (r % 2) * SEQ:(r % 2 + 1) * SEQ],
                                       ACT.Exp, bias=hcol[:, 1, 0, h:h + 1])
                        m = act.activation(decay[:, HALF + r * P:HALF + (r + 1) * P], psD[:, 3, r * P:(r + 1) * P],
                                           ACT.Exp, bias=hcol[:, 1, 1, h:h + 1])
                    m.then_inc(A["e_done"], 1)
                if g >= 0:
                    act.wait_ge(A["yz"], g + 1)
                    for t in range(NT):
                        act.activation(sq_junk[:, t, :], zs[:, t, g * 256:(g + 1) * 256], ACT.Square,
                                       accum_out=gss[:, g, t:t + 1]).then_inc(A["sq"], 1)
                k = g + 2
                if k < 8 and k % 2:
                    act.wait_ge(block_used, nz + k + 1)
                    q = k // 2
                    act.activation(zs[:, :, q * 512:(q + 1) * 512], psD[:, 0:2, :], ACT.Silu)\
                       .then_inc(A["z"], 1)
            for g in range(SSM_G):
                hi_upto(act, at, no + g + 1)
                act.wait_ge(A["gt"], g + 1)
                for c in range(2):
                    k = 2 * g + c
                    act.activation(gTh[:, k, :], psG[:, g % 2, c * SEQ:(c + 1) * SEQ], ACT.Copy,
                                   scale=cols[0][:, 112 + k:113 + k]).then_inc(A["gh"], 1)
            hi_upto(act, at, no + 9)

        def ssm_nat(act, b):
            act.wait_ge(A["turned"], b + 1)
            act.activation(xs_nat[:, :, b * 256:(b + 1) * 256],
                           psG[:, b % 2, :].rearrange("p (t n) -> p t n", t=NT), ACT.Copy).then_inc(A["nat"], 1)

        def ssm_dve(dve, at, own):
            nd, nx, nz, no = N["dt"], N["bc"], N["z"], N["ssm_out"]
            H = SSM_HEADS
            lo_upto(dve, at, nd + 2)

            def dt_input():
                dve.wait_ge(A["in"], 48)
                dve.wait_ge(block_used, nd + 1)
                own.link(dve.tensor_scalar(hrow[:, H_X, :], psT[0:H, 0:SEQ], dtb[:, 0:1], None, ALU.add))
                dve.scalar_tensor_tensor(out=hrow[:, H_Q, :], in0=hrow[:, H_X, :], scalar=-1.0, in1=hrow[:, H_X, :],
                                         op0=ALU.mult, op1=ALU.max).then_inc(A["xb"], 1)

            def dt_quotient():
                dve.wait_ge(A["e"], 2)
                own.link(dve.tensor_scalar(hrow[:, H_D, :], hrow[:, H_E, :], 1.0, -1.0, ALU.add, ALU.add))
                own.link(dve.tensor_scalar(hrow[:, H_Q, :], hrow[:, H_D, :], 1e-30, None, ALU.max))
                own.link(dve.reciprocal(hrow[:, H_Q, :], hrow[:, H_Q, :]))
                own.link(dve.tensor_tensor(hrow[:, H_Q, :], hrow[:, H_Q, :], hrow[:, H_E, :], ALU.mult))

            def dt_value():
                dve.wait_ge(A["e"], 3)
                own.link(dve.tensor_tensor(hrow[:, H_Q, :], hrow[:, H_Q, :], hrow[:, H_LN, :], ALU.mult))
                own.link(dve.scalar_tensor_tensor(out=hrow[:, H_D, :], in0=hrow[:, H_D, :], scalar=0.0,
                                                  in1=hrow[:, H_E, :], op0=ALU.is_equal, op1=ALU.mult))
                own.link(dve.tensor_tensor(hrow[:, H_Q, :], hrow[:, H_Q, :], hrow[:, H_D, :], ALU.add))
                own.link(dve.scalar_tensor_tensor(out=hrow[:, H_DT, :], in0=hrow[:, H_X, :], scalar=0.0,
                                                  in1=hrow[:, H_Q, :], op0=ALU.max, op1=ALU.add))

            def decay_sums():
                own.link(dve.tensor_scalar(hrow[:, H_DA, :], hrow[:, H_DT, :], expa[:, 0:1], -1.0, ALU.mult, ALU.mult))
                own.link(dve.tensor_tensor_scan(out=hrow[:, H_ACS, :], data0=ones[0:H, :], data1=hrow[:, H_DA, :],
                                                initial=0.0, op0=ALU.mult, op1=ALU.add))
                own.link(dve.tensor_copy(acs_hi[:, :], hrow[:, H_ACS, :]))
                dve.tensor_tensor(acs_lo[:, :], hrow[:, H_ACS, :], acs_hi[:, :].bitcast(FP32), ALU.subtract)\
                   .then_inc(A["dta"], 1)

            dt_input()
            for i in range(NXB):
                lo_upto(dve, at, nx + i + 2)
                conv_dve(dve, own, A, i, xbc_tiles(i), ssm_taps)
                if i == 1:
                    dt_quotient()
                if i == 2:
                    dt_value()
                if i == 3:
                    decay_sums()
                if i == 12:
                    mla_tables_dve(dve, own)
                if i == 7:
                    dve.wait_ge(A["dtN"], 1)
                    dve.tensor_copy(hcol[:, 0, :, :].rearrange("p t h -> p (t h)"), psS[:, 0:NT * H])
                    dve.tensor_scalar(hcol[:, 1, :, :].rearrange("p t h -> p (t h)"), psS[:, NT * H:2 * NT * H], -1.0,
                                      None, ALU.mult).then_inc(A["coln"], 1)
            dve.wait_ge(A["coln"], 1)
            for g in range(-1, SSM_G):
                gs = slice(g * 256, (g + 1) * 256)
                lo_upto(dve, at, nz + g + 3)
                if g >= 0:
                    dx = dxs[:, g % 2, :, :]
                    dve.wait_ge(A["y"], g + 1)
                    dve.tensor_tensor(dx, psS.rearrange("p (t n) -> p t n", t=NT), dx, ALU.add).then_inc(A["y_read"], 1)
                    dve.wait_ge(A["z"], g // 2 + 1)
                    dve.wait_ge(A["y_read"], g + 1)
                    dve.tensor_tensor(zs[:, :, gs], dx, zs[:, :, gs], ALU.mult).then_inc(A["yz"], 1)
                if g + 1 < SSM_G:
                    dve.wait_ge(A["e_done"], g + 2)
                    for part, w, k in ((slice(0, HALF), SEQ, slice(0, SEQ)), (slice(HALF, SSM_R * TRI), P, slice(SEQ, TRI))):
                        m = dve.tensor_tensor(mix[:, part].rearrange("p (r n) -> p r n", n=w),
                                              decay[:, part].rearrange("p (r n) -> p r n", n=w),
                                              psT[:, k].unsqueeze(1).to_broadcast([P, SSM_R, w]), ALU.mult)
                    m.then_inc(A["m"], 1)
                if g >= 0:
                    dve.wait_ge(A["sq"], 2 * g + 2)
                    dve.tensor_scalar(gvar[:, g, :], gss[:, g, :], 1.0 / 256, EPS, ALU.mult, ALU.add)\
                       .then_inc(A["var"], 1)
                    dve.wait_ge(A["r"], g + 1)
                    for t in range(NT):
                        m = dve.tensor_scalar(zs[:, t, gs], zs[:, t, gs], grstd[:, g, t:t + 1], None, ALU.mult)
                    m.then_inc(A["gs"], 1)
            for g in range(SSM_G):
                lo_upto(dve, at, no + g + 1)
                dve.wait_ge(A["gh"], 2 * g + 2)
                for c in range(2):
                    k = 2 * g + c
                    m = dve.scalar_tensor_tensor(out=gTl[:, k, :], in0=psG[:, g % 2, c * SEQ:(c + 1) * SEQ],
                                                 scalar=cols[0][:, 112 + k:113 + k], in1=gTh[:, k, :].bitcast(FP32),
                                                 op0=ALU.mult, op1=ALU.subtract)
                m.then_inc(A["gl"], 1)
            lo_upto(dve, at, no + 9)

        def ssm_pool(pool):
            def by_head(g, col):
                return col[:, g * SSM_R:(g + 1) * SSM_R].unsqueeze(2).to_broadcast([P, SSM_R, SSM_P])

            def inputs(g):
                if g >= 2:
                    pool.wait_ge(A["yz"], g - 1)
                x = [xs_nat[:, t, g * 256:(g + 1) * 256].rearrange("p (r n) -> p r n", r=SSM_R) for t in range(NT)]
                for t in range(NT):
                    pool.tensor_tensor(dxs[:, g % 2, t, :].rearrange("p (r n) -> p r n", r=SSM_R), x[t],
                                       by_head(g, dskip), ALU.mult)
                for t in range(NT):
                    m = pool.tensor_tensor(x[t], x[t], by_head(g, hcol[:, 0, t, :]), ALU.mult)
                m.then_inc(A["dx"], 1)
            pool.wait_ge(A["in"], 48)
            pool.wait_ge(A["coln"], 1)
            for g in range(2):
                pool.wait_ge(A["nat"], g + 1)
                inputs(g)
            for g in range(SSM_G):
                pool.wait_ge(A["var"], g + 1)
                pool.tensor_tensor(grstd[:, g, :], gvar[:, g, :], neghalf[:, 0:NT], ALU.pow).then_inc(A["r"], 1)
                if g + 2 < SSM_G:
                    pool.wait_ge(A["nat"], g + 3)
                    inputs(g + 2)

        mla_ctx = ExitStack()
        q_nat = sb("q_nat", [P, NT, MH, DQ], where=mla_ctx)
        k_nat = sb("k_nat", [P, NT, MH, DQ], where=mla_ctx)
        v_nat = sb("v_nat", [P, NT, MH, DV], where=mla_ctx)
        qT = sb("qT", [DQ, MH, SEQ], where=mla_ctx)
        hss, hvar, hroot, hrs = (sb(n, [P, 3, NT * MH], where=mla_ctx)
                                 for n in "head_sums head_var head_root head_rs".split())
        rot = sb("rot", [P, 4, NT, HR], where=mla_ctx)
        with ExitStack() as sub:
            rtmp = sb("rtmp", [P, NT, 4, MH, HR], where=sub)
        kT = sb("kT", [DQ, MH, SEQ], where=mla_ctx)
        with ExitStack() as sub:
            cn = sb("cn", [P, NT, QL + KVL], where=sub)
            cTh = sb("cTh", [P, 5, SEQ], FP32R, where=sub)
            cTl = sb("cTl", [P, 5, SEQ], FP32R, where=sub)
        with ExitStack() as sub:
            sS = sb("sS", [P, 2, TRI], where=sub)
            prob = sb("prob", [P, 2, TRI], where=sub)
            probT = sb("probT", [P, 2, TRI], where=sub)
        sq_nope = xn[:, :, :].rearrange("p t (h d) -> p t h d", h=MH)
        sq_rope = cn[:, :, 0:MH * DR].rearrange("p t (h d) -> p t h d", h=MH)
        sq_k = [b[:, :, :].rearrange("p a n -> p (a n)").rearrange("p (h d) -> p h d", d=DN) for b in (ff_s, ff_a)]
        mla_ctx.close()
        M = sems("mla", "in gain1 trig_in trig_out mask sq var r cn ct ch cl qcopied sqq sqk vcopied hv root qn rope krr kb kn "
                        "qt qtc ktc s nm e pt ptc o od lt lh ll")
        RW = KVL + DR

        def mla_tables_pool(pool, own):
            for i in range(HR):
                m = pool.memset(freq[:, i:i + 1], float(np.float32(1.0) / np.float32(ROPE_THETA) ** np.float32(2 * i / DR)))
            own.mark(m)
            pool.memset(q_gain[:, :], 1.0).then_inc(M["gain1"], 1)
            own.mark(pool.memset(notyet[:, :], 0.0))
            own.wait()
            pool.affine_select(out=notyet[:, 0:P], in_=notyet[:, 0:P], compare_op=ALU.is_ge, fill=-BIG, base=0,
                               pattern=[[-1, P]], channel_multiplier=1).then_inc(M["mask"], 1)
            pool.affine_select(out=notyet[:, 2 * P:TRI], in_=notyet[:, 2 * P:TRI], compare_op=ALU.is_ge, fill=-BIG,
                               base=0, pattern=[[-1, P]], channel_multiplier=1).then_inc(M["mask"], 1)

        def mla_tables_dve(dve, own):
            dve.wait_ge(M["in"], 80)
            own.link(dve.tensor_tensor(q_gain[0:DN, :], q_gain[0:DN, :], k_gain[:, :], ALU.mult))
            dve.wait_ge(M["mask"], 2)
            own.link(dve.tensor_copy(posf[:, :], posi[:, :]))
            for t in range(NT):
                m = dve.tensor_scalar(ang[:, t, :], freq[:, :], posf[:, t:t + 1], None, ALU.mult)
            own.link(m)
            for k, shift in enumerate((0.0, 0.25)):
                n, r = turns[:, :, :], trig[:, k, :, :]
                own.link(dve.tensor_scalar(n, ang[:, :, :], 1.0 / (2 * math.pi), shift, ALU.mult, ALU.add))
                own.link(dve.tensor_scalar(n, n, ROUND, None, ALU.add))
                own.link(dve.tensor_scalar(n, n, -ROUND, None, ALU.add))
                own.link(dve.scalar_tensor_tensor(out=r, in0=n, scalar=-TWO_PI[0], in1=ang[:, :, :],
                                                  op0=ALU.mult, op1=ALU.add))
                for c in TWO_PI[1:]:
                    own.link(dve.scalar_tensor_tensor(out=r, in0=n, scalar=-c, in1=r, op0=ALU.mult, op1=ALU.add))
                own.link(dve.tensor_scalar(r, r, math.pi / 2 if k else 0.0, 3.1415925, ALU.add, ALU.min))
                dve.tensor_scalar(r, r, -3.1415925, None, ALU.max).then_inc(M["trig_in"], 1)
                dve.wait_ge(M["trig_in"], k + 1)

        def mla_tables_act(act):
            act.wait_ge(M["trig_in"], 2)
            act.activation(trig[:, :, :, :], trig[:, :, :, :], ACT.Sin).then_inc(M["trig_out"], 1)

        KV_BANKS = [[2, 3, 4, 5], [6, 7, 0, 1]]

        def k_heads(a, c):
            return a[:, 2, :].rearrange("p (t h) -> p t h", t=NT)[:, :, 8 * c:8 * c + 8]

        SCORES_2 = 6

        def scores_bank(h):
            return h % 2 if h < SCORES_2 else 0

        def mla_pe(pe):
            nq, nk = N["cq"], N["kvr"]
            G = [psG[:, t, 0:QL] for t in range(NT)]
            mul_rows(pe, nq, 0, 0, 4, QL, G, True, False, ready=lambda k: normed(4, k))
            mul_rows(pe, nq + 1, 0, 4, 4, QL, G, False, True, ready=lambda k: normed(4, k))
            H = [PS[:, 6 + t, 0:RW] for t in range(NT)]
            mul_rows(pe, nk, 0, 0, 4, RW, H, True, False)
            mul_rows(pe, nk + 1, 0, 4, 4, RW, H, False, True)
            C_AT = [0, 1, 2, 4, 5]

            def turn_c(k_tiles):
                for c in k_tiles:
                    for t in range(NT):
                        o = C_AT[c] * SEQ + t * P
                        m = pe.transpose(flatD[:, o:o + P], cn[:, t, c * P:(c + 1) * P], ident[:, :])
                    m.then_inc(M["ct"], 1)

            pe.wait_ge(M["cn"], 2)
            turn_c(range(3))
            pe.wait_ge(M["cl"], 3)
            QB = [psG, PS[:, 6:8, :], psD[:, 0:2, :]]
            for c in range(3):
                if c == 1:
                    pe.wait_ge(M["cn"], 4)
                    turn_c(range(3, 5))
                    pe.wait_ge(M["krr"], 1)
                mul_rows(pe, N["wq"] + c, 0, 0, 3, 512, [QB[c][:, t, :] for t in range(NT)], True, True, Xh=cTh, Xl=cTl)
            left = [(lambda t, k=k: cTh[:, k, t * P:(t + 1) * P], lambda t, k=k: cTl[:, k, t * P:(t + 1) * P]) for k in (3, 4)]
            pe.wait_ge(M["cl"], 5)
            pe.wait_ge(M["qcopied"], 1)
            mul_out(pe, N["wkv"], 0, left, True, True, bank=lambda t, c: PS[:, KV_BANKS[0][2 * t + c], :])
            pe.wait_ge(M["qcopied"], 3)
            mul_out(pe, N["wkv"] + 1, 0, left, True, True, bank=lambda t, c: PS[:, KV_BANKS[1][2 * t + c], :])

            def turn_heads(src, i, bank, done):
                if i >= 2:
                    pe.wait_ge(done, i - 1)
                for h in range(2):
                    for t in range(NT):
                        m = pe.transpose(PS[0:DQ, bank + i % 2, h * SEQ + t * P:h * SEQ + (t + 1) * P],
                                         src[:, t, 2 * i + h, :], ident[:, :])
                m.then_inc(M["qt"], 1)

            pe.wait_ge(M["kb"], NT)
            pe.wait_ge(M["kn"], 1)
            for i in range(4):
                turn_heads(k_nat, i, 2, M["ktc"])
            pe.wait_ge(M["qn"], 2)
            for i in range(8):
                turn_heads(q_nat, i, 4, M["qtc"])
            pe.wait_ge(M["kn"], 2)
            for i in range(4, 8):
                turn_heads(k_nat, i, 2, M["ktc"])
            pe.wait_ge(M["ktc"], MH // 2)
            pe.wait_ge(M["qtc"], MH // 2)

            def scores(h):
                if h >= 2:
                    pe.wait_ge(M["nm"], h - 1 if h < SCORES_2 else h)
                o = psG[:, scores_bank(h), :]
                pe.matmul(o[:, 0:P], qT[:, h, 0:P], kT[:, h, 0:P], start=True, stop=True)
                pe.matmul(o[:, P:TRI], qT[:, h, P:SEQ], kT[:, h, :], start=True, stop=True).then_inc(M["s"], 1)

            def head_out(g):
                pe.wait_ge(M["ptc"], g + 1)
                if g % 4 == 0 and g:
                    pe.wait_ge(M["od"], g // 4)
                o = [psS[:, t * 256 + (g % 4) * DV:t * 256 + (g % 4 + 1) * DV] for t in range(NT)]
                pe.matmul(o[0], probT[:, g % 2, 0:P], v_nat[:, 0, g, :], start=True, stop=True)
                pe.matmul(o[1], probT[:, g % 2, P:2 * P], v_nat[:, 0, g, :], start=True, stop=False)
                pe.matmul(o[1], probT[:, g % 2, 2 * P:TRI], v_nat[:, 1, g, :], start=False, stop=True).then_inc(M["o"], 1)

            def turn_prob(g):
                pe.wait_ge(M["e"], 2 * g + 2)
                for c in range(3):
                    m = pe.transpose(psT[:, c * P:(c + 1) * P], prob[:, g % 2, c * P:(c + 1) * P], ident[:, :])
                m.then_inc(M["pt"], 1)

            def turn_out(b):
                pe.wait_ge(M["od"], b + 1)
                if b:
                    pe.wait_ge(M["ll"], b)
                for c in range(2):
                    for t in range(NT):
                        m = pe.transpose(psG[:, 1, (2 * c + t) * P:(2 * c + t + 1) * P],
                                         xn[:, t, (2 * b + c) * P:(2 * b + c + 1) * P], ident[:, :])
                m.then_inc(M["lt"], 1)

            def left_of(b):
                return [(lambda t, k=k: XTh[:, k, t * P:(t + 1) * P], lambda t, k=k: XTl[:, k, t * P:(t + 1) * P])
                        for k in (2 * b, 2 * b + 1)]

            def project_part(p):
                b, t, k = p // 4, p % 2, p // 2 % 2
                if p % 4 == 0:
                    pe.wait_ge(M["ll"], b + 1)
                    wait_block(pe, N["mla_out"] + b)
                m = mul_out_part(pe, N["mla_out"] + b, left_of(b), t, k, b == 0, False)
                if p % 4 == 3:
                    m.then_inc(block_used, 1)

            for h in range(MH + 2):
                if h < MH:
                    scores(h)
                if h >= 2:
                    head_out(h - 2)
                if h >= 8:
                    project_part(h - 8)
                if 1 <= h <= MH:
                    turn_prob(h - 1)
                if h % 4 == 2 and h >= 6:
                    turn_out((h - 6) // 4)
            turn_out(3)
            for p in range(MH + 2 - 8, 12):
                project_part(p)
            pe.wait_ge(M["ll"], 4)
            mul_out(pe, N["mla_out"] + 3, 0, left_of(3), False, True, by_tile=True)

        def mla_act(act, at):
            nq, nk = N["cq"], N["kvr"]
            hi_upto(act, at, nq + 3)
            act.wait_ge(block_used, nq + 2)
            for t in range(NT):
                act.activation(cn[:, t, 0:QL], psG[:, t, 0:QL], ACT.Square, accum_out=mss[:, 0, t:t + 1]).then_inc(M["sq"], 1)
            hi_upto(act, at, nk + 2)

            def c_hi(c):
                act.wait_ge(M["ct"], min(2 * (c // 2) + 2, 3) if c < 3 else 5)
                o = (0, 1, 2, 4, 5)[c] * SEQ
                act.activation(cTh[:, c, :], flatD[:, o:o + SEQ], ACT.Copy, scale=cols[2][:, 64 + c:65 + c])\
                   .then_inc(M["ch"], 1)

            for c in range(3):
                c_hi(c)
            act.wait_ge(block_used, nk + 2)
            for t in range(NT):
                act.activation(cn[:, t, QL:QL + KVL], PS[:, 6 + t, 0:KVL], ACT.Square, accum_out=mss[:, 1, t:t + 1])\
                   .then_inc(M["sq"], 1)
                act.activation(krot[:, t, :], PS[:, 6 + t, KVL:RW], ACT.Square, accum_out=mss[:, 2, t:t + 1])\
                   .then_inc(M["sq"], 1)
            hi_upto(act, at, N["wq"] + 1)
            for c in range(3, 5):
                c_hi(c)
            QB = [psG, PS[:, 6:8, :], psD[:, 0:2, :]]
            qf = q_nat[:, :, :, :].rearrange("p t h d -> p t (h d)")
            for c in range(3):
                hi_upto(act, at, N["wq"] + c + 2)
                act.wait_ge(block_used, N["wq"] + c + 1)
                act.activation(qf[:, :, c * 512:(c + 1) * 512], QB[c], ACT.Copy).then_inc(M["qcopied"], 1)
            act.wait_ge(M["qcopied"], 3)
            act.activation(sq_nope, q_nat[:, :, :, 0:DN], ACT.Square).then_inc(M["sqq"], 1)
            act.activation(sq_rope, q_nat[:, :, :, DN:DQ], ACT.Square).then_inc(M["sqq"], 1)

            def kv_chunk(c):
                act.wait_ge(block_used, N["wkv"] + c + 1)
                if c:
                    act.wait_ge(M["hv"], 2)
                v = [PS[:, b:b + 2, :].rearrange("p b (h e) -> p (b h) e", e=DN + DV) for b in KV_BANKS[c][0:4:2]]
                for t in range(NT):
                    act.activation(sq_k[t], v[t][:, :, 0:DN], ACT.Square).then_inc(M["sqk"], 1)
                for t in range(NT):
                    act.activation(v_nat[:, t, 8 * c:8 * c + 8, :], v[t][:, :, DN:DN + DV], ACT.Copy).then_inc(M["vcopied"], 1)

            def root(i, v, s):
                act.wait_ge(M["hv"], i + 1)
                act.activation(s, v, ACT.Sqrt).then_inc(M["root"], 1)

            kv_chunk(0)
            root(0, hvar[:, 0:2, :], hroot[:, 0:2, :])
            root(1, k_heads(hvar, 0), k_heads(hroot, 0))
            kv_chunk(1)
            root(2, k_heads(hvar, 1), k_heads(hroot, 1))
            for i in range(MH // 2):
                act.wait_ge(M["qt"], 4 + i + 1)
                act.activation(qT[:, 2 * i:2 * i + 2, :], PS[0:DQ, 4 + i % 2, :].rearrange("p (h n) -> p h n", h=2),
                               ACT.Copy, scale=q_gain[:, 0:1]).then_inc(M["qtc"], 1)

            def left_hi(b):
                act.wait_ge(M["lt"], b + 1)
                act.activation(XTh[:, 2 * b:2 * b + 2, :], psG[:, 1, :].rearrange("p (k n) -> p k n", k=2), ACT.Copy)\
                   .then_inc(M["lh"], 1)

            for h in range(MH + 2):
                if h < MH:
                    act.wait_ge(M["nm"], h + 1)
                    if h >= 2:
                        act.wait_ge(M["pt"], h - 1)
                    if h in (1, 3, 5):
                        hi_upto(act, at, N["mla_out"] + h // 2)
                    for t, sl in enumerate((slice(0, P), slice(P, TRI))):
                        act.activation(prob[:, h % 2, sl], sS[:, h % 2, sl], ACT.Exp, scale=DQ ** -0.5,
                                       bias=nmx[:, h % 2, t:t + 1], accum_out=psum_[:, t, h:h + 1]).then_inc(M["e"], 1)
                if h % 4 == 2 and h >= 6:
                    left_hi((h - 6) // 4)
                if h == 13:
                    hi_upto(act, at, N["mla_out"] + 3)
                if h == 17:
                    hi_upto(act, at, N["mla_out"] + 4)
            left_hi(3)
            hi_upto(act, at, N["mla_out"] + 5)

        def mla_dve(dve, at, own):
            nq, nk = N["cq"], N["kvr"]
            lo_upto(dve, at, nk + 1)
            dve.wait_ge(M["sq"], 2)
            dve.tensor_scalar(mvar[:, 0, :], mss[:, 0, :], 1.0 / QL, EPS, ALU.mult, ALU.add).then_inc(M["var"], 1)
            dve.wait_ge(M["r"], 1)
            for t in range(NT):
                dve.tensor_scalar(cn[:, t, 0:QL], psG[:, t, 0:QL], mrs[:, 0, t:t + 1], None, ALU.mult).then_inc(M["cn"], 1)
            dve.wait_ge(M["trig_out"], 1)
            sin, cos = trig[:, 0, :, :], trig[:, 1, :, :]
            g1, g2 = (qn_row[:, c:c + HR].unsqueeze(1).to_broadcast([P, NT, HR]) for c in (DN, DN + HR))
            for j, (a, b) in enumerate(((cos, g1), (sin, g2), (cos, g2), (sin, g1))):
                m = dve.tensor_tensor(rot[:, j, :, :], a, b, ALU.mult)
            m.then_inc(M["rope"], 1)
            lo_upto(dve, at, nk + 2)

            def c_lo(c):
                dve.wait_ge(M["ch"], min(2 * (c // 2) + 2, 3) if c < 3 else 5)
                o = (0, 1, 2, 4, 5)[c] * SEQ
                dve.scalar_tensor_tensor(out=cTl[:, c, :], in0=flatD[:, o:o + SEQ], scalar=cols[2][:, 64 + c:65 + c],
                                         in1=cTh[:, c, :].bitcast(FP32), op0=ALU.mult, op1=ALU.subtract)\
                   .then_inc(M["cl"], 1)

            for c in range(3):
                c_lo(c)
            dve.wait_ge(M["sq"], 6)
            dve.tensor_scalar(mvar[:, 1, :], mss[:, 1, :], 1.0 / KVL, EPS, ALU.mult, ALU.add)
            dve.tensor_scalar(mvar[:, 2, :], mss[:, 2, :], 1.0 / DR, EPS, ALU.mult, ALU.add).then_inc(M["var"], 1)
            dve.wait_ge(M["r"], 2)
            for t in range(NT):
                dve.tensor_scalar(cn[:, t, QL:QL + KVL], PS[:, 6 + t, 0:KVL], mrs[:, 1, t:t + 1], None, ALU.mult)\
                   .then_inc(M["cn"], 1)
            for t in range(NT):
                m = dve.scalar_tensor_tensor(out=krot[:, t, :], in0=PS[:, 6 + t, KVL:RW], scalar=mrs[:, 2, t:t + 1],
                                             in1=kn_row[:, DN:DQ], op0=ALU.mult, op1=ALU.mult)
            m.then_inc(M["krr"], 1)
            lo_upto(dve, at, N["wq"] + 1)
            for c in range(3, 5):
                c_lo(c)
            dve.wait_ge(M["krr"], 1)
            k1, k2 = krot[:, :, 0:HR], krot[:, :, HR:DR]
            for j, (a, b) in enumerate(((k1, cos), (k2, sin), (k2, cos), (k1, sin))):
                m = dve.tensor_tensor(ktmp[:, j, :, :], a, b, ALU.mult)
            own.link(m)
            dve.tensor_tensor(k1, ktmp[:, 0, :, :], ktmp[:, 1, :, :], ALU.subtract)
            own.link(dve.tensor_tensor(k2, ktmp[:, 2, :, :], ktmp[:, 3, :, :], ALU.add))
            for t in range(NT):
                dve.tensor_copy(k_nat[:, t, :, DN:DQ], krot[:, t, :].unsqueeze(1).to_broadcast([P, MH, DR]))\
                   .then_inc(M["kb"], 1)
            lo_upto(dve, at, N["wkv"] + 1)

            def rsqrt(i, v, s, r):
                dve.wait_ge(M["root"], i + 1)
                own.link(dve.reciprocal(r, s))
                own.link(dve.tensor_tensor(s, r, r, ALU.mult))
                own.link(dve.scalar_tensor_tensor(out=s, in0=s, scalar=-0.5, in1=v, op0=ALU.mult, op1=ALU.mult))
                own.link(dve.scalar_tensor_tensor(out=r, in0=s, scalar=1.5, in1=r, op0=ALU.add, op1=ALU.mult))

            def k_sums(c):
                for t in range(NT):
                    dve.wait_ge(M["sqk"], NT * c + t + 1)
                    m = dve.tensor_reduce(out=k_heads(hss, c)[:, t, :], in_=sq_k[t], axis=AX.X, op=ALU.add)
                own.link(m)
                dve.tensor_scalar(k_heads(hvar, c), k_heads(hss, c), 1.0 / DN, EPS, ALU.mult, ALU.add).then_inc(M["hv"], 1)

            def k_norm(c):
                rsqrt(1 + c, k_heads(hvar, c), k_heads(hroot, c), k_heads(hrs, c))
                dve.wait_ge(M["vcopied"], NT * (c + 1))
                for t in range(NT):
                    b = KV_BANKS[c][2 * t]
                    v = PS[:, b:b + 2, :].rearrange("p b (h e) -> p (b h) e", e=DN + DV)
                    m = dve.tensor_tensor(k_nat[:, t, 8 * c:8 * c + 8, 0:DN], v[:, :, 0:DN],
                                          k_heads(hrs, c)[:, t, :].unsqueeze(2).to_broadcast([P, 8, DN]), ALU.mult)
                m.then_inc(M["kn"], 1)

            dve.wait_ge(M["sqq"], 1)
            dve.tensor_reduce(out=hss[:, 0, :].rearrange("p (t h) -> p t h", t=NT), in_=sq_nope, axis=AX.X, op=ALU.add)
            dve.wait_ge(M["sqq"], 2)
            own.link(dve.tensor_reduce(out=hss[:, 1, :].rearrange("p (t h) -> p t h", t=NT), in_=sq_rope, axis=AX.X,
                                       op=ALU.add))
            dve.tensor_scalar(hvar[:, 0, :], hss[:, 0, :], 1.0 / DN, EPS, ALU.mult, ALU.add)
            dve.tensor_scalar(hvar[:, 1, :], hss[:, 1, :], 1.0 / DR, EPS, ALU.mult, ALU.add).then_inc(M["hv"], 1)
            k_sums(0)
            rsqrt(0, hvar[:, 0:2, :], hroot[:, 0:2, :], hrs[:, 0:2, :])
            qh = q_nat[:, :, :, :].rearrange("p t h d -> p (t h) d")
            dve.tensor_tensor(qh[:, :, 0:DN], qh[:, :, 0:DN], hrs[:, 0, :].unsqueeze(2).to_broadcast([P, NT * MH, DN]),
                              ALU.mult).then_inc(M["qn"], 1)
            k_norm(0)
            dve.wait_ge(M["rope"], 1 + NT)
            dve.tensor_tensor(qh[:, :, DN:DQ], qh[:, :, DN:DQ], hrs[:, 1, :].unsqueeze(2).to_broadcast([P, NT * MH, DR]),
                              ALU.mult).then_inc(M["qn"], 1)

            def turned_k(i, n):
                dve.wait_ge(M["qt"], n)
                dve.tensor_copy(kT[:, 2 * i:2 * i + 2, :], PS[0:DQ, 2 + i % 2, :].rearrange("p (h n) -> p h n", h=2))\
                   .then_inc(M["ktc"], 1)

            k_sums(1)
            for i in range(4):
                turned_k(i, i + 1)
            k_norm(1)
            for i in range(4, 8):
                turned_k(i, 8 + i + 1)

            def left_lo(b):
                dve.wait_ge(M["lh"], b + 1)
                dve.tensor_tensor(XTl[:, 2 * b:2 * b + 2, :], psG[:, 1, :].rearrange("p (k n) -> p k n", k=2),
                                  XTh[:, 2 * b:2 * b + 2, :].bitcast(FP32), ALU.subtract).then_inc(M["ll"], 1)

            for h in range(MH + 2):
                if h < MH:
                    dve.wait_ge(M["s"], h + 1)
                    if h >= 2:
                        dve.wait_ge(M["e"], 2 * h - 2)
                    for t, sl in enumerate((slice(0, P), slice(P, TRI))):
                        m = dve.tensor_tensor_reduce(out=sS[:, h % 2, sl], in0=psG[:, scores_bank(h), sl], in1=notyet[:, sl],
                                                     scale=1.0, scalar=-3.0e38, op0=ALU.add, op1=ALU.max,
                                                     accum_out=mx[:, h % 2, t:t + 1])
                    own.link(m)
                    dve.tensor_scalar(nmx[:, h % 2, :], mx[:, h % 2, :], -DQ ** -0.5, None, ALU.mult).then_inc(M["nm"], 1)
                if 1 <= h <= MH:
                    g = h - 1
                    dve.wait_ge(M["pt"], g + 1)
                    if g >= 2:
                        dve.wait_ge(M["o"], g - 1)
                    dve.tensor_copy(probT[:, g % 2, :], psT[:, 0:TRI]).then_inc(M["ptc"], 1)
                if h >= 2 and (h - 2) % 4 == 3:
                    g = (h - 2) // 4
                    hs = slice(4 * g, 4 * g + 4)
                    own.link(dve.reciprocal(rsum[:, :, hs], psum_[:, :, hs]))
                    dve.wait_ge(M["o"], 4 * g + 4)
                    dve.tensor_tensor(xn[:, :, g * 256:(g + 1) * 256].rearrange("p t (h d) -> p t h d", h=4),
                                      psS.rearrange("p (t h d) -> p t h d", t=NT, h=4),
                                      rsum[:, :, hs].unsqueeze(3).to_broadcast([P, NT, 4, DV]), ALU.mult)\
                       .then_inc(M["od"], 1)
                if h in (1, 3, 5):
                    lo_upto(dve, at, N["mla_out"] + h // 2)
                if h % 4 == 3 and h >= 7:
                    left_lo((h - 7) // 4)
                if h == 14:
                    lo_upto(dve, at, N["mla_out"] + 3)
                if h == 17:
                    lo_upto(dve, at, N["mla_out"] + 4)
            left_lo(3)
            lo_upto(dve, at, N["mla_out"] + 5)

        def mla_pool(pool, own):
            half = neghalf[:, 0:1]
            pool.wait_ge(M["var"], 1)
            pool.tensor_tensor(mrs[:, 0, :], mvar[:, 0, :], neghalf[:, 0:NT], ALU.pow).then_inc(M["r"], 1)
            pool.wait_ge(M["var"], 2)
            pool.tensor_tensor(mrs[:, 1:3, :], mvar[:, 1:3, :], half.unsqueeze(2).to_broadcast([P, 2, NT]), ALU.pow)\
                .then_inc(M["r"], 1)
            pool.wait_ge(M["qcopied"], 3)
            pool.wait_ge(M["sqq"], 2)
            pool.wait_ge(M["rope"], 1)
            for t in range(NT):
                q1, q2 = q_nat[:, t, :, DN:DN + HR], q_nat[:, t, :, DN + HR:DQ]
                for j, a in enumerate((q1, q2, q2, q1)):
                    m = pool.tensor_tensor(rtmp[:, t, j, :, :], a, rot[:, j, t, :].unsqueeze(1).to_broadcast([P, MH, HR]),
                                           ALU.mult)
                own.link(m)
                pool.tensor_tensor(q1, rtmp[:, t, 0, :, :], rtmp[:, t, 1, :, :], ALU.subtract)
                pool.tensor_tensor(q2, rtmp[:, t, 2, :, :], rtmp[:, t, 3, :, :], ALU.add).then_inc(M["rope"], 1)

        b2 = ExitStack()
        QK = sb("QK", [P, 2 * KD, SEQ], where=b2)
        V = sb("V", [P, NT, LH * LDV], where=b2)
        Y = sb("Y", [P, NT, DM], where=b2)
        GT = sb("GT", [P, NT, DM], where=b2)
        HTh = sb("HTh", [P, KD, SEQ], FP32R, where=b2)
        HTl = sb("HTl", [P, KD, SEQ], FP32R, where=b2)
        gain_row = sb("gain_row", [P, DM], where=b2)
        lam_row = sb("lam_row", [P, 4, DHD], where=b2)
        sub_row = sb("sub_row", [P, 2 * DHD], where=b2)
        gbias = sb("gbias", [LH, 2], where=b2)
        lcol = sb("lcol", [P, 2, NT, LH], where=b2)
        lsum = sb("lsum", [P, 2], where=b2)
        neglam = sb("neglam", [P, 1], where=b2)
        oss = sb("oss", [P, 16, NT], where=b2)
        ovar = sb("ovar", [P, 16, NT], where=b2)
        ors = sb("ors", [P, 16, NT], where=b2)
        den = sb("den", [P, 3, NT], where=b2)
        dmx = sb("dmx", [P, 2, NT, 2], where=b2)
        dnm = sb("dnm", [P, 2, NT, 2], where=b2)
        dsum = sb("dsum", [P, 2, NT, 2], where=b2)
        zss = sb("zss", [P, NT, 2], where=b2)
        zvar = sb("zvar", [P, NT, 2], where=b2)
        with ExitStack() as sub:
            gate_w = sb("gate_w", [P, TRI], where=sub)
            W = sb("W", [P, TRI], where=sub)
            rdec = sb("rdec", [P, LH, TRI], where=sub)
        with ExitStack() as sub:
            dist = sb("dist", [P, TRI], where=sub)
            U = sb("U", [P, 2, 2, TRI], where=sub)
            AW = sb("AW", [P, TRI], where=sub)
            AWT = sb("AWT", [P, TRI], where=sub)
        b2.close()
        grow = Y[0:LH, :, :].rearrange("p t (r n) -> p (t r) n", n=SEQ)
        G_F, G_E, G_LN, G_D, G_Q, G_I, G_B, G_CM = range(8)
        B = sems("b2", "in x0 e gr gcolt gcol acc tap silu cp gev vone hs yv fcp s seg w wm W o sq var r h "
                       "lt lh ll dm nm de aw at atc ssq lam dtab rtab zsq zvar zr half")

        def chunk(pe, n, pair):
            banks = [psD[:, 2 * pair + t, :] for t in range(NT)]
            mul_rows(pe, n, 0, 0, 4, 512, banks, True, False)
            mul_rows(pe, n + 1, 0, 4, 4, 512, banks, False, True)

        def half_chunk(pe, n0, k, wait):
            pair, h = k // 2, k % 2
            if h == 0:
                pe.wait_ge(*wait(pair))
            mul_rows(pe, n0 + k, 0, 4 * h, 4, 512, [psD[:, 2 * pair + t, :] for t in range(NT)], h == 0, h == 1)

        def scores_T(pe, h):
            for k in range(2):
                pe.matmul(psG[:, 0, 0:SEQ], QK[:, KD + 2 * h + k, 0:P], QK[:, 2 * h + k, :], start=(k == 0), stop=(k == 1))
            for k in range(2):
                m = pe.matmul(psG[:, 0, SEQ:TRI], QK[:, KD + 2 * h + k, P:SEQ], QK[:, 2 * h + k, P:SEQ],
                              start=(k == 0), stop=(k == 1))
            return m

        def values_T(pe, h, width):
            v = V[:, :, h * width:(h + 1) * width]
            pe.matmul(PS[:, 6, 0:width], W[:, 0:P], v[:, 0, :], start=True, stop=True)
            pe.matmul(PS[:, 7, 0:width], W[:, P:2 * P], v[:, 0, :], start=True, stop=False)
            return pe.matmul(PS[:, 7, 0:width], W[:, 2 * P:TRI], v[:, 1, :], start=False, stop=True)

        def b2_pe(pe):
            pe_n = N["if"]
            mul_first_features(pe, N["mqk0"], 6)
            mul_narrow(pe, pe_n, [(psT[0:LH, 0:SEQ], 0, LH), (psS[0:LH, 0:SEQ], LH, LH)])
            for i in range(8):
                if i >= 4:
                    pe.wait_ge(B["tap"], i - 3)
                if i:
                    mul_features(pe, N["mqk"] + i, psD[:, i % 4, :])
                if i == 7:
                    pe.wait_ge(B["gr"], 1)
                    pe.wait_ge(B["e"], 3)
                    for k, r in enumerate((G_D, G_LN)):
                        for t in range(NT):
                            c = (k * NT + t) * LH
                            m = pe.transpose(psS[:, c:c + LH], grow[:, r, t * P:(t + 1) * P], ident[0:LH, 0:LH])
                    m.then_inc(B["gcolt"], 1)
            for c in range(2):
                pe.wait_ge(B["tap"], 6 + 2 * c)
                chunk(pe, N["mv"] + 2 * c, c)
            pe.wait_ge(B["silu"], 8)
            pe.wait_ge(B["gcol"], 1)
            for h in range(LH):
                if h:
                    pe.wait_ge(B["W"], h)
                pe.matmul(psG[:, 1, 0:SEQ], ident[0:LH, h:h + 1].to_broadcast([LH, P]), grow[:, G_CM, :],
                          start=True, stop=True)
                scores_T(pe, h).then_inc(B["s"], 1)
                half_chunk(pe, N["mo"], h, lambda q: (B["cp"], q + 1))
                pe.wait_ge(B["W"], h + 1)
                pe.wait_ge(B["cp"], 2)
                pe.wait_ge(B["vone"], 1)
                if h:
                    pe.wait_ge(B["h"], h)
                values_T(pe, h, LDV).then_inc(B["o"], 1)
            for c in range(2):
                pe.wait_ge(B["gev"], 1 + c)
                chunk(pe, N["gm"] + 2 * c, c)
            left_pe(pe, B, xn, lambda b: (B["hs"], b // 2 + 1))
            pe.wait_ge(B["gev"], 4)
            project_pe(pe, B, N["mlstm_out"], HTh, HTl)

            for i in range(8):
                if i == 4:
                    pe.wait_ge(B["yv"], 1)
                mul_features(pe, N["dqk"] + i, PS[:, (4 + i) % 8, :])
            def diff_scores(h):
                if h:
                    pe.wait_ge(B["dm"], h)
                for c in range(2):
                    ps = slice(c * DHD, (c + 1) * DHD)
                    pe.matmul(psG[:, c, 0:P], QK[ps, h, 0:P], QK[ps, KD + h, 0:P], start=True, stop=True)
                    m = pe.matmul(psG[:, c, P:TRI], QK[ps, h, P:SEQ], QK[ps, KD + h, :], start=True, stop=True)
                m.then_inc(B["ssq"], 1)

            for c in range(2):
                pe.wait_ge(B["fcp"], 6 + 2 * c)
                chunk(pe, N["dv"] + 2 * c, c)
                if c == 0:
                    pe.wait_ge(B["fcp"], 8)
                    diff_scores(0)
            pe.wait_ge(B["cp"], 4)
            for h in range(DH + 2):
                if h < DH:
                    if h:
                        diff_scores(h)
                    q, b, part = h // 4, h // 2, range(2 * (h % 2), 2 * (h % 2) + 2)
                    if h % 4 == 0:
                        pe.wait_ge(B["cp"], 3 + q)
                    mul_rows(pe, N["gd"] + b, 0, 4 * (b % 2), 4, 512, [psD[:, 2 * q + t, :] for t in range(NT)],
                             b % 2 == 0, b % 2 == 1, part=part)
                if h >= 2:
                    g = h - 2
                    pe.wait_ge(B["atc"], g + 1)
                    if g:
                        pe.wait_ge(B["h"], LH + g)
                    v = V[:, :, g * 2 * DHD:(g + 1) * 2 * DHD]
                    pe.matmul(psS[:, 0:P], AWT[:, 0:P], v[:, 0, :], start=True, stop=True)
                    pe.matmul(psS[:, P:2 * P], AWT[:, P:2 * P], v[:, 0, :], start=True, stop=False)
                    pe.matmul(psS[:, P:2 * P], AWT[:, 2 * P:TRI], v[:, 1, :], start=False, stop=True).then_inc(B["o"], 1)
                if 1 <= h <= DH:
                    pe.wait_ge(B["aw"], h)
                    for c in range(3):
                        m = pe.transpose(psT[:, c * P:(c + 1) * P], AW[:, c * P:(c + 1) * P], ident[:, :])
                    m.then_inc(B["at"], 1)
            left_pe(pe, B, xn, lambda b: (B["h"], LH + 2 * b + 2))
            pe.wait_ge(B["gev"], 6)
            project_pe(pe, B, N["diff_out"], HTh, HTl, 4)

            for i in range(8):
                if i == 4:
                    pe.wait_ge(B["yv"], 2)
                mul_features(pe, N["rqk"] + i, PS[:, (4 + i) % 8, :])
            for c in range(2):
                pe.wait_ge(B["fcp"], 14 + 2 * c)
                chunk(pe, N["rv"] + 2 * c, c)
            pe.wait_ge(B["fcp"], 16)
            pe.wait_ge(B["cp"], 6)
            for h in range(LH):
                if h:
                    pe.wait_ge(B["W"], LH + h)
                scores_T(pe, h).then_inc(B["s"], 1)
                half_chunk(pe, N["rg"], h, lambda q: (B["cp"], 5 + q))
                pe.wait_ge(B["W"], LH + h + 1)
                if h:
                    pe.wait_ge(B["h"], LH + DH + h)
                values_T(pe, h, LD).then_inc(B["o"], 1)
            for c in range(2):
                pe.wait_ge(B["gev"], 7 + c)
                chunk(pe, N["gr"] + 2 * c, c)
            left_pe(pe, B, xn, lambda b: (B["hs"], 2 + b // 2 + 1))
            pe.wait_ge(B["gev"], 10)
            project_pe(pe, B, N["ret_out"], HTh, HTl, 8, by_half=B["half"])
            left_pe(pe, B, Y, lambda b: (B["yv"], 3 + b // 2))
            project_pe(pe, B, N["y_out"], HTh, HTl, 12, by_tile=True)

        def b2_taps(ct, j):
            return cols[2][:, j * 2 * KD + ct:j * 2 * KD + ct + 1]

        def values_act(act, at, n, dst):
            for c in range(2):
                hi_upto(act, at, n + 2 * c + 3)
                act.wait_ge(block_used, n + 2 * c + 2)
                act.activation(dst(c), PS[:, 2 * c:2 * c + 2, :] if dst(c).shape[-1] == 512 else
                               PS[:, 2 * c:2 * c + 2, :].rearrange("p t (h n) -> p t h n", h=2), ACT.Copy)\
                   .then_inc(B["cp"], 1)

        def gate_act(act, at, n, c, func, free):
            hi_upto(act, at, n + 2 * c + 3)
            act.wait_ge(block_used, n + 2 * c + 2)
            if free is not None:
                act.wait_ge(*free)
            act.activation(GT[:, :, c * 512:(c + 1) * 512], PS[:, 2 * c:2 * c + 2, :], func).then_inc(B["gev"], 1)

        def squares_act(act, i, width, banks):
            act.wait_ge(B["o"], i + 1)
            for t in range(NT):
                act.activation(ff_s[:, t, 0:width], banks[t], ACT.Square, accum_out=oss[:, i, t:t + 1]).then_inc(B["sq"], 1)

        def features_act(act, at, n):
            for i in range(8):
                hi_upto(act, at, n + i + 2)
                act.wait_ge(block_used, n + i + 1)
                act.activation(QK[:, 2 * i:2 * i + 2, :], PS[:, (4 + i) % 8, :].rearrange("p (c n) -> p c n", c=2),
                               ACT.Copy)\
                   .then_inc(B["fcp"], 1)

        def b2_act(act, at):
            hi_upto(act, at, N["if"] + 2)
            n = N["mqk"]
            for i in range(9):
                hi_upto(act, at, n + i + 2)
                if i == 1:
                    act.wait_ge(B["x0"], 1)
                    act.activation(grow[:, G_E, :], grow[:, G_Q, :], ACT.Exp, scale=-1.0).then_inc(B["e"], 1)
                if i == 2:
                    act.wait_ge(B["e"], 1)
                    act.activation(grow[:, G_LN, :], grow[:, G_E, :], ACT.Ln, bias=ones[0:LH, 0:1]).then_inc(B["e"], 1)
                if i == 6:
                    act.wait_ge(B["gr"], 1)
                    act.activation(grow[:, G_LN, :], grow[:, G_Q, :], ACT.Exp, scale=-1.0).then_inc(B["e"], 1)
                    act.wait_ge(B["lam"], 1)
                    act.activation(lsum[:, :], lsum[:, :], ACT.Exp).then_inc(B["lam"], 1)
                conv_act(act, B, i, (n + i if i else N["mqk0"]) if i < 8 else None, (2 * i, 2 * i + 1), b2_taps,
                         lambda ct: 0.0, QK[:, 2 * (i - 1):2 * i, :] if i else None)
            Vh = V[:, :, :].rearrange("p t (h n) -> p t h n", n=LDV)
            values_act(act, at, N["mv"], lambda c: Vh[:, :, 2 * c:2 * c + 2, 0:LD])
            for h in range(LH):
                hi_upto(act, at, N["mo"] + h + 2)
                act.wait_ge(B["seg"], h + 1)
                act.activation(gate_w[:, :], gate_w[:, :], ACT.Exp, scale=-1.0).then_inc(B["w"], 1)
                squares_act(act, h, LD, [PS[:, 6, 0:LD], PS[:, 7, 0:LD]])
                if h % 2:
                    gate_act(act, at, N["mo"], h // 2, ACT.Sigmoid, None)
            for c in range(2):
                gate_act(act, at, N["gm"], c, ACT.Sigmoid, (B["hs"], c + 1))
            left_act(act, B, HTh)
            hi_upto(act, at, N["mlstm_out"] + 4)

            features_act(act, at, N["dqk"])
            values_act(act, at, N["dv"], lambda c: V[:, :, c * 512:(c + 1) * 512])
            for h in range(DH + 1):
                if h < DH:
                    act.wait_ge(B["nm"], h + 1)
                    for t, sl in enumerate((slice(0, P), slice(P, TRI))):
                        for c in range(2):
                            act.activation(U[:, h % 2, c, sl], U[:, h % 2, c, sl], ACT.Exp, scale=DHD ** -0.5,
                                           bias=dnm[:, h % 2, t, c:c + 1],
                                           accum_out=dsum[:, h % 2, t, c:c + 1]).then_inc(B["de"], 1)
                hi_upto(act, at, N["gd"] + min(h // 2, 3) + 2)
                if h >= 1:
                    g = h - 1
                    act.wait_ge(B["at"], g + 1)
                    if g:
                        act.wait_ge(B["o"], LH + g)
                    act.activation(AWT[:, :], psT[:, 0:TRI], ACT.Copy).then_inc(B["atc"], 1)
                if h >= 2:
                    squares_act(act, LH + h - 2, P, [psS[:, 0:P], psS[:, P:2 * P]])
            squares_act(act, LH + DH - 1, P, [psS[:, 0:P], psS[:, P:2 * P]])
            for c in range(2):
                gate_act(act, at, N["gd"], c, ACT.Sigmoid, (B["yv"], 1))
            left_act(act, B, HTh, 4)
            hi_upto(act, at, N["diff_out"] + 4)

            for h in range(LH):
                act.wait_ge(B["rtab"], 1)
                act.activation(rdec[:, h, :], gate_w[:, :], ACT.Exp,
                               scale=math.log(1.0 - 2.0 ** (-5.0 - h))).then_inc(B["rtab"], 1)
            features_act(act, at, N["rqk"])
            values_act(act, at, N["rv"], lambda c: V[:, :, c * 512:(c + 1) * 512])
            for h in range(LH):
                hi_upto(act, at, N["rg"] + h + 2)
                squares_act(act, LH + DH + h, LD, [PS[:, 6, 0:LD], PS[:, 7, 0:LD]])
                if h % 2:
                    gate_act(act, at, N["rg"], h // 2, ACT.Silu, (B["yv"], 2))
            for c in range(2):
                gate_act(act, at, N["gr"], c, ACT.Sigmoid, (B["hs"], 2 + c + 1))
            left_act(act, B, HTh, 8)
            hi_upto(act, at, N["ret_out"] + 4)
            left_act(act, B, HTh, 12)
            hi_upto(act, at, N["y_out"] + 5)
            post_act(act, 6, N["y_out"] + 4)

        def post_act(act, sublayer, used):
            for t in range(NT):
                if t == 0:
                    act.wait_ge(tile0_done, sublayer + 1)
                else:
                    act.wait_ge(block_used, used)
                for c in range(2):
                    act.activation(Y[:, t, c * 512:(c + 1) * 512], psD[:, 2 * t + c, :], ACT.Square,
                                   accum_out=zss[:, t, c:c + 1]).then_inc(B["zsq"], 1)

        def post_dve(dve, own, i, gain_ready):
            def add(t):
                dve.wait_ge(*gain_ready)
                for c in range(2):
                    dve.wait_ge(B["zsq"], 2 * (NT * i + t) + c + 1)
                    own.mark(dve.tensor_scalar(zvar[:, t, c:c + 1], zss[:, t, c:c + 1], 1.0 / DM, EPS / 2,
                                               ALU.mult, ALU.add))
                    if c:
                        own.wait()
                        dve.tensor_tensor(var[:, t:t + 1], zvar[:, t, 0:1], zvar[:, t, 1:2], ALU.add)\
                           .then_inc(B["zvar"], 1)
                    m = dve.tensor_tensor(xn[:, t, c * 512:(c + 1) * 512], psD[:, 2 * t + c, :],
                                          gain_row[:, c * 512:(c + 1) * 512], ALU.mult)
                own.link(m)
                dve.wait_ge(B["zr"], NT * i + t + 1)
                dve.scalar_tensor_tensor(out=xs_[:, t, :], in0=xn[:, t, :], scalar=rstd[:, t:t + 1], in1=xs_[:, t, :],
                                         op0=ALU.mult, op1=ALU.add).then_inc(x_added, 1)
            return add

        def post_pool(pool, i):
            for t in range(NT):
                pool.wait_ge(B["zvar"], NT * i + t + 1)
                pool.tensor_tensor(rstd[:, t:t + 1], var[:, t:t + 1], neghalf[:, 0:1], ALU.pow).then_inc(B["zr"], 1)

        def head_variance_dve(dve, i, width):
            dve.wait_ge(B["sq"], NT * (i + 1))
            dve.tensor_scalar(ovar[:, i, :], oss[:, i, :], 1.0 / width, EPS, ALU.mult, ALU.add).then_inc(B["var"], 1)

        def head_norm_dve(dve, own, i, width, eps_scale=None):
            if eps_scale is None:
                head_variance_dve(dve, i, width)
            else:
                dve.wait_ge(B["sq"], NT * (i + 1))
                own.link(dve.tensor_tensor(ovar[:, i, :], oss[:, i, :], eps_scale, ALU.mult))
                own.link(dve.tensor_tensor(ovar[:, i, :], ovar[:, i, :], eps_scale, ALU.mult))
                dve.tensor_scalar(ovar[:, i, :], ovar[:, i, :], 1.0 / width, EPS, ALU.mult, ALU.add).then_inc(B["var"], 1)
            dve.wait_ge(B["r"], i + 1)

        def gate_out_dve(dve, first):
            for c in range(2):
                dve.wait_ge(B["gev"], first + c)
                dve.tensor_tensor(xn[:, :, c * 512:(c + 1) * 512], xn[:, :, c * 512:(c + 1) * 512],
                                  GT[:, :, c * 512:(c + 1) * 512], ALU.mult).then_inc(B["hs"], 1)

        def b2_dve(dve, at, own):
            lo_upto(dve, at, N["if"] + 2)
            dve.wait_ge(B["in"], 80)
            Vh = V[:, :, :].rearrange("p t (h n) -> p t h n", n=LDV)
            dve.memset(Vh[:, :, :, LD:LDV], 1.0).then_inc(B["vone"], 1)

            def lambda_input():
                for k in range(2):
                    m = dve.tensor_tensor(ff_a[:, 0, k * DHD:(k + 1) * DHD], lam_row[:, 2 * k, :],
                                          lam_row[:, 2 * k + 1, :], ALU.mult)
                own.link(m)
                dve.tensor_reduce(out=lsum[:, :], in_=ff_a[:, 0, 0:2 * DHD].rearrange("p (k n) -> p k n", k=2), axis=AX.X,
                                  op=ALU.add).then_inc(B["lam"], 1)
                own.link(dve.tensor_scalar(sub_row[:, :], sub_row[:, :], 1.0 - LAM_INIT, None, ALU.mult))

            def gate_input():
                dve.wait_ge(block_used, N["if"] + 1)
                dve.tensor_scalar(grow[:, G_I, :], psT[0:LH, 0:SEQ], gbias[:, 0:1], None, ALU.add)
                own.link(dve.tensor_scalar(grow[:, G_F, :], psS[0:LH, 0:SEQ], gbias[:, 1:2], None, ALU.add))
                dve.scalar_tensor_tensor(out=grow[:, G_Q, :], in0=grow[:, G_F, :], scalar=-1.0, in1=grow[:, G_F, :],
                                         op0=ALU.mult, op1=ALU.max).then_inc(B["x0"], 1)

            def gate_quotient():
                dve.wait_ge(B["e"], 1)
                own.link(dve.tensor_scalar(grow[:, G_D, :], grow[:, G_E, :], 1.0, -1.0, ALU.add, ALU.add))
                own.link(dve.tensor_scalar(grow[:, G_Q, :], grow[:, G_D, :], 1e-30, None, ALU.max))
                own.link(dve.reciprocal(grow[:, G_Q, :], grow[:, G_Q, :]))
                own.link(dve.tensor_tensor(grow[:, G_Q, :], grow[:, G_Q, :], grow[:, G_E, :], ALU.mult))

            def gate_value():
                dve.wait_ge(B["e"], 2)
                own.link(dve.tensor_tensor(grow[:, G_Q, :], grow[:, G_Q, :], grow[:, G_LN, :], ALU.mult))
                own.link(dve.scalar_tensor_tensor(out=grow[:, G_D, :], in0=grow[:, G_D, :], scalar=0.0,
                                                  in1=grow[:, G_E, :], op0=ALU.is_equal, op1=ALU.mult))
                own.link(dve.tensor_tensor(grow[:, G_Q, :], grow[:, G_Q, :], grow[:, G_D, :], ALU.add))
                own.link(dve.scalar_tensor_tensor(out=grow[:, G_F, :], in0=grow[:, G_F, :], scalar=0.0,
                                                  in1=grow[:, G_Q, :], op0=ALU.min, op1=ALU.subtract))

            def gate_sums():
                own.link(dve.tensor_tensor_scan(out=grow[:, G_B, :], data0=ones[0:LH, :], data1=grow[:, G_F, :],
                                                initial=0.0, op0=ALU.mult, op1=ALU.add))
                own.link(dve.tensor_tensor(grow[:, G_D, :], grow[:, G_I, :], grow[:, G_B, :], ALU.subtract))
                own.link(dve.tensor_tensor_scan(out=grow[:, G_CM, :], data0=grow[:, G_D, :], data1=grow[:, G_D, :],
                                                initial=0.0, op0=ALU.max, op1=ALU.max))
                dve.tensor_tensor(grow[:, G_Q, :], grow[:, G_B, :], grow[:, G_CM, :], ALU.add).then_inc(B["gr"], 1)

            gate_input()
            for i in range(8):
                lo_upto(dve, at, N["mqk"] + i + 2)
                conv_dve(dve, own, B, i, (2 * i, 2 * i + 1), b2_taps)
                if i == 1:
                    gate_quotient()
                if i == 2:
                    gate_value()
                if i == 3:
                    gate_sums()
                if i == 4:
                    lambda_input()
            dve.wait_ge(B["gcolt"], 1)
            dve.tensor_copy(lcol[:, :, :, :].rearrange("p k t h -> p (k t h)"), psS[:, 0:4 * LH])\
               .then_inc(B["gcol"], 1)
            lo_upto(dve, at, N["mv"] + 5)
            dve.wait_ge(B["gcol"], 1)
            for h in range(LH):
                lo_upto(dve, at, N["mo"] + h + 1)
                dve.wait_ge(B["s"], h + 1)
                if h:
                    dve.wait_ge(B["W"], h)
                for t, (sl, c0) in enumerate(((slice(0, SEQ), 0), (slice(SEQ, TRI), P))):
                    m = dve.tensor_scalar(gate_w[:, sl], psG[:, 1, c0:SEQ], lcol[:, 0, t, h:h + 1], 0.0,
                                          ALU.subtract, ALU.max)
                m.then_inc(B["seg"], 1)
                lo_upto(dve, at, N["mo"] + h + 2)
                dve.wait_ge(B["wm"], h + 1)
                if h:
                    dve.wait_ge(B["o"], h)
                dve.scalar_tensor_tensor(out=W[:, :], in0=psG[:, 0, 0:TRI], scalar=LD ** -0.5, in1=gate_w[:, :],
                                         op0=ALU.mult, op1=ALU.mult).then_inc(B["W"], 1)
                dve.wait_ge(B["sq"], NT * (h + 1))
                own.link(dve.tensor_copy(den[:, 0, :], PS[:, 6:8, LD]))
                own.link(dve.scalar_tensor_tensor(out=den[:, 1, :], in0=den[:, 0, :], scalar=-1.0, in1=den[:, 0, :],
                                                  op0=ALU.mult, op1=ALU.max))
                own.link(dve.tensor_tensor(den[:, 1, :], den[:, 1, :], lcol[:, 1, :, h], ALU.max))
                own.link(dve.reciprocal(den[:, 2, :], den[:, 1, :]))
                head_norm_dve(dve, own, h, LD, den[:, 2, :])
                own.link(dve.tensor_tensor(den[:, 2, :], den[:, 2, :], ors[:, h, :], ALU.mult))
                for t in range(NT):
                    m = dve.tensor_scalar(xn[:, t, h * LD:(h + 1) * LD], PS[:, 6 + t, 0:LD], den[:, 2, t:t + 1], None,
                                          ALU.mult)
                m.then_inc(B["h"], 1)
            dve.wait_ge(B["h"], LH)
            gate_out_dve(dve, 1)
            lo_upto(dve, at, N["mlstm_out"] + 1)
            left_dve(dve, B, HTh, HTl)
            lo_upto(dve, at, N["mlstm_out"] + 4)
            dve.wait_ge(block_used, N["mlstm_out"] + 4)
            dve.wait_ge(B["gev"], 4)
            dve.tensor_tensor(Y[:, :, :].rearrange("p t n -> p (t n)"), flatD, GT[:, :, :].rearrange("p t n -> p (t n)"),
                              ALU.mult).then_inc(B["yv"], 1)

            dve.wait_ge(B["dtab"], 2)
            own.link(dve.scalar_tensor_tensor(out=dist[:, :], in0=dist[:, :], scalar=-1.0, in1=dist[:, :],
                                              op0=ALU.mult, op1=ALU.max))
            dve.memset(dist[0:64, 64:P], BIG)
            own.link(dve.memset(dist[0:64, P + 192:TRI], BIG))
            dve.wait_ge(B["lam"], 2)
            own.link(dve.tensor_tensor(neglam[:, :], lsum[:, 1:2], lsum[:, 0:1], ALU.subtract))
            own.link(dve.tensor_scalar(neglam[:, :], neglam[:, :], -LAM_INIT, None, ALU.add))
            lo_upto(dve, at, N["dv"] + 5)
            for h in range(DH + 3):
                if h >= 3:
                    head_variance_dve(dve, LH + h - 3, P)
                if h < DH:
                    slope = 2.0 ** (-8.0 * (h + 1.0) / DH)
                    dve.wait_ge(B["ssq"], h + 1)
                    if h >= 2:
                        dve.wait_ge(B["aw"], h - 1)
                    own.mark(dve.scalar_tensor_tensor(out=U[:, h % 2, :, :],
                                                      in0=dist[:, :].unsqueeze(1).to_broadcast([P, 2, TRI]),
                                                      scalar=-slope * DHD ** 0.5, in1=psG[:, :, 0:TRI],
                                                      op0=ALU.mult, op1=ALU.add))
                if h >= 3:
                    g = h - 3
                    dve.wait_ge(B["r"], LH + g + 1)
                    for t in range(NT):
                        m = dve.scalar_tensor_tensor(out=xn[:, t, g * P:(g + 1) * P], in0=psS[:, t * P:(t + 1) * P],
                                                     scalar=ors[:, LH + g, t:t + 1], in1=sub_row[:, :],
                                                     op0=ALU.mult, op1=ALU.mult)
                    m.then_inc(B["h"], 1)
                if h < DH:
                    own.wait()
                    dve.tensor_reduce(out=dmx[:, h % 2, 0, :], in_=U[:, h % 2, :, 0:P], axis=AX.X, op=ALU.max)\
                       .then_inc(B["dm"], 1)
                    own.link(dve.tensor_reduce(out=dmx[:, h % 2, 1, :], in_=U[:, h % 2, :, P:TRI], axis=AX.X, op=ALU.max))
                    dve.wait_ge(B["dm"], h + 1)
                    dve.tensor_scalar(dnm[:, h % 2, :, :], dmx[:, h % 2, :, :], -DHD ** -0.5, None, ALU.mult)\
                       .then_inc(B["nm"], 1)
                if 1 <= h <= DH:
                    g, u = h - 1, (h - 1) % 2
                    dve.wait_ge(B["de"], 4 * g + 4)
                    own.link(dve.reciprocal(dsum[:, u, :, :], dsum[:, u, :, :]))
                    own.link(dve.tensor_scalar(dsum[:, u, :, 1], dsum[:, u, :, 1], neglam[:, 0:1], None, ALU.mult))
                    if g:
                        dve.wait_ge(B["at"], g)
                    for t, sl in enumerate((slice(0, P), slice(P, TRI))):
                        m = dve.tensor_scalar(AW[:, sl], U[:, u, 0, sl], dsum[:, u, t, 0:1], None, ALU.mult)
                    own.link(m)
                    for t, sl in enumerate((slice(0, P), slice(P, TRI))):
                        m = dve.scalar_tensor_tensor(out=AW[:, sl], in0=U[:, u, 1, sl], scalar=dsum[:, u, t, 1:2],
                                                     in1=AW[:, sl], op0=ALU.mult, op1=ALU.add)
                    m.then_inc(B["aw"], 1)
                lo_upto(dve, at, N["gd"] + min((h - 1) // 2, 3) + 2)
            lo_upto(dve, at, N["diff_out"] + 1)
            left_dve(dve, B, HTh, HTl, 4)
            lo_upto(dve, at, N["diff_out"] + 4)
            add_gated(dve, own, N["diff_out"] + 4, 6)

            lo_upto(dve, at, N["rv"] + 1)
            dve.wait_ge(B["rtab"], LH + 1)
            own.link(dve.scalar_tensor_tensor(out=rdec[:, :, :], in0=rdec[:, :, :], scalar=LD ** -0.5,
                                              in1=causal[:, :].unsqueeze(1).to_broadcast([P, LH, TRI]),
                                              op0=ALU.mult, op1=ALU.mult))
            lo_upto(dve, at, N["rv"] + 5)
            for h in range(LH):
                lo_upto(dve, at, N["rg"] + h + 2)
                dve.wait_ge(B["s"], LH + h + 1)
                if h:
                    dve.wait_ge(B["o"], LH + DH + h)
                dve.tensor_tensor(W[:, :], psG[:, 0, 0:TRI], rdec[:, h, :], ALU.mult).then_inc(B["W"], 1)
                head_norm_dve(dve, own, LH + DH + h, LD)
                for t in range(NT):
                    m = dve.tensor_scalar(xn[:, t, h * LD:(h + 1) * LD], PS[:, 6 + t, 0:LD],
                                          ors[:, LH + DH + h, t:t + 1], None, ALU.mult)
                m.then_inc(B["h"], 1)
            dve.wait_ge(B["h"], 2 * LH + DH)
            gate_out_dve(dve, 7)
            lo_upto(dve, at, N["ret_out"] + 1)
            left_dve(dve, B, HTh, HTl, 8)
            lo_upto(dve, at, N["ret_out"] + 4)
            dve.wait_ge(B["gev"], 10)
            for c, done in enumerate(((B["half"], 1), (block_used, N["ret_out"] + 4))):
                dve.wait_ge(*done)
                sl = slice(c * 512, (c + 1) * 512)
                for t in range(NT):
                    m = dve.tensor_tensor(GT[:, t, sl], psD[:, 2 * t + c, :], GT[:, t, sl], ALU.mult)
                own.link(m)
                dve.tensor_tensor(Y[:, :, sl], Y[:, :, sl], GT[:, :, sl], ALU.add).then_inc(B["yv"], 1)
            left_dve(dve, B, HTh, HTl, 12)
            lo_upto(dve, at, N["y_out"] + 5)

        def add_gated(dve, own, used, gev):
            dve.wait_ge(block_used, used)
            dve.wait_ge(B["gev"], gev)
            own.link(dve.tensor_tensor(GT[:, :, :].rearrange("p t n -> p (t n)"), flatD,
                                       GT[:, :, :].rearrange("p t n -> p (t n)"), ALU.mult))
            dve.tensor_tensor(Y[:, :, :], Y[:, :, :], GT[:, :, :], ALU.add).then_inc(B["yv"], 1)

        def b2_pool(pool, own):
            for h in range(LH):
                pool.wait_ge(B["w"], h + 1)
                pool.tensor_tensor(gate_w[:, :], gate_w[:, :], causal[:, :], ALU.mult).then_inc(B["wm"], 1)
                pool.wait_ge(B["var"], h + 1)
                pool.tensor_tensor(ors[:, h, :], ovar[:, h, :], neghalf[:, 0:NT], ALU.pow).then_inc(B["r"], 1)
            pool.wait_ge(B["o"], LH)
            pool.iota(dist[:, 0:P], [[-1, P]], base=0, channel_multiplier=1, allow_small_or_imprecise_dtypes=True)\
                .then_inc(B["dtab"], 1)
            pool.iota(dist[:, P:TRI], [[-1, SEQ]], base=P, channel_multiplier=1, allow_small_or_imprecise_dtypes=True)\
                .then_inc(B["dtab"], 1)
            for g in range(DH):
                i = LH + g
                pool.wait_ge(B["var"], i + 1)
                pool.tensor_tensor(ors[:, i, :], ovar[:, i, :], neghalf[:, 0:NT], ALU.pow).then_inc(B["r"], 1)
            pool.wait_ge(B["h"], LH + DH)
            own.mark(pool.iota(gate_w[:, 0:SEQ], [[1, SEQ]], base=0, channel_multiplier=-1,
                               allow_small_or_imprecise_dtypes=True))
            own.link(pool.iota(gate_w[:, SEQ:TRI], [[1, P]], base=0, channel_multiplier=-1,
                               allow_small_or_imprecise_dtypes=True))
            pool.tensor_scalar(gate_w[:, :], gate_w[:, :], 0.0, None, ALU.max).then_inc(B["rtab"], 1)
            for h in range(LH):
                i = LH + DH + h
                pool.wait_ge(B["var"], i + 1)
                pool.tensor_tensor(ors[:, i, :], ovar[:, i, :], neghalf[:, 0:NT], ALU.pow).then_inc(B["r"], 1)
            post_pool(pool, 0)

        block = ctx.enter_context(nc.Block())

        @block.sync
        def _(sp):
            def stream(lo, hi):
                for n in range(lo, hi):
                    load_block(sp, blocks[n], n)

            def ffn_stream(i):
                wg, wu, wd = FFN_W[i]
                n0, cu = N[f"ffn{i}"], (FF if i == 4 else 0)

                with sp.Fori(0, NFF - 2) as j:
                    load_block(sp, rows_block(wu, 0, KD, j * FCH + (cu + FCH), FCH), n0 + 3, j)
                    load_block(sp, down_block(wd, j), n0 + 4, j)
                    load_block(sp, rows_block(wg, 0, KD, j * FCH + 2 * FCH, FCH), n0 + 5, j)
                stream(n0 + 3 * NFF - 3, n0 + 3 * NFF)

            for t in range(NT):
                sp.dma_start(xs_[:, t, :], x[0, t * P:(t + 1) * P, :]).then_inc(x_in[t], 16)
            stream(0, 1)
            for src, r, at in NROW:
                sp.dma_start(rows[r][at:at + src.shape[0], :], src).then_inc(s_rows, 16)
            stream(1, 3)
            sp.dma_start(dtb[:, :], ssm_dt_bias.rearrange("i h -> h i")).then_inc(A["in"], 16)
            sp.dma_start(alog[:, :], ssm_a_log.rearrange("i h -> h i")).then_inc(A["in"], 16)
            sp.dma_start(dskip[:, :], ssm_d[0:1, :].to_broadcast([P, SSM_HEADS])).then_inc(A["in"], 16)
            sp.dma_start(posi[:, :], positions.rearrange("b (t p) -> p (b t)", p=P)).then_inc(M["in"], 16)
            sp.dma_start(qn_row[:, :], mla_q_norm[0:1, :].to_broadcast([P, DQ])).then_inc(M["in"], 16)
            sp.dma_start(kn_row[:, :], mla_k_norm[0:1, :].to_broadcast([P, DQ])).then_inc(M["in"], 16)
            sp.dma_start(k_gain[:, :], mla_k_norm[0:1, 0:DN].rearrange("i d -> d i")).then_inc(M["in"], 16)
            sp.wait_ge(M["gain1"], 1)
            sp.dma_start(q_gain[0:DN, :], mla_q_norm[0:1, 0:DN].rearrange("i d -> d i")).then_inc(M["in"], 16)
            ffn_stream(0)
            stream(N["bc0"], N["ssm_out"] + 8)
            stream(N["ffn1"], N["ffn1"] + 3)
            ffn_stream(1)
            stream(N["ffn2"], N["ffn2"] + 3)
            ffn_stream(2)
            stream(N["cq"], N["mla_out"] + 4)
            stream(N["ffn3"], N["ffn3"] + 3)
            ffn_stream(3)
            sp.wait_ge(x_added, 5 * NT)
            for dst, src in ((gain_row[:, :], norm_gains_2[0, 1:2, :].to_broadcast([P, DM])),
                             (lam_row[:, :, :].rearrange("p k n -> p (k n)"),
                              diff_lambda_2.rearrange("i k n -> i (k n)").to_broadcast([P, 4 * DHD])),
                             (sub_row[:, :], diff_subln_2[0:1, :].to_broadcast([P, 2 * DHD])),
                             (gbias[:, 0:1], mlstm_gate_bias_2[0, 0:1, :].rearrange("k h -> h k")),
                             (gbias[:, 1:2], mlstm_gate_bias_2[0, 1:2, :].rearrange("k h -> h k"))):
                sp.dma_start(dst, src).then_inc(B["in"], 16)
            stream(N["mqk0"], N["ffn4"] + 2)
            sp.wait_ge(x_added, 7 * NT)
            sp.dma_start(gain_row[:, :], norm_gains_2[0, 3:4, :].to_broadcast([P, DM])).then_inc(B["in"], 16)
            stream(N["ffn4"] + 2, N["ffn4"] + 3)
            ffn_stream(4)
            for t in range(NT):
                sp.wait_ge(x_added, NT * 7 + t + 1)
                sp.dma_start(out[0, t * P:(t + 1) * P, :], xs_[:, t, :]).then_inc(s_out, 16)
            sp.wait_ge(s_out, 16 * NT)

        @block.gpsimd
        def _(pool):
            own = Chain(pool, pool_own)
            own.mark(pool.memset(ident[:, :], 0.0))
            own.mark(pool.memset(causal[:, :], 1.0))
            pool.memset(neghalf[:, :], -0.5)
            pool.memset(ones[:, :], 1.0).then_inc(s_const, 1)
            own.wait()
            pool.affine_select(out=ident[:, :], in_=ident[:, :], compare_op=ALU.not_equal, fill=1.0,
                               base=0, pattern=[[-1, P]], channel_multiplier=1).then_inc(s_const, 1)
            for c in (0, 2 * P):
                pool.affine_select(out=causal[:, c:c + P], in_=causal[:, c:c + P], compare_op=ALU.is_ge,
                                   fill=0.0, base=0, pattern=[[1, P]], channel_multiplier=-1).then_inc(s_const, 1)
            mla_tables_pool(pool, own)
            norm_pool(pool, 0)
            norm_pool(pool, 1)
            ssm_pool(pool)
            norm_pool(pool, 2)
            norm_pool(pool, 3)
            norm_pool(pool, 4)
            mla_pool(pool, own)
            norm_pool(pool, 5)
            norm_pool(pool, 6)
            b2_pool(pool, own)
            norm_pool(pool, 7)
            post_pool(pool, 1)

        @block.scalar
        def _(act):
            at, own = Position(), Chain(act, act_own)
            norm_squares(act, 0)
            hi_upto(act, at, 0)
            for i in range(3):
                act.wait_ge(s_rowt, i + 1)
                act.activation(cols[i][:, 0:ROWS_IN[i]], PS[:, 2 + i, 0:ROWS_IN[i]], ACT.Copy).then_inc(s_rowc, 1)
            act.wait_ge(s_rowc, 3)
            norm_hi(act, 0, 0)
            hi_upto(act, at, 2)
            ffn_act(act, 0, at)
            norm_act(act, 1, 8)
            ssm_act(act, at)
            norm_act(act, 2, 16)
            ffn_act(act, 1, at)
            norm_act(act, 3, 24)
            ffn_act(act, 2, at)
            norm_act(act, 4, 32)
            mla_act(act, at)
            norm_act(act, 5, 40)
            ffn_act(act, 3, at)
            norm_act(act, 6, 48)
            b2_act(act, at)
            norm_act(act, 7, 64)
            ffn_act(act, 4, at)
            post_act(act, 7, NB)

        @block.vector
        def _(dve):
            at, own = Position(), Chain(dve, dve_own)
            dve.wait_ge(s_const, 4)

            def first_block():
                lo_upto(dve, at, 0)
                dve.wait_ge(s_rowc, 3)
            norm_dve(dve, 0, 0, between=first_block)
            lo_upto(dve, at, 2)
            dve.tensor_copy(ident_r[:, :], ident[:, :])
            dve.tensor_scalar(masked[:, :], causal[:, 0:SEQ], -1.0, 2.0 ** 100, ALU.add, ALU.mult).then_inc(A["masked"], 1)
            ffn_dve(dve, 0, at)
            norm_dve(dve, 1, 8, add_product(dve, 0, N["ffn0"] + 3 * NFF, 0.5))
            ssm_dve(dve, at, own)
            norm_dve(dve, 2, 16, add_product(dve, 1, N["ssm_out"] + 8, 1.0))
            ffn_dve(dve, 1, at)
            norm_dve(dve, 3, 24, add_product(dve, 2, N["ffn1"] + 3 * NFF, 0.5))
            ffn_dve(dve, 2, at)
            norm_dve(dve, 4, 32, add_product(dve, 3, N["ffn2"] + 3 * NFF, 0.5))
            mla_dve(dve, at, own)
            norm_dve(dve, 5, 40, add_product(dve, 4, N["mla_out"] + 4, 1.0))
            ffn_dve(dve, 3, at)
            norm_dve(dve, 6, 48, add_product(dve, 5, N["ffn3"] + 3 * NFF, 0.5))
            b2_dve(dve, at, own)
            norm_dve(dve, 7, 64, post_dve(dve, own, 0, (B["in"], 80)), early=False)
            ffn_dve(dve, 4, at)
            post = post_dve(dve, own, 1, (B["in"], 96))
            for t in range(NT):
                post(t)

        @block.tensor
        def _(pe):
            own = Chain(pe, pe_own)
            pe.wait_ge(s_const, 4)
            norm_pe(pe, 0)
            pe.wait_ge(s_rows, 16 * len(NROW))
            for i in range(3):
                pe.transpose(PS[:, 2 + i, 0:ROWS_IN[i]], rows[i][0:ROWS_IN[i], :], ident[0:ROWS_IN[i], 0:ROWS_IN[i]])\
                  .then_inc(s_rowt, 1)
            pe.wait_ge(s_rowc, 3)
            ffn_pe(pe, 0, 0)
            norm_pe(pe, 1)
            ssm_pe(pe)
            norm_pe(pe, 2)
            ffn_pe(pe, 1, 2)
            norm_pe(pe, 3)
            ffn_pe(pe, 2, 3)
            norm_pe(pe, 4)
            mla_pe(pe)
            norm_pe(pe, 5)
            ffn_pe(pe, 3, 5)
            norm_pe(pe, 6)
            b2_pe(pe)
            norm_pe(pe, 7)
            ffn_pe(pe, 4, 7)


_INS = ['x', 'positions', 'norm_w', 'ffn_w_gate', 'ffn_w_up', 'ffn_w_down', 'ssm_w_in', 'ssm_conv_w',
        'ssm_conv_b', 'ssm_dt_bias', 'ssm_a_log', 'ssm_d', 'ssm_norm_w', 'ssm_w_out', 'mla_w_in',
        'mla_q_a_norm', 'mla_kv_a_norm', 'mla_w_q_b', 'mla_w_kv_b', 'mla_q_norm', 'mla_k_norm', 'mla_w_out',
        'norm_gains_2', 'w_in_2', 'mlstm_conv_2', 'mlstm_gate_bias_2', 'diff_lambda_2', 'diff_subln_2',
        'w_mlstm_out_2', 'w_diff_out_2', 'w_ret_out_2', 'w_out_2', 'w_ffn_in_2', 'w_ffn_out_2']


def kernel(**inputs):
    import concourse.bacc as bacc
    from concourse.bass_utils import run_bass_kernel_spmd

    nc = bacc.Bacc("TRN2", target_bir_lowering=False, num_devices=1)
    arrays, args = {}, []
    for name in _INS:
        a = np.ascontiguousarray(inputs[name])
        arrays[f"in_{name}"] = a
        args.append(nc.dram_tensor(f"in_{name}", a.shape, mybir.dt.from_np(a.dtype), kind="ExternalInput").ap())
    args.append(nc.dram_tensor("out_x", (1, SEQ, DM), FP32, kind="ExternalOutput").ap())
    build(nc, *args)
    return run_bass_kernel_spmd(nc, [arrays], core_ids=[0]).results[0]["out_x"]
```
